# Optimizing a Trainium2 kernel written in Bass

```python
import math
import jax
import jax.numpy as jnp
from jax import lax
import numpy as np

D_MODEL = 2048
BATCH = 1
SEQ = 256
DEPTH = 1

HEAD_DIM = 64
SCALE = HEAD_DIM ** -0.5
Q_BLOCK = 128
NORM_EPS = 1e-6
NEG = -1e30
TINY = 1e-30

DIL_GROUPS = ((128, 1), (512, 4), (2048, 16))
N_DIL_GROUPS = 3
A_HEADS = 8
A_WIDTH = A_HEADS * HEAD_DIM

B_HEADS = 16
B_KV_GROUPS = 2
B_HEADS_PER_GROUP = B_HEADS // B_KV_GROUPS
CMP_LEN = 32
CMP_STRIDE = 16
CMP_HIDDEN = 256
SEL_LEN = 64
SEL_TOPK = 16
SEL_LOCAL = 2
FORCED_SCORE = 1e6
WIN = 512
B_WIDTH = B_HEADS * HEAD_DIM

C_HEADS = 8
C_VDIM = 2 * HEAD_DIM
C_WIDTH = C_HEADS * C_VDIM

N_BUCKETS = 32
BIAS_MAX_DIST = 2048
N_BIAS_A = N_DIL_GROUPS * A_HEADS
N_BIAS_HEADS = N_BIAS_A + B_HEADS + C_HEADS

D_FF = 4 * D_MODEL
N_BRANCHES = 3

IN_SPLITS = (
    3 * N_DIL_GROUPS * A_HEADS * HEAD_DIM,
    B_HEADS * HEAD_DIM,
    6 * B_KV_GROUPS * HEAD_DIM,
    3 * B_HEADS,
    C_HEADS * 2 * HEAD_DIM,
    C_HEADS * 2 * HEAD_DIM,
    C_HEADS * C_VDIM,
    N_BRANCHES * D_MODEL,
)
IN_COLS = sum(IN_SPLITS)
IN_OFFSETS = tuple(int(v) for v in np.cumsum(IN_SPLITS)[:-1])

kernel_name = "hybrid_gated_dilated_nsa_diff_block"

def rms_norm(x, gain):
    xf = x.astype(jnp.float32)
    y = xf * lax.rsqrt(jnp.mean(xf * xf, axis=-1, keepdims=True) + NORM_EPS)
    return (y * gain.astype(jnp.float32)).astype(x.dtype)

def masked_softmax(logits, mask):
    logits = jnp.where(mask, logits, NEG)
    m = jnp.max(logits, axis=-1, keepdims=True)
    e = jnp.where(mask, jnp.exp(logits - m), 0.0)
    s = jnp.maximum(jnp.sum(e, axis=-1, keepdims=True), TINY)
    return e / s, (m + jnp.log(s))[..., 0]

def t5_bucket(dist):
    exact = N_BUCKETS // 2
    d = jnp.maximum(dist, 0)
    logd = jnp.log(jnp.maximum(d, 1).astype(jnp.float32) / exact)
    far = exact + (logd / math.log(BIAS_MAX_DIST / exact) * (N_BUCKETS - exact)).astype(jnp.int32)
    return jnp.where(d < exact, d, jnp.minimum(far, N_BUCKETS - 1))

def sweep_query_blocks(block_fn, seq):
    out = lax.map(block_fn, jnp.arange(seq // Q_BLOCK))
    out = jnp.moveaxis(out, 0, 1)
    return out.reshape((out.shape[0], seq) + out.shape[3:])

def dilated_attention(q, k, v, rel_a):
    seq = q.shape[1]

    def block(bi):
        t = bi * Q_BLOCK + jnp.arange(Q_BLOCK)
        qb = lax.dynamic_slice_in_dim(q, bi * Q_BLOCK, Q_BLOCK, axis=1)
        outs, lses = [], []
        for g, (win, dil) in enumerate(DIL_GROUPS):
            offs = jnp.arange(win // dil + 1) * dil
            idx = t[:, None] - offs[None, :]
            valid = idx >= 0
            idx = jnp.maximum(idx, 0)
            kg = k[:, :, g][:, idx]
            vg = v[:, :, g][:, idx]
            logits = jnp.einsum("bqhd,bqjhd->bhqj", qb[:, :, g], kg).astype(jnp.float32) * SCALE
            bias = rel_a[t5_bucket(offs), g].T.astype(jnp.float32)
            p, lse = masked_softmax(logits + bias[None, :, None, :], valid[None, None])
            outs.append(jnp.einsum("bhqj,bqjhd->bqhd", p.astype(v.dtype), vg))
            lses.append(jnp.transpose(lse, (0, 2, 1)))
        wts = jax.nn.softmax(jnp.stack(lses, axis=0), axis=0).astype(v.dtype)
        return (wts[0][..., None] * outs[0] + wts[1][..., None] * outs[1]
                + wts[2][..., None] * outs[2])

    return sweep_query_blocks(block, seq)

def nsa_attention(q, kv, gates, cmp_k_pos, cmp_v_pos, cmp_k_w1, cmp_k_w2, cmp_v_w1, cmp_v_w2, rel_b):
    bsz, seq = q.shape[:2]
    G, Hg, hd = B_KV_GROUPS, B_HEADS_PER_GROUP, HEAD_DIM
    qg = q.reshape(bsz, seq, G, Hg, hd)
    k_cmp, v_cmp, k_sel, v_sel, k_win, v_win = [kv[:, :, i] for i in range(6)]
    t_all = jnp.arange(seq)

    n_cmp = (seq - CMP_LEN) // CMP_STRIDE + 1
    starts = jnp.arange(n_cmp) * CMP_STRIDE
    cidx = starts[:, None] + jnp.arange(CMP_LEN)[None, :]

    def compress(kx, pos, w1, w2):
        blocks = kx[:, cidx] + pos[None, None, :, None, :]
        blocks = jnp.transpose(blocks, (0, 1, 3, 2, 4)).reshape(bsz, n_cmp, G, CMP_LEN * hd)
        return jax.nn.gelu(blocks @ w1) @ w2

    kc = compress(k_cmp, cmp_k_pos, cmp_k_w1, cmp_k_w2)
    vc = compress(v_cmp, cmp_v_pos, cmp_v_w1, cmp_v_w2)
    cmask = (starts + CMP_LEN - 1)[None, :] <= t_all[:, None]
    logits_c = jnp.einsum("bsghd,bngd->bghsn", qg, kc).astype(jnp.float32) * SCALE
    p_cmp, _ = masked_softmax(logits_c, cmask)
    o_cmp = jnp.einsum("bghsn,bngd->bsghd", p_cmp.astype(v_cmp.dtype), vc)

    n_sel = seq // SEL_LEN
    top = min(SEL_TOPK, n_sel)
    bstart = jnp.arange(n_sel) * SEL_LEN
    overlap = ((starts[:, None] < bstart[None, :] + SEL_LEN)
               & (starts[:, None] + CMP_LEN > bstart[None, :])).astype(jnp.float32)
    score = jnp.einsum("bghsn,nj->bgsj", p_cmp, overlap)
    cur = t_all // SEL_LEN
    back = cur[:, None] - jnp.arange(n_sel)[None, :]
    forced = (jnp.arange(n_sel)[None, :] == 0) | ((back >= 0) & (back < SEL_LOCAL))
    score = jnp.where(forced, FORCED_SCORE, score)
    score = jnp.where(bstart[None, :] <= t_all[:, None], score, NEG)
    _, sel_idx = lax.top_k(score, top)

    k_blk = jnp.transpose(k_sel.reshape(bsz, n_sel, SEL_LEN, G, hd), (0, 3, 1, 2, 4))
    v_blk = jnp.transpose(v_sel.reshape(bsz, n_sel, SEL_LEN, G, hd), (0, 3, 1, 2, 4))
    bidx = jnp.arange(bsz)[:, None, None, None]
    gidx = jnp.arange(G)[None, :, None, None]
    rel_bg = jnp.transpose(rel_b, (1, 0, 2))

    def sel_block(bi):
        qs = bi * Q_BLOCK
        t = qs + jnp.arange(Q_BLOCK)
        qb = lax.dynamic_slice_in_dim(qg, qs, Q_BLOCK, axis=1)
        ib = lax.dynamic_slice_in_dim(sel_idx, qs, Q_BLOCK, axis=2)
        kb = k_blk[bidx, gidx, ib].reshape(bsz, G, Q_BLOCK, top * SEL_LEN, hd)
        vb = v_blk[bidx, gidx, ib].reshape(bsz, G, Q_BLOCK, top * SEL_LEN, hd)
        kpos = (ib[..., None] * SEL_LEN + jnp.arange(SEL_LEN)).reshape(bsz, G, Q_BLOCK, top * SEL_LEN)
        dist = t[None, None, :, None] - kpos
        bias = rel_bg[gidx, t5_bucket(dist)]
        logits = (jnp.einsum("bqghd,bgqkd->bghqk", qb, kb).astype(jnp.float32) * SCALE
                  + jnp.transpose(bias, (0, 1, 4, 2, 3)).astype(jnp.float32))
        p, _ = masked_softmax(logits, (dist >= 0)[:, :, None])
        return jnp.einsum("bghqk,bgqkd->bqghd", p.astype(vb.dtype), vb)

    o_sel = sweep_query_blocks(sel_block, seq)

    kw = jnp.pad(k_win, ((0, 0), (WIN, 0), (0, 0), (0, 0)))
    vw = jnp.pad(v_win, ((0, 0), (WIN, 0), (0, 0), (0, 0)))

    def win_block(bi):
        qs = bi * Q_BLOCK
        t = qs + jnp.arange(Q_BLOCK)
        qb = lax.dynamic_slice_in_dim(qg, qs, Q_BLOCK, axis=1)
        kb = lax.dynamic_slice_in_dim(kw, qs, Q_BLOCK + WIN, axis=1)
        vb = lax.dynamic_slice_in_dim(vw, qs, Q_BLOCK + WIN, axis=1)
        kpos = qs - WIN + jnp.arange(Q_BLOCK + WIN)
        dist = t[:, None] - kpos[None, :]
        valid = (dist >= 0) & (dist < WIN) & (kpos[None, :] >= 0)
        bias = jnp.transpose(rel_b[t5_bucket(dist)], (2, 3, 0, 1)).astype(jnp.float32)
        logits = jnp.einsum("bqghd,bkgd->bghqk", qb, kb).astype(jnp.float32) * SCALE + bias
        p, _ = masked_softmax(logits, valid)
        return jnp.einsum("bghqk,bkgd->bqghd", p.astype(vb.dtype), vb)

    o_win = sweep_query_blocks(win_block, seq)

    shp = (bsz, seq, B_HEADS, hd)
    out = (gates[..., 0:1] * o_cmp.reshape(shp) + gates[..., 1:2] * o_sel.reshape(shp)
           + gates[..., 2:3] * o_win.reshape(shp))
    return out.reshape(bsz, seq, B_WIDTH)

def diff_attention(q, k, v, lam_vecs, sub_gain, rel_c, lam_init):
    bsz, seq = q.shape[:2]
    lv = lam_vecs.astype(jnp.float32)
    lam = jnp.exp(jnp.sum(lv[0] * lv[1])) - jnp.exp(jnp.sum(lv[2] * lv[3])) + lam_init
    kpos = jnp.arange(seq)

    def block(bi):
        t = bi * Q_BLOCK + jnp.arange(Q_BLOCK)
        qb = lax.dynamic_slice_in_dim(q, bi * Q_BLOCK, Q_BLOCK, axis=1)
        dist = t[:, None] - kpos[None, :]
        bias = jnp.transpose(rel_c[t5_bucket(dist)], (2, 0, 1)).astype(jnp.float32)
        logits = jnp.einsum("bqhcd,bkhcd->bchqk", qb, k).astype(jnp.float32) * SCALE + bias
        p, _ = masked_softmax(logits, dist >= 0)
        attn = p[:, 0] - lam * p[:, 1]
        return jnp.einsum("bhqk,bkhd->bqhd", attn.astype(v.dtype), v)

    o = sweep_query_blocks(block, seq)
    o = rms_norm(o, sub_gain) * (1.0 - lam_init)
    return o.reshape(bsz, seq, C_WIDTH)

def setup_inputs(seed: int = 0) -> dict:
    key = jax.random.key(seed)
    ks = jax.random.split(key, 24)
    f32 = jnp.float32
    L = DEPTH

    def w(k, shape, fan_in):
        return jax.random.normal(k, shape, f32) * fan_in ** -0.5

    def gain(k, shape):
        return 1.0 + 0.02 * jax.random.normal(k, shape, f32)

    return {
        "x": jax.random.normal(ks[0], (BATCH, SEQ, D_MODEL), f32),
        "rel_bias": 0.2 * jax.random.normal(ks[1], (N_BUCKETS, N_BIAS_HEADS), f32),
        "w_in": w(ks[2], (L, D_MODEL, IN_COLS), D_MODEL),
        "cmp_k_pos": 0.2 * jax.random.normal(ks[3], (L, CMP_LEN, HEAD_DIM), f32),
        "cmp_v_pos": 0.2 * jax.random.normal(ks[4], (L, CMP_LEN, HEAD_DIM), f32),
        "cmp_k_w1": w(ks[5], (L, CMP_LEN * HEAD_DIM, CMP_HIDDEN), CMP_LEN * HEAD_DIM),
        "cmp_k_w2": w(ks[6], (L, CMP_HIDDEN, HEAD_DIM), CMP_HIDDEN),
        "cmp_v_w1": w(ks[7], (L, CMP_LEN * HEAD_DIM, CMP_HIDDEN), CMP_LEN * HEAD_DIM),
        "cmp_v_w2": w(ks[8], (L, CMP_HIDDEN, HEAD_DIM), CMP_HIDDEN),
        "diff_lambda": 0.1 * jax.random.normal(ks[9], (L, 4, HEAD_DIM), f32),
        "diff_norm": gain(ks[10], (L, C_VDIM)),
        "w_branch_a": w(ks[11], (L, A_WIDTH, D_MODEL), A_WIDTH),
        "w_branch_b": w(ks[12], (L, B_WIDTH, D_MODEL), B_WIDTH),
        "w_branch_c": w(ks[13], (L, C_WIDTH, D_MODEL), C_WIDTH),
        "w_out": w(ks[14], (L, D_MODEL, D_MODEL), D_MODEL),
        "norm_mix_pre": gain(ks[15], (L, D_MODEL)),
        "norm_mix_post": gain(ks[16], (L, D_MODEL)),
        "norm_mlp_pre": gain(ks[17], (L, D_MODEL)),
        "norm_mlp_post": gain(ks[18], (L, D_MODEL)),
        "w_up": w(ks[19], (L, D_MODEL, D_FF), D_MODEL),
        "w_down": w(ks[20], (L, D_FF, D_MODEL), D_FF),
    }

def reference(x, rel_bias, w_in, cmp_k_pos, cmp_v_pos, cmp_k_w1, cmp_k_w2, cmp_v_w1, cmp_v_w2,
              diff_lambda, diff_norm, w_branch_a, w_branch_b, w_branch_c, w_out,
              norm_mix_pre, norm_mix_post, norm_mlp_pre, norm_mlp_post, w_up, w_down):
    bsz, seq, _ = x.shape
    rel_a = rel_bias[:, :N_BIAS_A].reshape(N_BUCKETS, N_DIL_GROUPS, A_HEADS)
    rel_b = rel_bias[:, N_BIAS_A:N_BIAS_A + B_HEADS].reshape(N_BUCKETS, B_KV_GROUPS, B_HEADS_PER_GROUP)
    rel_c = rel_bias[:, N_BIAS_A + B_HEADS:]

    for l in range(DEPTH):
        lam_init = 0.8 - 0.6 * math.exp(-0.3 * l)
        h = rms_norm(x, norm_mix_pre[l])
        proj = h @ w_in[l]
        a_qkv, b_q, b_kv, b_gate, c_q, c_k, c_v, m_gate = jnp.split(proj, IN_OFFSETS, axis=-1)

        a = a_qkv.reshape(bsz, seq, 3, N_DIL_GROUPS, A_HEADS, HEAD_DIM)
        o_a = dilated_attention(a[:, :, 0], a[:, :, 1], a[:, :, 2], rel_a).reshape(bsz, seq, A_WIDTH)

        o_b = nsa_attention(b_q.reshape(bsz, seq, B_HEADS, HEAD_DIM),
                            b_kv.reshape(bsz, seq, 6, B_KV_GROUPS, HEAD_DIM),
                            jax.nn.sigmoid(b_gate.reshape(bsz, seq, B_HEADS, 3)),
                            cmp_k_pos[l], cmp_v_pos[l], cmp_k_w1[l], cmp_k_w2[l],
                            cmp_v_w1[l], cmp_v_w2[l], rel_b)

        o_c = diff_attention(c_q.reshape(bsz, seq, C_HEADS, 2, HEAD_DIM),
                             c_k.reshape(bsz, seq, C_HEADS, 2, HEAD_DIM),
                             c_v.reshape(bsz, seq, C_HEADS, C_VDIM),
                             diff_lambda[l], diff_norm[l], rel_c, lam_init)

        g = jax.nn.sigmoid(m_gate.reshape(bsz, seq, N_BRANCHES, D_MODEL))
        mixed = (g[:, :, 0] * (o_a @ w_branch_a[l]) + g[:, :, 1] * (o_b @ w_branch_b[l])
                 + g[:, :, 2] * (o_c @ w_branch_c[l]))
        x = x + rms_norm(mixed @ w_out[l], norm_mix_post[l])

        h = rms_norm(x, norm_mlp_pre[l])
        u = jnp.square(jax.nn.relu(h @ w_up[l]))
        x = x + rms_norm(u @ w_down[l], norm_mlp_post[l])
    return x


_drawn_inputs = setup_inputs


def setup_inputs(seed=0):
    import zlib

    import numpy as np

    out = dict(_drawn_inputs(seed))
    spreads = {}
    factors = {'cmp_k_pos': 78.403,
     'diff_lambda': 3.712,
     'diff_norm': 3.6,
     'norm_mix_post': 10.626,
     'norm_mlp_pre': 36.152,
     'norm_mlp_post': 60.346,
     'cmp_v_pos': 2.842}
    for name, (base, spread) in spreads.items():
        noise = np.random.default_rng([zlib.crc32(name.encode()), seed]).standard_normal(out[name].shape)
        drawn = base * np.exp(spread * noise) if base else spread * noise
        out[name] = jnp.asarray(drawn.astype(out[name].dtype))
    for name, factor in factors.items():
        out[name] = (out[name] * factor).astype(out[name].dtype)
    return out
```

```python
import math
from contextlib import ExitStack

import concourse.bass as bass
from concourse import mybir
from concourse.alu_op_type import AluOpType as ALU

F32 = mybir.dt.float32
F32R = mybir.dt.float32r
ACT = mybir.ActivationFunctionType
AX = mybir.AxisListType.X

P = 128
D = 2048
SEQ = 256
HD = 64
DFF = 8192
KC = D // P
W = 512
UR = 2
RING = 4
LEAD = 3
EPS = 1e-6
SCALE = HD ** -0.5
TINY = 1e-30
NEG = -1e30
LAM_INIT = 0.8 - 0.6
NCMP = 15
CSTRIDE = 16

A_Q, A_K, A_V = 0, 1536, 3072
B_Q, B_KV = 4608, 5632
C_Q, C_K, C_V = 6448, 7472, 8496
M_G = 9520
B_LAST = 304

CH = KC // UR
ORDER = [("qk_a", 6, CH), ("v_a", 3, CH), ("q_b", 2, CH), ("kv_b", 2, CH), ("qk_c", 4, CH), ("v_c", 2, CH),
         ("gate", 12, CH), ("branch", 4, 10), ("out", 4, CH),
         ("up0", 8, CH), ("down0", 4, 16), ("up1", 8, CH), ("down1", 4, 16)]
U0 = {}
_u = 0
for _n, _c, _k in ORDER:
    U0[_n] = _u
    _u += _c * _k
UNITS = _u
V_OF = {"branch": 3}
S_OF = {"branch": 0, "down1": 0}
T_OF = {"v_a": 0, "v_c": 0, "gate": 0, "out": 0, "down0": 0, "down1": 0}
V0, S0, T0 = {}, {}, {}
_v = _s = _t = 0
for _n, _c, _k in ORDER:
    V0[_n], S0[_n], T0[_n] = _v, _s, _t
    _v += _c * V_OF.get(_n, 1)
    _s += _c * S_OF.get(_n, 1)
    _t += _c * T_OF.get(_n, 1)

SCORES_AT = [0, 0, 1, 2, 3, 3, 4, 5]
NSTEP = 24


class Pos:

    def __init__(self, k, per=0, i=0):
        self.k, self.per, self.i = k, per, i

    def __add__(self, n):
        return Pos(self.k + n, self.per, self.i)

    def count(self, n=0):
        if isinstance(self.i, int):
            return self.k + n + self.per * self.i
        return self.i * self.per + (self.k + n)

    def loads(self):
        r = 16 * (self.k // RING + 1)
        if isinstance(self.i, int):
            return r + 16 * (self.per // RING) * self.i
        return self.i * (16 * (self.per // RING)) + r


def wait(eng, sem, value):
    if not (isinstance(value, int) and value <= 0):
        eng.wait_ge(sem, value)


def held(eng, register, value):
    if isinstance(value, int):
        return value
    eng.reg_add(register, eng.snap(value - 1), 1)
    return register


def trunk(nc, x, rel_bias, w_in, cmp_k_pos, cmp_v_pos, cmp_k_w1, cmp_k_w2, cmp_v_w1, cmp_v_w2, diff_lambda,
          diff_norm, w_branch_a, w_branch_b, w_branch_c, w_out, norm_mix_pre, norm_mix_post, norm_mlp_pre,
          norm_mlp_post, w_up, w_down, identity, bucket_onehot, distance_mask, block_mask, out):
    bias_table = nc.dram_tensor("bias_table", (48, 512), F32, kind="Internal").ap()
    gate_dram = nc.dram_tensor("gate_dram", (P, 12, 1024), F32, kind="Internal").ap()
    hankel = bass.AP(bias_table.tensor, 0, [[512, 48], [1, P], [1, 256]])

    ctx = ExitStack()
    sems = {}

    def sem(name):
        if name not in sems:
            sems[name] = ctx.enter_context(nc.semaphore(name))
        return sems[name]

    base = 16512
    regions = {"small": [0, 5888], "ring": [5888, 49152], "h": [55040, 32768], "u": [87808, 65536],
               "f": [153344, 59392]}
    marks = {k: v[0] for k, v in regions.items()}

    def put(region, name, shape, dt=F32, at=None):
        size = 4 * math.prod(shape[1:])
        off = marks[region] if at is None else regions[region][0] + at
        off = (off + 31) // 32 * 32
        assert off + size <= regions[region][0] + regions[region][1], (name, off + size)
        if at is None:
            marks[region] = off + size
        return nc.alloc_sbuf_tensor_at(name, shape, dt, offset=base + off)

    ident = put("small", "ident", [P, P])
    columns = put("small", "columns", [P, 64])
    ssq = put("small", "ssq", [P, 4, 2])
    mean = put("small", "mean", [P, 4, 2])
    root = put("small", "root", [P, 4, 2])
    inv = put("small", "inv", [P, 4, 2])
    newton = put("small", "newton", [P, 4, 2])
    rstd = put("small", "rstd", [P, 4, 2])
    head_gates = put("small", "head_gates", [P, 2, 3, 16])
    negmax = put("small", "negmax", [P, 2, 8])
    sums = put("small", "sums", [P, 2, 8])
    coef = put("small", "coef", [P, 2, 4])
    rsum = put("small", "rsum", [P, 2, 4])
    a_negmax = put("small", "a_negmax", [P, 2, 24])
    a_sums = put("small", "a_sums", [P, 2, 24])
    a_min = put("small", "a_min", [P, 2, 8])
    a_w = put("small", "a_w", [P, 2, 24])
    a_ws = put("small", "a_ws", [P, 2, 24])
    a_tot = put("small", "a_tot", [P, 2, 8])
    lam2 = put("small", "lam2", [P, 4])
    neg_lam = put("small", "neg_lam", [P, 1])
    c_ssq = put("small", "c_ssq", [P, 2, 8])
    c_mean = put("small", "c_mean", [P, 2, 8])
    c_root = put("small", "c_root", [P, 2, 8])
    c_rstd = put("small", "c_rstd", [P, 2, 8])
    sub_gain = put("small", "sub_gain", [P, P])
    bmask = put("small", "bmask", [P, 2, NCMP])
    m_max = put("small", "m_max", [P, 2, 16])
    m_sum = put("small", "m_sum", [P, 2, 16])
    m_coef = put("small", "m_coef", [P, 2, 16])
    kc_t = put("small", "kc_t", [P, 2 * NCMP])

    raw = put("ring", "raw", [P, RING, UR, W])
    w_hi = put("ring", "w_hi", [P, RING, UR, W], F32R)
    w_lo = put("ring", "w_lo", [P, RING, UR, W], F32R)
    h_hi = put("h", "h_hi", [P, KC, SEQ], F32R)
    h_lo = put("h", "h_lo", [P, KC, SEQ], F32R)

    q_c = put("u", "q_c", [P, 8, SEQ])
    k_c = put("u", "k_c", [P, 8, SEQ])
    v_c = put("u", "v_c", [P, 2, 1024])
    v_a = put("u", "v_a", [P, 2, 1536])
    logits = put("u", "logits", [P, 4, 384])
    blocks_t = put("u", "blocks_t", [P, 2, KC, 2 * NCMP])
    q_b = put("u", "q_b", [P, 8, SEQ])
    k_b = put("u", "k_b", [P, 4, SEQ])
    v_b = put("u", "v_b", [P, 2, 2, P])
    cmp_t = put("u", "cmp_t", [P, 4, SEQ])
    x_in = put("u", "x_in", [P, 2, D], at=0)
    x_normed = put("u", "x_normed", [P, 2, D], at=16384)
    w1k = put("u", "w1k", [P, KC, 256], at=0)
    w1v = put("u", "w1v", [P, KC, 256], at=16384)
    hid = put("u", "hid", [P, 3, 8 * NCMP], at=36864)
    hid_k = put("u", "hid_k", [P, 2, 2 * NCMP], at=36864 + 1536)
    hid_v = put("u", "hid_v", [P, 2, 2, 4, 32], at=36864 + 2048)
    o_hi = put("u", "o_hi", [P, 20, SEQ], F32R, at=0)
    o_lo = put("u", "o_lo", [P, 20, SEQ], F32R, at=32768)
    u_hi = put("u", "u_hi", [P, 32, SEQ], F32R, at=0)
    u_lo = put("u", "u_lo", [P, 32, SEQ], F32R, at=32768)
    mid_normed = put("u", "mid_normed", [P, 2, D], at=0)
    square_out = put("u", "square_out", [P, 2, D], at=32768)

    o_a = put("f", "o_a", [P, 3, 2, 512])
    k_a = put("f", "k_a", [P, 12, SEQ])
    q_a = put("f", "q_a", [P, 12, SEQ])
    stage = put("f", "stage", [P, 2, 2, W])
    q_pad = put("f", "q_pad", [P, 4, SEQ])
    bias = put("f", "bias", [P, 4, SEQ])
    p_t = put("f", "p_t", [P, 2, 384])
    w2k = put("f", "w2k", [P, 2, 2, HD])
    w2v = put("f", "w2v", [P, 2, HD])
    o_c = put("f", "o_c", [P, 2, 1024], at=12288)
    o_b = put("f", "o_b", [P, 2, 1024], at=24576)
    merged = put("f", "merged", [P, 2, 2, 128], at=36864 + 4096)
    dup = put("f", "dup", [P, 2, 8, 2, HD], at=0)
    rows64 = put("f", "rows64", [64, P], at=0)
    onehot = put("f", "onehot", [32, 512], at=1024)
    dmask = put("f", "dmask", [48, 512], at=3072)
    rel = put("f", "rel", [32, 48], at=5120)
    table = put("f", "table", [48, 512], at=6144)
    lam_rows = put("f", "lam_rows", [P, 4, HD], at=8192)
    lam_prod = put("f", "lam_prod", [P, 2, HD], at=9216)
    cmp_l = put("f", "cmp_l", [P, 2, 16, NCMP], at=36864 + 8192 + 4096)
    cmp_p = put("f", "cmp_p", [P, 2, 16, 32], at=36864 + 8192)
    cmp_pt = put("f", "cmp_pt", [P, 8, P], at=36864 + 4096)
    vc_diag = put("f", "vc_diag", [P, 2, 4, HD], at=36864 + 16384)
    c_square = put("f", "c_square", [P, 16, P], at=4096)
    gates_in = put("f", "gates_in", [P, 2, 3, 2, W], at=0)
    br_tmp = put("f", "br_tmp", [P, 2, W], at=24576)
    br_stage = put("f", "br_stage", [P, 2, 2, W], at=36864)
    mid = put("f", "mid", [P, 2, D], at=0)
    y = put("f", "y", [P, 2, D], at=16384)
    gain_row = put("f", "gain_row", [P, D], at=32768)
    up_stage = put("f", "up_stage", [P, 2, 2, W], at=40960)

    ps = ctx.enter_context(nc.psum_tensor("ps", [P, 8, 512], F32))
    T_BANK = 6

    w_in_v = w_in.rearrange("l (c p) n -> p (l c) n", p=P)
    w_out_v = w_out.rearrange("l (c p) n -> p (l c) n", p=P)
    w_up_v = w_up.rearrange("l (c p) n -> p (l c) n", p=P)
    w_down_v = w_down.rearrange("l (c p) n -> p (l c) n", p=P)
    w_br_v = [w.rearrange("l (c p) n -> p (l c) n", p=P) for w in (w_branch_a, w_branch_b, w_branch_c)]
    BR_UNITS = [2, 4, 4]
    BR_KC = [0, 4, 12]

    def attn(kind, i, j):
        if kind == "a":
            return i * 4 + j // 2, i * 4 + j // 2, i * 8 + j
        if kind == "b":
            key = i // 2 + 2 * ((j // 2) % 2)
            return i * 2 + j // 4, key, i * 4 + (24 + 2 * (j // 4) + j % 2)
        return i * 4 + j // 2, i * 4 + j // 2, i * 4 + (40 + j // 2)

    FIRST_IT = {"a": 0, "b": 3, "c": 7}
    LOOPS = [("a", 3), ("b", 4), ("c", 2)]

    def bank_of(kind, j):
        n = j // 2 if kind == "c" else j // 4
        return n, 6 + n % 2

    def banks_before(kind):
        return {"a": 0, "b": 6, "c": 14}[kind], 4 if kind == "c" else 2

    def bank_last(kind):
        return [1, 3, 5, 7] if kind == "c" else [3, 7]

    block = ctx.enter_context(nc.Block())

    @block.sync
    def _(sp):
        def load(u, slot, view, kc, col, cols=W):
            wait(sp, sem("lo_ready"), u.count(1 - RING))
            sp.dma_start(raw[:, slot, :, 0:cols], view[:, kc:kc + UR, bass.ds(col, cols)]).then_inc(
                sem(f"raw_loaded{slot}"), 16)

        def chunk(u, view, kc, n, col, cols=W, s0=0):
            for j in range(n):
                load(u + j, (s0 + j) % RING, view, kc + UR * j, col, cols)

        for t in range(2):
            sp.dma_start(x_in[:, t, :], x[0, t * P:(t + 1) * P, :]).then_inc(sem(f"x_loaded{t}"), 16)

        def qk_a(i):
            chunk(Pos(U0["qk_a"], 2 * CH, i), w_in_v, 0, CH, i * W + A_Q)
            chunk(Pos(U0["qk_a"] + CH, 2 * CH, i), w_in_v, 0, CH, i * W + A_K)

        qk_a(0)
        with sp.Fori(1, 3) as i:
            qk_a(i)
        with sp.Fori(0, 3) as i:
            chunk(Pos(U0["v_a"], CH, i), w_in_v, 0, CH, i * W + A_V)
        for c in range(2):
            chunk(Pos(U0["q_b"] + CH * c), w_in_v, 0, CH, B_Q + W * c)
        chunk(Pos(U0["kv_b"]), w_in_v, 0, CH, B_KV)
        chunk(Pos(U0["kv_b"] + CH), w_in_v, 0, CH, B_KV + W, B_LAST)
        with sp.Fori(0, 2) as i:
            chunk(Pos(U0["qk_c"], 2 * CH, i), w_in_v, 0, CH, i * W + C_Q)
            chunk(Pos(U0["qk_c"] + CH, 2 * CH, i), w_in_v, 0, CH, i * W + C_K)
        with sp.Fori(0, 2) as i:
            chunk(Pos(U0["v_c"], CH, i), w_in_v, 0, CH, i * W + C_V)

        def store_gates(c):
            sp.wait_ge(sem("evac_v"), c + (V0["gate"] + 1))
            sp.dma_start(gate_dram[:, bass.ds(c, 1), :].rearrange("p a n -> p (a n)"),
                         stage[:, 0, :, :].rearrange("p t n -> p (t n)")).then_inc(sem("gates_stored"), 16)

        chunk(Pos(U0["gate"]), w_in_v, 0, CH, M_G)
        with sp.Fori(1, 12) as i:
            chunk(Pos(U0["gate"], CH, i), w_in_v, 0, CH, i * W + M_G)
            store_gates(i - 1)

        def load_gates(n):
            wait(sp, sem("merge_done"), n - 1)
            sp.dma_start(gates_in[:, n % 2, :, :, :].rearrange("p b t n -> p b (t n)"),
                         gate_dram[:, n:n + 9:4, :]).then_inc(sem(f"gates_loaded{n % 2}"), 16)

        for n in range(4):
            for b in range(3):
                if b == 2:
                    if n == 0:
                        store_gates(11)
                        sp.wait_ge(sem("gates_stored"), 16 * 12)
                        sp.wait_ge(sem("o_split_lo"), 10)
                    load_gates(n)
                before = sum(BR_UNITS[:b])
                chunk(Pos(U0["branch"] + 10 * n + before), w_br_v[b], 0, BR_UNITS[b], W * n,
                      s0=(10 * n + before) % RING)
        with sp.Fori(0, 4) as i:
            chunk(Pos(U0["out"], CH, i), w_out_v, 0, CH, i * W)

        def up(h, i):
            for c in range(2):
                chunk(Pos(U0[f"up{h}"] + CH * c, 2 * CH, i), w_up_v, 0, CH, i * (2 * W) + (h * DFF // 2 + W * c))

        def down(h, i):
            chunk(Pos(U0[f"down{h}"], 16, i), w_down_v, 32 * h, 16, i * W)

        for h in range(2):
            with sp.Fori(0, 4) as i:
                up(h, i)
            with sp.Fori(0, 4) as i:
                down(h, i)

    @block.gpsimd
    def _(pool):
        pool_count = pool.alloc_register("pool_count")

        def load(dst, src, name="const_loaded"):
            pool.dma_start(dst, src).then_inc(sem(name), 16)

        load(ident[:, :], identity)
        load(rows64[0:16, :], norm_mix_pre.rearrange("l (c p) -> (l c) p", p=P))
        load(rows64[16:32, :], norm_mlp_pre.rearrange("l (c p) -> (l c) p", p=P))
        load(rows64[32:48, :], cmp_k_pos.rearrange("l (c a) d -> (l c) (a d)", a=2))
        load(rows64[48:64, :], cmp_v_pos.rearrange("l (c a) d -> (l c) (a d)", a=2))
        load(onehot[:, :], bucket_onehot)
        load(dmask[:, :], distance_mask)
        load(rel[:, :], rel_bias)
        load(bmask[:, :, :], block_mask)
        load(lam_rows[:, :, :], bass.AP(diff_lambda.tensor, 0, [[0, P], [HD, 4], [1, HD]]))
        load(sub_gain[:, :], bass.AP(diff_norm.tensor, 0, [[0, P], [1, P]]))
        pool.wait_ge(sem("table_ready"), 1)
        pool.dma_start(bias_table, table[:, :]).then_inc(sem("table_stored"), 16)
        pool.memset(q_pad[:, :, :], 0.0).then_inc(sem("pad_zero"), 1)

        def queries_and_bias(kind, i):
            src = {"a": q_a, "b": q_b, "c": q_c}[kind]
            m0 = Pos(8 * FIRST_IT[kind], 8, i)
            for j in range(8):
                tile, _, row = attn(kind, i, j)
                half = slice(64 * (j % 2), 64 * (j % 2) + 64)
                behind = held(pool, pool_count, (m0 + j).count(-3))
                pool.wait_ge(sem("pad_zero"), 1)
                wait(pool, sem("scores_ready"), behind)
                pool.tensor_copy(q_pad[half, j % 4, :], src[half, bass.ds(tile, 1), :].rearrange("p a n -> p (a n)")
                                 ).then_inc(sem("query_ready"), 1)
                pool.wait_ge(sem("table_stored"), 16)
                wait(pool, sem("logits_ready"), behind)
                pool.dma_start(bias[:, j % 4, :], hankel[bass.ds(row, 1)].rearrange("a p n -> (a p) n")).then_inc(
                    sem(f"bias_loaded{j % 4}"), 16)

        for name, n in (("tevac_v", T0["gate"]), ("tevac_s", T0["gate"])):
            pool.wait_ge(sem(name), n)
        for kind, n in LOOPS:
            queries_and_bias(kind, 0)
            with pool.Fori(1, n) as i:
                queries_and_bias(kind, i)
        pool.wait_ge(sem("pv_done"), 72)
        for dst, src, name in ((w1k, cmp_k_w1, "w1_loaded"), (w1v, cmp_v_w1, "w1_loaded")):
            pool.dma_start(dst[:, :, :], src.rearrange("l (c p) n -> p (l c) n", p=P)).then_inc(sem(name), 16)
        w2_k = cmp_k_w2.rearrange("l (c p) n -> p (l c) n", p=P)
        for a in range(2):
            pool.dma_start(w2k[:, :, a, :], w2_k).then_inc(sem("w2_loaded"), 16)
        pool.dma_start(w2v[:, :, :], cmp_v_w2.rearrange("l (c p) n -> p (l c) n", p=P)).then_inc(sem("w2_loaded"), 16)
        pool.memset(hid_v[:, :, :, :, :], 0.0).then_inc(sem("cmp_zero"), 1)
        pool.memset(vc_diag[:, :, :, :], 0.0).then_inc(sem("cmp_zero"), 1)
        pool.memset(cmp_p[:, :, :, :], 0.0).then_inc(sem("cmp_zero"), 1)
        pool.wait_ge(sem("merge_done"), 4)
        for t in range(2):
            pool.dma_start(mid[:, t, :], x[0, t * P:(t + 1) * P, :]).then_inc(sem("x_again"), 16)
        pool.wait_ge(sem("tevac_v"), T0["out"])
        pool.dma_start(gain_row[:, :], bass.AP(norm_mix_post.tensor, 0, [[0, P], [1, D]])).then_inc(sem("gain_loaded"), 16)
        pool.wait_ge(sem("mid_ready"), 2)
        pool.dma_start(gain_row[:, :], bass.AP(norm_mlp_post.tensor, 0, [[0, P], [1, D]])).then_inc(sem("gain_loaded"), 16)
        for t in range(2):
            pool.wait_ge(sem("result_ready"), t + 1)
            pool.dma_start(out[0, t * P:(t + 1) * P, :], mid[:, t, :]).then_inc(sem("stored"), 16)
        pool.wait_ge(sem("stored"), 32)

    @block.tensor
    def _(pe):
        def unit(u, slot, hi, lo, kc, pair, cols=W, first=False, last=False):
            pe.wait_ge(sem("lo_ready"), u.count(1))
            for t in range(2):
                acc = ps[:, 2 * pair + t, 0:cols]
                for k in range(UR):
                    tok = slice(t * P, (t + 1) * P)
                    a, b = first and k == 0, last and k == UR - 1
                    pe.matmul(acc, hi[:, kc + k, tok], w_hi[:, slot, k, 0:cols], start=a, stop=False)
                    pe.matmul(acc, hi[:, kc + k, tok], w_lo[:, slot, k, 0:cols], start=False, stop=False)
                    mm = pe.matmul(acc, lo[:, kc + k, tok], w_hi[:, slot, k, 0:cols], start=False, stop=b)
            mm.then_inc(sem("unit_used"), 1)

        def chunk(u, n, hi, lo, kc, pair, cols=W, s0=0, between=()):
            for j in range(n):
                unit(u + j, (s0 + j) % RING, hi, lo, kc + UR * j, pair, cols, j == 0, j == n - 1)
                if j == 1:
                    for f in between:
                        f()

        def transposed(t, source, ready):
            for name, value in ready:
                wait(pe, sem(name), value)
            wait(pe, sem("tevac_v"), t.count())
            wait(pe, sem("tevac_s"), t.count())
            for q in range(4):
                for h in range(2):
                    tr = pe.transpose(ps[:, T_BANK + q // 2, 256 * (q % 2) + P * h:256 * (q % 2) + P * h + P],
                                      source(q, h), ident[:, :])
            tr.then_inc(sem("transposed"), 1)

        def norm_transposes(k, src):
            pe.wait_ge(sem(f"normed_v{k}"), 1)
            pe.wait_ge(sem(f"normed_s{k}"), 1)
            for g in range(8):
                wait(pe, sem(f"norm_lo{k}"), 2 * (g - 5))
                for c in range(2):
                    for t in range(2):
                        kc = 2 * g + c
                        tr = pe.transpose(ps[:, g % 6, 256 * c + P * t:256 * c + P * t + P],
                                          src[:, t, kc * P:(kc + 1) * P], ident[:, :])
                tr.then_inc(sem(f"norm_t{k}"), 1)
            pe.wait_ge(sem(f"norm_lo{k}"), 16)

        pe.wait_ge(sem("const_loaded"), 16 * 11)
        pe.transpose(ps[:, 7, 0:64], rows64[:, :], ident[0:64, 0:64]).then_inc(sem("columns_t"), 1)
        pe.matmul(ps[0:48, 6, :], rel[:, :], onehot[:, :], start=True, stop=True).then_inc(sem("table_mm"), 1)
        norm_transposes(0, x_normed)

        def stage_tiles(slot):
            return lambda q, h: stage[:, slot, h, q * P:(q + 1) * P]

        def qk(name, i):
            e = Pos(V0[name], 2, i)
            es = Pos(S0[name], 2, i)
            t = Pos(T0[name], 2, i)
            wait(pe, sem("evac_v"), e.count(-1))
            wait(pe, sem("evac_s"), es.count(-1))
            chunk(Pos(U0[name], 2 * CH, i), CH, h_hi, h_lo, 0, 0)
            wait(pe, sem("evac_v"), e.count())
            wait(pe, sem("evac_s"), es.count())
            chunk(Pos(U0[name] + CH, 2 * CH, i), CH, h_hi, h_lo, 0, 1, between=[
                lambda: transposed(t, stage_tiles(0), [("evac_v", e.count(1)), ("evac_s", es.count(1))])])
            transposed(t + 1, stage_tiles(1), [("evac_v", e.count(2)), ("evac_s", es.count(2))])

        def values(name, i):
            wait(pe, sem("evac_v"), Pos(V0[name], 1, i).count())
            wait(pe, sem("evac_s"), Pos(S0[name], 1, i).count())
            chunk(Pos(U0[name], CH, i), CH, h_hi, h_lo, 0, 0)

        qk("qk_a", 0)
        with pe.Fori(1, 3) as i:
            qk("qk_a", i)
        with pe.Fori(0, 3) as i:
            values("v_a", i)
        pe.wait_ge(sem("evac_v"), V0["q_b"])
        pe.wait_ge(sem("evac_s"), S0["q_b"])
        qk("q_b", 0)
        e, es, t = V0["kv_b"], S0["kv_b"], Pos(T0["kv_b"])
        pe.wait_ge(sem("evac_v"), e)
        pe.wait_ge(sem("evac_s"), es)

        chunk(Pos(U0["kv_b"]), CH, h_hi, h_lo, 0, 0)
        chunk(Pos(U0["kv_b"] + CH), CH, h_hi, h_lo, 0, 1, B_LAST, between=[
            lambda: transposed(t, lambda q, h: dup[:, h, q, :, :].rearrange("p a n -> p (a n)"), [("dup_ready", 1)])])
        transposed(t + 1, lambda q, h: dup[:, h, 4 + q, :, :].rearrange("p a n -> p (a n)"), [("dup_ready", 2)])
        pe.wait_ge(sem("evac_v"), V0["qk_c"])
        pe.wait_ge(sem("evac_s"), S0["qk_c"])
        with pe.Fori(0, 2) as i:
            qk("qk_c", i)
        with pe.Fori(0, 2) as i:
            values("v_c", i)
        pe.wait_ge(sem("tevac_v"), T0["gate"])
        pe.wait_ge(sem("tevac_s"), T0["gate"])

        def maps(kind, i):
            it = FIRST_IT[kind]
            m0 = Pos(8 * it, 8, i)
            keys = {"a": k_a, "b": k_b, "c": k_c}[kind]
            ob0, ob_n = banks_before(kind)

            def scores(j):
                _, tile, _ = attn(kind, i, j)
                wait(pe, sem("query_ready"), (m0 + j).count(1))
                wait(pe, sem("logits_ready"), (m0 + j).count(-1))
                key = keys[:, bass.ds(tile, 1), :].rearrange("p a n -> p (a n)")
                pe.matmul(ps[:, 2 + j % 2, 0:P], q_pad[:, j % 4, 0:P], key[:, 0:P], start=True, stop=True)
                pe.matmul(ps[:, 2 + j % 2, P:3 * P], q_pad[:, j % 4, P:2 * P], key, start=True,
                          stop=True).then_inc(sem("scores_ready"), 1)

            def transposes(j):
                half = Pos(4 * it, 4, i) + j // 2
                wait(pe, sem("probs_ready"), (m0 + j).count(1))
                wait(pe, sem(f"pt_copied{j % 2}"), half.count())
                for b in range(3):
                    tr = pe.transpose(ps[:, 4 + j % 2, b * P:(b + 1) * P], logits[:, j % 4, b * P:(b + 1) * P],
                                      ident[:, :])
                tr.then_inc(sem("pt_ready"), 1)

            def outputs(j):
                half = Pos(4 * it, 4, i) + j // 2
                n, bank = bank_of(kind, j)
                wait(pe, sem(f"pt_copied{j % 2}"), half.count(1))
                if j == 0 or bank_of(kind, j - 1)[0] != n:
                    wait(pe, sem("o_taken"), (Pos(ob0, ob_n, i) + n).count(-1))
                if kind == "a":
                    at = j % 4
                    val = [v_a[:, s, bass.ds(i * 512 + 64 * j, 64)] for s in range(2)]
                elif kind == "b":
                    at = j % 4
                    val = [v_b[:, s, (j // 2) % 2, bass.ds((i // 2) * 64, 64)] for s in range(2)]
                else:
                    at = j % 2
                    val = [v_c[:, s, bass.ds(i * 512 + 128 * (j // 2), 128)] for s in range(2)]
                n_out = 128 if kind == "c" else 64
                o = [ps[:, bank, 256 * t + n_out * at:256 * t + n_out * at + n_out] for t in range(2)]
                pe.matmul(o[0], p_t[:, j % 2, 0:P], val[0], start=True, stop=True)
                pe.matmul(o[1], p_t[:, j % 2, P:2 * P], val[0], start=True, stop=False)
                pe.matmul(o[1], p_t[:, j % 2, 2 * P:3 * P], val[1], start=False, stop=True).then_inc(
                    sem("pv_done"), 1)

            wait(pe, sem("evac_s"), Pos(S0["gate"] + it, 1, i).count())
            u = Pos(U0["gate"] + CH * it, CH, i)
            for s in range(CH):
                unit(u + s, s % RING, h_hi, h_lo, UR * s, 0, W, s == 0, s == CH - 1)
                for j in range(8):
                    if SCORES_AT[j] + 1 == s:
                        transposes(j)
                for j in range(8):
                    if SCORES_AT[j] + 2 == s:
                        outputs(j)
                for j in range(8):
                    if SCORES_AT[j] == s:
                        scores(j)

        pe.wait_ge(sem("evac_v"), V0["gate"])
        for kind, n in LOOPS:
            maps(kind, 0)
            with pe.Fori(1, n) as i:
                maps(kind, i)

        def compress():
            pe.wait_ge(sem("w1_loaded"), 32)
            pe.wait_ge(sem("blocks_ready"), 8)
            for v in range(2):
                w1 = (w1k, w1v)[v]
                for hc in range(2):
                    for c in range(KC):
                        mm = pe.matmul(ps[:, 2, 30 * (2 * v + hc):30 * (2 * v + hc) + 30],
                                       w1[:, c, hc * P:(hc + 1) * P], blocks_t[:, v, c, :], start=c == 0,
                                       stop=c == KC - 1)
            mm.then_inc(sem("hidden_mm"), 1)

        def compress2():
            pe.wait_ge(sem("w2_loaded"), 48)
            pe.wait_ge(sem("gelu_ready"), 3)
            for hc in range(2):
                pe.matmul(ps[:, 3, 0:30], w2k[:, hc, :, :].rearrange("p a n -> p (a n)"), hid_k[:, hc, :],
                          start=hc == 0, stop=hc == 1)
            for g in range(2):
                for hc in range(2):
                    mm = pe.matmul(ps[:, 3, 64 + 64 * g:128 + 64 * g],
                                   hid_v[:, hc, g, :, :].rearrange("p a n -> p (a n)"), w2v[:, hc, :],
                                   start=hc == 0, stop=hc == 1)
            mm.then_inc(sem("compressed_mm"), 1)

        def cmp_scores():
            pe.wait_ge(sem("compressed"), 1)
            pe.wait_ge(sem("o_taken"), 22)
            for t in range(2):
                for h in range(16):
                    half = slice(64 * (h % 2), 64 * (h % 2) + 64)
                    at = 16 * (h // 2)
                    mm = pe.matmul(ps[:, 4 + 2 * (h % 2) + t, at:at + NCMP], q_b[half, h // 2, t * P:(t + 1) * P],
                                   kc_t[half, NCMP * (h // 8):NCMP * (h // 8) + NCMP], start=True, stop=True)
            mm.then_inc(sem("cmp_scores"), 1)

        def cmp_transposes():
            pe.wait_ge(sem("cmp_probs"), 1)
            for n in range(8):
                t, q = n // 4, n % 4
                tr = pe.transpose(ps[:, 6 + n // 4, P * (n % 4):P * (n % 4) + P],
                                  cmp_p[:, t, 4 * q:4 * q + 4, :].rearrange("p a n -> p (a n)"), ident[:, :])
            tr.then_inc(sem("cmp_pt"), 1)

        def cmp_outputs():
            pe.wait_ge(sem("cmp_pt_copied"), 1)
            for n in range(8):
                t, q = n // 4, n % 4
                mm = pe.matmul(ps[:, 2 + 2 * t + q // 2, 256 * (q % 2):256 * (q % 2) + 256], cmp_pt[:, n, :],
                               vc_diag[:, q // 2, :, :].rearrange("p a n -> p (a n)"), start=True, stop=True)
            mm.then_inc(sem("cmp_pv"), 1)

        def output_transposes(g):
            for name, value in ((("a_ready", 1),) if g < 2 else (("b_ready", 1),) if g < 6 else (("c_ready", 1),)):
                pe.wait_ge(sem(name), value)
            wait(pe, sem("o_split_lo"), g - 5)
            for c in range(2):
                b = 2 * g + c
                for t in range(2):
                    src = (o_a[:, 0, t, P * b:P * b + P] if b < 4 else
                           o_b[:, t, P * (b - 4):P * (b - 3)] if b < 12 else o_c[:, t, P * (b - 12):P * (b - 11)])
                    tr = pe.transpose(ps[:, 2 + g % 6, 256 * c + P * t:256 * c + P * t + P], src, ident[:, :])
            tr.then_inc(sem("o_transposed"), 1)

        pe_steps = {4: compress, 8: compress2, 10: cmp_scores, 14: cmp_transposes, 16: cmp_outputs}
        for n in range(NSTEP):
            c, s = divmod(n, CH)
            if s == 0:
                pe.wait_ge(sem("evac_s"), S0["gate"] + 9 + c)
            unit(Pos(U0["gate"] + 72 + n), s % RING, h_hi, h_lo, UR * s, 0, W, s == 0, s == CH - 1)
            if n in pe_steps:
                pe_steps[n]()
        pe.wait_ge(sem("b_ready"), 1)
        for g in range(10):
            output_transposes(g)
        pe.wait_ge(sem("o_split_lo"), 10)
        pe.wait_ge(sem("evac_s"), S0["branch"])

        for n in range(4):
            for b in range(3):
                wait(pe, sem("evac_v"), V0["branch"] + 3 * n + b - 2)
                before = sum(BR_UNITS[:b])
                t = Pos(T0["branch"] + n - 1)
                between = [] if (n == 0 or b != 1) else [
                    lambda t=t, n=n: transposed(t, lambda q, h: br_stage[:, (n - 1) % 2, h, q * P:(q + 1) * P],
                                                [("merge_done", n)])]
                chunk(Pos(U0["branch"] + 10 * n + before), BR_UNITS[b], o_hi, o_lo, BR_KC[b], b,
                      s0=(10 * n + before) % RING, between=between)
        transposed(Pos(T0["branch"] + 3), lambda q, h: br_stage[:, 1, h, q * P:(q + 1) * P], [("merge_done", 4)])
        pe.wait_ge(sem("tevac_v"), T0["out"])

        def plain(name, i, n, hi, lo):
            wait(pe, sem("evac_v"), Pos(V0[name], 1, i).count())
            wait(pe, sem("evac_s"), Pos(S0[name], S_OF.get(name, 1), i).count() if S_OF.get(name, 1) else S0[name])
            chunk(Pos(U0[name], n, i), n, hi, lo, 0, 0)

        with pe.Fori(0, 4) as i:
            plain("out", i, CH, h_hi, h_lo)
        pe.wait_ge(sem("evac_v"), V0["up0"])
        pe.wait_ge(sem("evac_s"), S0["up0"])
        norm_transposes(2, mid_normed)

        def up(name, i):
            e, es, t = Pos(V0[name], 2, i), Pos(S0[name], 2, i), Pos(T0[name], 2, i)
            wait(pe, sem("evac_s"), es.count(-1))
            chunk(Pos(U0[name], 2 * CH, i), CH, h_hi, h_lo, 0, 0)
            wait(pe, sem("evac_s"), es.count())
            chunk(Pos(U0[name] + CH, 2 * CH, i), CH, h_hi, h_lo, 0, 1, between=[
                lambda: transposed(t, lambda q, h: up_stage[:, 0, h, q * P:(q + 1) * P], [("evac_v", e.count(1))])])
            transposed(t + 1, lambda q, h: up_stage[:, 1, h, q * P:(q + 1) * P], [("evac_v", e.count(2))])

        for h in range(2):
            pe.wait_ge(sem("evac_s"), S0[f"up{h}"])
            pe.wait_ge(sem("evac_v"), V0[f"up{h}"])
            with pe.Fori(0, 4) as i:
                up(f"up{h}", i)
            pe.wait_ge(sem("tevac_v"), T0[f"down{h}"])
            with pe.Fori(0, 4) as i:
                plain(f"down{h}", i, 16, u_hi, u_lo)
        pe.wait_ge(sem("unit_used"), UNITS)

    @block.scalar
    def _(act):
        def split(u, slot):
            if isinstance(u.count(), int) and u.count() >= UNITS:
                return
            act.wait_ge(sem(f"raw_loaded{slot}"), u.loads())
            wait(act, sem("unit_used"), u.count(1 - RING))
            act.activation(w_hi[:, slot, :, :], raw[:, slot, :, :], ACT.Copy).then_inc(sem("hi_ready"), 1)

        def chunk(u, n, s0=0, after=None):
            for j in range(n):
                split(u + (j + LEAD), (s0 + j + LEAD) % RING)
                for f in (after or {}).get(j, ()):
                    f()

        def copy_out(dst, pair, e, scale=1.0):
            u_done, count = e
            act.wait_ge(sem("unit_used"), u_done)
            act.activation(dst, ps[:, 2 * pair + 1, 0:dst.shape[-1]], ACT.Copy, scale=scale).then_inc(sem("evac_s"), 1)

        def t_out(t, dst):
            act.wait_ge(sem("transposed"), t.count(1))
            act.activation(dst, ps[:, T_BANK + 1, :].rearrange("p (a n) -> p a n", a=2), ACT.Copy).then_inc(
                sem("tevac_s"), 1)

        def t_split(t, dst):
            act.wait_ge(sem("transposed"), t.count(1))
            act.activation(dst, ps[:, T_BANK:T_BANK + 2, :].rearrange("p b (a n) -> p (b a) n", a=2), ACT.Copy
                           ).then_inc(sem("tevac_s"), 1)

        def norm_stats(k, src):
            if k >= 2:
                act.wait_ge(sem(f"ssq_s{k - 1}"), 1)
            act.activation(square_out[:, 1, :] if k else x_normed[:, 1, :], src[:, 1, :], ACT.Square,
                           accum_out=ssq[:, k, 1:2]).then_inc(sem(f"ssq_s{k}"), 1)
            act.wait_ge(sem(f"rstd_steps{k}"), 1)
            act.activation(root[:, k, :], mean[:, k, :], ACT.Sqrt).then_inc(sem(f"root{k}"), 1)

        def norm_split(k, src, dst):
            act.wait_ge(sem(f"rstd_steps{k}"), 6)
            act.activation(dst[:, 1, :], src[:, 1, :], ACT.Copy, scale=rstd[:, k, 1:2]).then_inc(sem(f"normed_s{k}"), 1)
            for g in range(8):
                act.wait_ge(sem(f"norm_t{k}"), g + 1)
                for c in range(2):
                    kc = 2 * g + c
                    act.activation(h_hi[:, kc, :], ps[:, g % 6, 256 * c:256 * c + 256], ACT.Copy,
                                   scale=columns[:, 8 * k + kc:8 * k + kc + 1]).then_inc(sem(f"norm_hi{k}"), 1)

        act.wait_ge(sem("x_loaded1"), 16)
        norm_stats(0, x_in)
        act.wait_ge(sem("columns_ready"), 1)
        norm_split(0, x_in, x_normed)
        act.wait_ge(sem("lam_steps"), 2)
        act.activation(lam2[:, 2:4], lam2[:, 0:2], ACT.Exp).then_inc(sem("lam_exp"), 1)
        for j in range(LEAD):
            split(Pos(j), j)

        def qk(name, i, q_dst, k_dst):
            u = Pos(U0[name], 2 * CH, i)
            t = Pos(T0[name], 2, i)
            chunk(u, CH)
            copy_out(stage[:, 0, 1, :], 0, (u.count(CH), 1), SCALE)
            chunk(u + CH, CH, after={2: [lambda: t_out(t, q_dst[:, bass.ds(i * 4 + 2, 2), :])]})
            copy_out(stage[:, 1, 1, :], 1, (u.count(2 * CH), 1))
            t_out(t + 1, k_dst[:, bass.ds(i * 4 + 2, 2), :])

        def values(name, i, dst):
            u = Pos(U0[name], CH, i)
            chunk(u, CH)
            copy_out(dst[:, 1, bass.ds(i * W, W)], 0, (u.count(CH), 1))

        qk("qk_a", 0, q_a, k_a)
        with act.Fori(1, 3) as i:
            qk("qk_a", i, q_a, k_a)
        with act.Fori(0, 3) as i:
            values("v_a", i, v_a)
        u, t = Pos(U0["q_b"]), Pos(T0["q_b"])
        chunk(u, CH)
        copy_out(stage[:, 0, 1, :], 0, (u.count(CH), 1), SCALE)
        chunk(u + CH, CH, after={2: [lambda: t_out(t, q_b[:, 2:4, :])]})
        copy_out(stage[:, 1, 1, :], 1, (u.count(2 * CH), 1), SCALE)
        t_out(t + 1, q_b[:, 6:8, :])
        u2, t2 = Pos(U0["kv_b"]), Pos(T0["kv_b"])
        chunk(u2, CH)
        copy_out(stage[:, 0, 1, :], 0, (u2.count(CH), 1))
        chunk(u2 + CH, CH, after={2: [lambda: t_out(t2, cmp_t[:, 2:4, :])]})
        copy_out(stage[:, 1, 1, 0:B_LAST], 1, (u2.count(2 * CH), 1))
        t_out(t2 + 1, k_b[:, 2:4, :])
        act.wait_ge(sem("bgate_steps"), 1)
        act.activation(head_gates[:, :, :, :], head_gates[:, :, :, :], ACT.Exp, scale=-1.0).then_inc(sem("bgate_exp"), 1)
        with act.Fori(0, 2) as i:
            qk("qk_c", i, q_c, k_c)
        with act.Fori(0, 2) as i:
            values("v_c", i, v_c)

        def gate_exp(c):
            act.wait_ge(sem("unit_used"), Pos(U0["gate"] + CH, CH, c).count())
            wait(act, sem("gates_stored"), c * 16)
            act.activation(stage[:, 0, :, :], ps[:, 0:2, :], ACT.Exp, scale=-1.0).then_inc(sem("evac_s"), 1)

        def maps(kind, i):
            it = FIRST_IT[kind]
            m0 = Pos(8 * it, 8, i)
            u = Pos(U0["gate"] + CH * it, CH, i)

            def exps(j):
                wait(act, sem("logits_ready"), (m0 + j).count(1))
                if isinstance(i, int) and i == 0:
                    prev = {"a": None, "b": ("a", 2), "c": ("b", 3)}[kind]
                    if prev is not None:
                        n0, n1 = banks_before(prev[0])
                        wait(act, sem("o_taken"), n0 + n1 * prev[1] + bank_of(prev[0], j)[0] + 1)
                else:
                    n0, n1 = banks_before(kind)
                    wait(act, sem("o_taken"), (Pos(n0 - n1, n1, i) + (bank_of(kind, j)[0] + 1)).count())
                for t in range(2):
                    part = logits[:, j % 4, 0:P] if t == 0 else logits[:, j % 4, P:3 * P]
                    e = act.activation(part, part, ACT.Exp, bias=negmax[:, t, j:j + 1], scale=-1.0,
                                       accum_out=sums[:, t, j:j + 1])
                e.then_inc(sem("probs_ready"), 1)

            def pt_copy(j):
                half = Pos(4 * it, 4, i) + j // 2
                act.wait_ge(sem("pt_ready"), (m0 + j).count(1))
                wait(act, sem("pv_done"), (m0 + j).count(-1))
                act.activation(p_t[:, 1, :], ps[:, 5, 0:384], ACT.Copy).then_inc(sem("pt_copied1"), 1)

            for s in range(CH):
                split(u + (s + LEAD), (s + LEAD) % RING)
                for j in range(1, 8, 2):
                    if SCORES_AT[j] + 1 == s:
                        pt_copy(j)
                for j in range(8):
                    if SCORES_AT[j] == s:
                        exps(j)
            gate_exp(i + it)

        for kind, n in LOOPS:
            maps(kind, 0)
            with act.Fori(1, n) as i:
                maps(kind, i)

        def gelu_exp():
            act.wait_ge(sem("gelu_steps"), 5)
            act.activation(hid[:, 2, :], hid[:, 1, :], ACT.Exp, scale=-2.0 * math.sqrt(2.0 / math.pi)).then_inc(
                sem("gelu_exp"), 1)

        def a_exp():
            act.wait_ge(sem("a_steps"), 2)
            act.activation(a_w[:, :, :], a_w[:, :, :], ACT.Exp, scale=-1.0).then_inc(sem("a_exp"), 1)

        def c_root_step():
            act.wait_ge(sem("c_steps"), 3)
            act.activation(c_root[:, :, :], c_mean[:, :, :], ACT.Sqrt).then_inc(sem("c_root"), 1)

        def cmp_exp():
            act.wait_ge(sem("cmp_steps"), 4)
            act.activation(cmp_l[:, :, :, :], cmp_l[:, :, :, :], ACT.Exp).then_inc(sem("cmp_exp"), 1)

        act_steps = {1: a_exp, 6: gelu_exp, 3: c_root_step, 12: cmp_exp}
        for n in range(NSTEP):
            c, s = divmod(n, CH)
            split(Pos(U0["gate"] + 72 + n + LEAD), (s + LEAD) % RING)
            if n in act_steps:
                act_steps[n]()
            if s == CH - 1:
                gate_exp(9 + c)
        for g in range(10):
            act.wait_ge(sem("o_transposed"), g + 1)
            if g == 0:
                act.wait_ge(sem("cmp_pv"), 1)
            act.activation(o_hi[:, 2 * g:2 * g + 2, :], ps[:, 2 + g % 6, :].rearrange("p (a n) -> p a n", a=2),
                           ACT.Copy).then_inc(sem("o_split_hi"), 1)

        for n in range(4):
            chunk(Pos(U0["branch"] + 10 * n), 10, s0=(10 * n) % RING, after={5: [] if n == 0 else [
                lambda n=n: t_split(Pos(T0["branch"] + n - 1), h_hi[:, 4 * (n - 1):4 * n, :])]})
        t_split(Pos(T0["branch"] + 3), h_hi[:, 12:16, :])

        with act.Fori(0, 4) as i:
            u = Pos(U0["out"], CH, i)
            chunk(u, CH)
            copy_out(y[:, 1, bass.ds(i * W, W)], 0, (u.count(CH), 1))
        act.wait_ge(sem("evac_s"), S0["up0"])
        norm_stats(1, y)
        act.wait_ge(sem("mid_ready"), 2)
        norm_stats(2, mid)
        norm_split(2, mid, mid_normed)

        def up(name, i, h):
            u, t = Pos(U0[name], 2 * CH, i), Pos(T0[name], 2, i)

            def relu(c):
                act.wait_ge(sem("unit_used"), (u + CH * (c + 1)).count())
                act.activation(up_stage[:, c, :, :], ps[:, 2 * c:2 * c + 2, :], ACT.Relu).then_inc(sem("evac_s"), 1)

            chunk(u, CH)
            relu(0)
            chunk(u + CH, CH, after={2: [lambda: t_split(t, u_hi[:, bass.ds(i * 8, 4), :])]})
            relu(1)
            t_split(t + 1, u_hi[:, bass.ds(i * 8 + 4, 4), :])

        def down(h, i):
            u = Pos(U0[f"down{h}"], 16, i)
            chunk(u, 16)
            act.wait_ge(sem("unit_used"), u.count(16))
            if h == 0:
                act.activation(y[:, 1, bass.ds(i * W, W)], ps[:, 1, :], ACT.Copy).then_inc(sem("evac_s"), 1)

        for h in range(2):
            with act.Fori(0, 4) as i:
                up(f"up{h}", i, h)
            if h == 0:
                with act.Fori(0, 4) as i:
                    down(h, i)
            else:
                with act.Fori(0, 3) as i:
                    down(h, i)
                down(h, 3)
        act.wait_ge(sem("evac_v"), V0["down1"] + 4)
        norm_stats(3, y)

    @block.vector
    def _(dve):
        dve_count = dve.alloc_register("dve_count")

        def split(u, slot):
            if isinstance(u.count(), int) and u.count() >= UNITS:
                return
            dve.wait_ge(sem("hi_ready"), u.count(1))
            wait(dve, sem("unit_used"), u.count(1 - RING))
            dve.tensor_tensor(w_lo[:, slot, :, :], raw[:, slot, :, :], w_hi[:, slot, :, :].bitcast(F32),
                              ALU.subtract).then_inc(sem("lo_ready"), 1)

        def chunk(u, n, s0=0, after=None):
            for j in range(n):
                split(u + (j + LEAD), (s0 + j + LEAD) % RING)
                for f in (after or {}).get(j, ()):
                    f()

        def copy_out(dst, pair, u_done, scale=None):
            dve.wait_ge(sem("unit_used"), u_done)
            src = ps[:, 2 * pair, 0:dst.shape[-1]]
            if scale is None:
                dve.tensor_copy(dst, src).then_inc(sem("evac_v"), 1)
            else:
                dve.tensor_scalar(dst, src, scale, None, ALU.mult).then_inc(sem("evac_v"), 1)

        def t_out(t, dst):
            dve.wait_ge(sem("transposed"), t.count(1))
            dve.tensor_copy(dst, ps[:, T_BANK, :].rearrange("p (a n) -> p a n", a=2)).then_inc(sem("tevac_v"), 1)

        def t_split(t, dst, hi):
            dve.wait_ge(sem("tevac_s"), t.count(1))
            dve.tensor_tensor(dst, ps[:, T_BANK:T_BANK + 2, :].rearrange("p b (a n) -> p (b a) n", a=2),
                              hi.bitcast(F32), ALU.subtract).then_inc(sem("tevac_v"), 1)

        def chain(name, ops):
            s = sem(name)
            for op in ops:
                done[name] = done.get(name, 0) + 1
                op().then_inc(s, 1)
                dve.wait_ge(s, done[name])

        done = {}

        def norm_stats(k, src):
            name = f"rstd_steps{k}"
            dve.tensor_tensor_reduce(square_out[:, 0, :] if k else x_normed[:, 0, :], src[:, 0, :], src[:, 0, :], 1.0,
                                     0.0, ALU.mult, ALU.add, ssq[:, k, 0:1]).then_inc(sem(f"ssq_v{k}"), 1)
            dve.wait_ge(sem(f"ssq_v{k}"), 1)
            dve.wait_ge(sem(f"ssq_s{k}"), 1)
            chain(name, [lambda: dve.tensor_scalar(mean[:, k, :], ssq[:, k, :], 1.0 / D, EPS, ALU.mult, ALU.add)])
            dve.wait_ge(sem(f"root{k}"), 1)
            a, b, c, n = inv[:, k, :], newton[:, k, :], rstd[:, k, :], mean[:, k, :]
            chain(name, [
                lambda: dve.reciprocal(a, root[:, k, :]),
                lambda: dve.tensor_tensor(b, a, a, ALU.mult),
                lambda: dve.tensor_tensor(b, b, n, ALU.mult),
                lambda: dve.tensor_scalar(b, b, -0.5, 1.5, ALU.mult, ALU.add),
                lambda: dve.tensor_tensor(c, a, b, ALU.mult)])

        def norm_split(k, src, dst):
            dve.tensor_scalar(dst[:, 0, :], src[:, 0, :], rstd[:, k, 0:1], None, ALU.mult).then_inc(
                sem(f"normed_v{k}"), 1)
            for g in range(8):
                dve.wait_ge(sem(f"norm_hi{k}"), 2 * g + 2)
                for c in range(2):
                    kc = 2 * g + c
                    dve.scalar_tensor_tensor(h_lo[:, kc, :], ps[:, g % 6, 256 * c:256 * c + 256],
                                             columns[:, 8 * k + kc:8 * k + kc + 1], h_hi[:, kc, :].bitcast(F32),
                                             ALU.mult, ALU.subtract).then_inc(sem(f"norm_lo{k}"), 1)

        dve.wait_ge(sem("columns_t"), 1)
        dve.tensor_copy(columns[:, :], ps[:, 7, 0:64]).then_inc(sem("columns_ready"), 1)
        dve.wait_ge(sem("table_mm"), 1)
        dve.tensor_tensor(table[:, :], ps[0:48, 6, :], dmask[:, :], ALU.add).then_inc(sem("table_ready"), 1)
        for n in range(2):
            dve.tensor_tensor_reduce(lam_prod[:, n, :], lam_rows[:, 2 * n, :], lam_rows[:, 2 * n + 1, :], 1.0, 0.0,
                                     ALU.mult, ALU.add, lam2[:, n:n + 1]).then_inc(sem("lam_steps"), 1)
        dve.wait_ge(sem("x_loaded0"), 16)
        norm_stats(0, x_in)
        dve.wait_ge(sem("columns_ready"), 1)
        norm_split(0, x_in, x_normed)
        dve.wait_ge(sem("lam_exp"), 1)
        dve.scalar_tensor_tensor(neg_lam[:, :], lam2[:, 3:4], -LAM_INIT, lam2[:, 2:3], ALU.add, ALU.subtract).then_inc(
            sem("neg_lam"), 1)
        for j in range(LEAD):
            split(Pos(j), j)

        def qk(name, i, q_dst, k_dst):
            u = Pos(U0[name], 2 * CH, i)
            t = Pos(T0[name], 2, i)
            chunk(u, CH)
            copy_out(stage[:, 0, 0, :], 0, u.count(CH), SCALE)
            chunk(u + CH, CH, after={2: [lambda: t_out(t, q_dst[:, bass.ds(i * 4, 2), :])]})
            copy_out(stage[:, 1, 0, :], 1, u.count(2 * CH))
            t_out(t + 1, k_dst[:, bass.ds(i * 4, 2), :])

        def values(name, i, dst):
            u = Pos(U0[name], CH, i)
            chunk(u, CH)
            copy_out(dst[:, 0, bass.ds(i * W, W)], 0, u.count(CH))

        qk("qk_a", 0, q_a, k_a)
        with dve.Fori(1, 3) as i:
            qk("qk_a", i, q_a, k_a)
        with dve.Fori(0, 3) as i:
            values("v_a", i, v_a)
        u, t = Pos(U0["q_b"]), Pos(T0["q_b"])
        chunk(u, CH)
        copy_out(stage[:, 0, 0, :], 0, u.count(CH), SCALE)
        chunk(u + CH, CH, after={2: [lambda: t_out(t, q_b[:, 0:2, :])]})
        copy_out(stage[:, 1, 0, :], 1, u.count(2 * CH), SCALE)
        t_out(t + 1, q_b[:, 4:6, :])

        u2, t2 = Pos(U0["kv_b"]), Pos(T0["kv_b"])

        def double(slot, cols, first, wait_for=True):
            dve.wait_ge(sem("evac_v"), V0["kv_b"] + 1 + slot)
            dve.wait_ge(sem("evac_s"), S0["kv_b"] + 1 + slot)
            for h in range(2):
                for a in range(2):
                    last = dve.tensor_copy(dup[:, h, first:first + cols // HD, a, :],
                                           stage[:, slot, h, 0:cols].rearrange("p (q n) -> p q n", n=HD)
                                           if first != 4 else
                                           stage[:, slot, h, 256:256 + cols].rearrange("p (q n) -> p q n", n=HD))
            return last

        chunk(u2, CH)
        copy_out(stage[:, 0, 0, :], 0, u2.count(CH))
        dve.wait_ge(sem("table_stored"), 16)
        double(0, 256, 0).then_inc(sem("dup_ready"), 1)
        double(0, 128, 4)
        dve.tensor_copy(v_b[:, :, 0, :], stage[:, 0, :, 384:512]).then_inc(sem("v_b_copied"), 1)
        chunk(u2 + CH, CH, after={2: [lambda: t_out(t2, cmp_t[:, 0:2, :])]})
        copy_out(stage[:, 1, 0, 0:B_LAST], 1, u2.count(2 * CH))
        double(1, 128, 6).then_inc(sem("dup_ready"), 1)
        dve.tensor_copy(v_b[:, :, 1, :], stage[:, 1, :, 128:256]).then_inc(sem("v_b_copied"), 1)
        for h in range(2):
            last = dve.tensor_copy(head_gates[:, h, :, :], stage[:, 1, h, 256:304].rearrange("p (h b) -> p b h", b=3))
        last.then_inc(sem("bgate_steps"), 1)
        t_out(t2 + 1, k_b[:, 0:2, :])
        dve.wait_ge(sem("bgate_exp"), 1)
        done["bgate_steps"] = 1
        chain("bgate_steps", [
            lambda: dve.tensor_scalar(head_gates[:, :, :, :], head_gates[:, :, :, :], 1.0, None, ALU.add),
            lambda: dve.reciprocal(head_gates[:, :, :, :], head_gates[:, :, :, :])])
        with dve.Fori(0, 2) as i:
            qk("qk_c", i, q_c, k_c)
        with dve.Fori(0, 2) as i:
            values("v_c", i, v_c)

        def gate_sigmoid(c):
            dve.wait_ge(sem("evac_s"), Pos(S0["gate"] + 1, 1, c).count())
            dve.tensor_scalar(stage[:, 0, :, :], stage[:, 0, :, :], 1.0, None, ALU.add).then_inc(sem("gate_plus1"), 1)
            dve.wait_ge(sem("gate_plus1"), Pos(1, 1, c).count())
            dve.reciprocal(stage[:, 0, :, :], stage[:, 0, :, :]).then_inc(sem("evac_v"), 1)

        def maps(kind, i):
            it = FIRST_IT[kind]
            m0 = Pos(8 * it, 8, i)
            u = Pos(U0["gate"] + CH * it, CH, i)
            ob0, ob_n = banks_before(kind)

            def add_bias(j):
                wait(dve, sem("scores_ready"), (m0 + j).count(1))
                loads = Pos(2 * it + j // 4 + 1, 2, i)
                dve.wait_ge(sem(f"bias_loaded{j % 4}"), Pos(16 * loads.k, 32, i).count())
                transposed_before = held(dve, dve_count, (m0 + j).count(-3))
                dve.wait_ge(sem("table_ready"), 1)
                wait(dve, sem("pt_ready"), transposed_before)
                dve.tensor_tensor_reduce(logits[:, j % 4, 0:P], ps[:, 2 + j % 2, 0:P], bias[:, j % 4, P - 1::-1], -1.0,
                                         3.0e38, ALU.add, ALU.min, negmax[:, 0, j:j + 1])
                dve.tensor_tensor_reduce(logits[:, j % 4, P:3 * P], ps[:, 2 + j % 2, P:3 * P], bias[:, j % 4, ::-1],
                                         -1.0, 3.0e38, ALU.add, ALU.min, negmax[:, 1, j:j + 1]).then_inc(
                    sem("logits_ready"), 1)

            def pt_copy(j):
                dve.wait_ge(sem("pt_ready"), (m0 + j).count(1))
                wait(dve, sem("pv_done"), (m0 + j).count(-1))
                dve.tensor_copy(p_t[:, 0, :], ps[:, 4, 0:384]).then_inc(sem("pt_copied0"), 1)

            def take(j):
                n, bank = bank_of(kind, j)
                dve.wait_ge(sem("pv_done"), (m0 + j).count(1))
                if kind == "a":
                    dve.tensor_copy(o_a[:, bass.ds(i, 1), :, 256 * n:256 * n + 256].rearrange("p a t n -> p (a t) n"),
                                    ps[:, bank, :].rearrange("p (t n) -> p t n", t=2))
                    dve.tensor_copy(a_negmax[:, :, bass.ds(i * 8 + 4 * n, 4)], negmax[:, :, 4 * n:4 * n + 4])
                    dve.tensor_copy(a_sums[:, :, bass.ds(i * 8 + 4 * n, 4)], sums[:, :, 4 * n:4 * n + 4]).then_inc(
                        sem("o_taken"), 1)
                    return
                steps = Pos(0, 6, i) + 3 * n if kind == "b" else Pos(24, 12, i) + 3 * n
                s = sem("take_steps")
                if kind == "b":
                    cf = coef[:, :, 0:4]
                    dve.reciprocal(rsum[:, :, :], sums[:, :, 4 * n:4 * n + 4]).then_inc(s, 1)
                    dve.wait_ge(s, steps.count(1))
                    dve.tensor_tensor(
                        coef[:, :, :].rearrange("p t (b h) -> p t b h", b=2),
                        rsum[:, :, :].rearrange("p t (b h) -> p t b h", b=2),
                        head_gates[:, :, 1:3, bass.ds(i * 4 + 2 * n, 2)], ALU.mult).then_inc(s, 1)
                    width, dst = 64, o_b[:, :, bass.ds(i * 256 + 128 * n, 128)]
                else:
                    cf = coef[:, :, 0:2]
                    dve.reciprocal(coef[:, :, 0:2], sums[:, :, 2 * n:2 * n + 2]).then_inc(s, 1)
                    dve.wait_ge(s, steps.count(1))
                    dve.tensor_scalar(coef[:, :, 1:2], coef[:, :, 1:2], neg_lam[:, 0:1], None, ALU.mult).then_inc(s, 1)
                    width, dst = 128, o_c[:, :, bass.ds(i * 512 + 128 * n, 128)]
                dve.wait_ge(s, steps.count(2))
                k = 256 // width
                dve.tensor_tensor(merged[:, :, :, :].rearrange("p t b n -> p t (b n)").rearrange(
                    "p t (k n) -> p t k n", k=k), ps[:, bank, :].rearrange("p (t k n) -> p t k n", t=2, k=k),
                    cf.rearrange("p t (k a) -> p t k a", a=1).to_broadcast([P, 2, k, width]), ALU.mult).then_inc(s, 1)
                dve.wait_ge(s, steps.count(3))
                dve.tensor_tensor(dst, merged[:, :, 0, :], merged[:, :, 1, :], ALU.add).then_inc(sem("o_taken"), 1)

            ends = bank_last(kind)
            for s in range(CH):
                split(u + (s + LEAD), (s + LEAD) % RING)
                for j in range(0, 8, 2):
                    if SCORES_AT[j] + 1 == s:
                        pt_copy(j)
                for j in range(8):
                    if SCORES_AT[j] == s:
                        add_bias(j)
                for j in ends:
                    if SCORES_AT[j] + 3 == s:
                        take(j)
            gate_sigmoid(i + it)
            for j in ends:
                if SCORES_AT[j] + 3 >= CH:
                    take(j)

        for kind, n in LOOPS:
            maps(kind, 0)
            with dve.Fori(1, n) as i:
                maps(kind, i)

        def blocks():
            for v in range(2):
                for g in range(2):
                    for par in range(2):
                        half = slice(64 * par, 64 * par + 64)
                        t = cmp_t[half, 2 * v + g, :]
                        src = bass.AP(t.tensor, t.offset + par, [list(t.ap[0]), [2, KC], [CSTRIDE, NCMP]])
                        pos = columns[half, 32 + 16 * v:48 + 16 * v].rearrange("p (c a) -> p c a", a=1)
                        dve.tensor_tensor(blocks_t[half, v, :, NCMP * g:NCMP * g + NCMP], src,
                                          pos.to_broadcast([64, KC, NCMP]), ALU.add).then_inc(sem("blocks_ready"), 1)

        def a_first():
            w = a_w[:, :, :].rearrange("p t (g h) -> p t g h", g=3)
            chain("a_steps", [
                lambda: dve.tensor_reduce(a_min[:, :, :], a_negmax[:, :, :].rearrange("p t (g h) -> p t h g", g=3), AX,
                                          ALU.min),
                lambda: dve.tensor_tensor(w, a_negmax[:, :, :].rearrange("p t (g h) -> p t g h", g=3),
                                          a_min[:, :, :].rearrange("p t (a h) -> p t a h", a=1).to_broadcast(
                                              [P, 2, 3, 8]), ALU.subtract)])

        def a_second():
            dve.wait_ge(sem("a_exp"), 1)
            w = a_w[:, :, :].rearrange("p t (g h) -> p t g h", g=3)
            ops = [
                lambda: dve.tensor_tensor(a_ws[:, :, :], a_w[:, :, :], a_sums[:, :, :], ALU.mult),
                lambda: dve.tensor_reduce(a_tot[:, :, :], a_ws[:, :, :].rearrange("p t (g h) -> p t h g", g=3), AX,
                                          ALU.add),
                lambda: dve.reciprocal(a_tot[:, :, :], a_tot[:, :, :]),
                lambda: dve.tensor_tensor(w, w, a_tot[:, :, :].rearrange("p t (a h) -> p t a h", a=1).to_broadcast(
                    [P, 2, 3, 8]), ALU.mult)]

            def scaled(g):
                o = o_a[:, g, :, :].rearrange("p t (h n) -> p t h n", n=HD)
                return lambda: dve.tensor_tensor(o, o, a_w[:, :, 8 * g:8 * g + 8].rearrange(
                    "p t (h a) -> p t h a", a=1).to_broadcast([P, 2, 8, HD]), ALU.mult)

            ops += [scaled(g) for g in range(3)]
            ops.append(lambda: dve.tensor_tensor(o_a[:, 0, :, :], o_a[:, 0, :, :], o_a[:, 1, :, :], ALU.add))
            chain("a_steps", ops)
            dve.tensor_tensor(o_a[:, 0, :, :], o_a[:, 0, :, :], o_a[:, 2, :, :], ALU.add).then_inc(sem("a_ready"), 1)

        c_heads = o_c[:, :, :].rearrange("p t (h n) -> p (t h) n", n=P)

        def c_first():
            sq = c_square[:, :, :]
            dve.wait_ge(sem("a_ready"), 1)
            chain("c_steps", [
                lambda: dve.tensor_tensor(sq, c_heads, c_heads, ALU.mult),
                lambda: dve.tensor_reduce(c_ssq[:, :, :].rearrange("p t h -> p (t h)"), sq, AX, ALU.add),
                lambda: dve.tensor_scalar(c_mean[:, :, :], c_ssq[:, :, :], 1.0 / P, EPS, ALU.mult, ALU.add)])

        def c_second():
            dve.wait_ge(sem("c_root"), 1)
            flat = lambda a: a[:, :, :].rearrange("p t h -> p (t h)")
            chain("c_steps", [
                lambda: dve.reciprocal(flat(c_rstd), flat(c_root)),
                lambda: dve.tensor_tensor(flat(c_ssq), flat(c_rstd), flat(c_rstd), ALU.mult),
                lambda: dve.tensor_tensor(flat(c_ssq), flat(c_ssq), flat(c_mean), ALU.mult),
                lambda: dve.tensor_scalar(flat(c_ssq), flat(c_ssq), -0.5, 1.5, ALU.mult, ALU.add),
                lambda: dve.tensor_tensor(flat(c_rstd), flat(c_rstd), flat(c_ssq), ALU.mult),
                lambda: dve.tensor_scalar(flat(c_rstd), flat(c_rstd), 1.0 - LAM_INIT, None, ALU.mult),
                lambda: dve.tensor_tensor(c_heads, c_heads, flat(c_rstd).rearrange("p (h a) -> p h a", a=1)
                                          .to_broadcast([P, 16, P]), ALU.mult)])
            dve.tensor_tensor(c_heads, c_heads, sub_gain[:, :].rearrange("p (a n) -> p a n", a=1)
                              .to_broadcast([P, 16, P]), ALU.mult).then_inc(sem("c_ready"), 1)

        def gelu_first():
            dve.wait_ge(sem("hidden_mm"), 1)
            h, a = hid[:, 0, :], hid[:, 1, :]
            chain("gelu_steps", [
                lambda: dve.tensor_copy(h, ps[:, 2, 0:120]),
                lambda: dve.tensor_tensor(a, h, h, ALU.mult),
                lambda: dve.tensor_scalar(a, a, 0.044715, 1.0, ALU.mult, ALU.add),
                lambda: dve.tensor_tensor(a, a, h, ALU.mult),
                lambda: dve.tensor_scalar(a, a, -50.0, None, ALU.max)])

        def gelu_second():
            dve.wait_ge(sem("gelu_exp"), 1)
            h, e = hid[:, 0, :], hid[:, 2, :]
            chain("gelu_steps", [
                lambda: dve.tensor_scalar(e, e, 1.0, None, ALU.add),
                lambda: dve.reciprocal(e, e)])
            dve.tensor_tensor(hid_k[:, :, :].rearrange("p a n -> p (a n)"), h[:, 0:60], e[:, 0:60], ALU.mult).then_inc(
                sem("gelu_ready"), 1)
            dve.wait_ge(sem("cmp_zero"), 3)
            chain("gelu_steps", [lambda: dve.tensor_tensor(h[:, 60:120], h[:, 60:120], e[:, 60:120], ALU.mult)])
            for g in range(2):
                dve.tensor_copy(hid_v[:, :, g, :, 0:NCMP], h[:, 60:120].rearrange(
                    "p (c g n) -> p c g n", c=2, g=2)[:, :, g, :].rearrange("p c (a n) -> p c a n", a=1)
                    .to_broadcast([P, 2, 4, NCMP])).then_inc(sem("gelu_ready"), 1)

        def compressed():
            dve.wait_ge(sem("compressed_mm"), 1)
            for q in range(4):
                part = slice(32 * q, 32 * q + 32)
                dve.tensor_copy(vc_diag[part, :, q, :], ps[part, 3, 64:192].rearrange("p (g n) -> p g n", g=2))
            dve.tensor_copy(kc_t[:, :], ps[:, 3, 0:30]).then_inc(sem("compressed"), 1)

        def cmp_first():
            dve.wait_ge(sem("cmp_scores"), 1)
            for t in range(2):
                for odd in range(2):
                    last = dve.tensor_tensor(
                        cmp_l[:, t, odd::2, :], ps[:, 4 + 2 * odd + t, 0:128].rearrange("p (h n) -> p h n", h=8)[
                            :, :, 0:NCMP], bmask[:, t, :].rearrange("p (a n) -> p a n", a=1).to_broadcast(
                                [P, 8, NCMP]), ALU.add)
            last.then_inc(sem("cmp_steps"), 1)
            dve.wait_ge(sem("cmp_steps"), 1)
            done["cmp_steps"] = 1
            l4 = cmp_l[:, :, :, :].rearrange("p t h n -> p (t h) n")
            mx = m_max[:, :, :].rearrange("p t h -> p (t h)")
            chain("cmp_steps", [
                lambda: dve.tensor_reduce(mx, l4, AX, ALU.max),
                lambda: dve.tensor_scalar(mx, mx, 0.5 * NEG, None, ALU.max),
                lambda: dve.tensor_tensor(l4, l4, mx.rearrange("p (h a) -> p h a", a=1).to_broadcast([P, 32, NCMP]),
                                          ALU.subtract)])

        def cmp_second():
            dve.wait_ge(sem("cmp_exp"), 1)
            l4 = cmp_l[:, :, :, :].rearrange("p t h n -> p (t h) n")
            sm = m_sum[:, :, :].rearrange("p t h -> p (t h)")
            chain("cmp_steps", [
                lambda: dve.tensor_reduce(sm, l4, AX, ALU.add),
                lambda: dve.tensor_scalar(sm, sm, TINY, None, ALU.max),
                lambda: dve.reciprocal(sm, sm),
                lambda: dve.tensor_tensor(m_coef[:, :, :], m_sum[:, :, :], head_gates[:, :, 0, :], ALU.mult)])
            dve.tensor_tensor(cmp_p[:, :, :, 0:NCMP].rearrange("p t h n -> p (t h) n"), l4,
                              m_coef[:, :, :].rearrange("p t (h a) -> p (t h) a", a=1).to_broadcast([P, 32, NCMP]),
                              ALU.mult).then_inc(sem("cmp_probs"), 1)

        def cmp_third():
            dve.wait_ge(sem("cmp_pt"), 1)
            dve.tensor_copy(cmp_pt[:, :, :].rearrange("p (b a) n -> p b (a n)", b=2), ps[:, 6:8, :]).then_inc(
                sem("cmp_pt_copied"), 1)

        def cmp_fourth():
            dve.wait_ge(sem("cmp_pv"), 1)
            for t in range(2):
                o = o_b[:, t, :].rearrange("p (b n) -> p b n", b=2)
                last = dve.tensor_tensor(o, ps[:, 2 + 2 * t:4 + 2 * t, :], o, ALU.add)
            last.then_inc(sem("b_ready"), 1)

        dve_steps = {0: [blocks, a_first], 2: [a_second], 3: [c_first], 5: [gelu_first, c_second], 7: [gelu_second],
                     9: [compressed], 11: [cmp_first], 13: [cmp_second], 15: [cmp_third], 17: [cmp_fourth]}
        for n in range(NSTEP):
            c, s = divmod(n, CH)
            split(Pos(U0["gate"] + 72 + n + LEAD), (s + LEAD) % RING)
            if s == CH - 1:
                gate_sigmoid(9 + c)
            for f in dve_steps.get(n, ()):
                if n == 0 and f is a_first:
                    dve.wait_ge(sem("o_taken"), 22)
                f()
        for g in range(10):
            dve.wait_ge(sem("o_split_hi"), g + 1)
            dve.tensor_tensor(o_lo[:, 2 * g:2 * g + 2, :], ps[:, 2 + g % 6, :].rearrange("p (a n) -> p a n", a=2),
                              o_hi[:, 2 * g:2 * g + 2, :].bitcast(F32), ALU.subtract).then_inc(sem("o_split_lo"), 1)

        def merge(n, b):
            dve.wait_ge(sem("unit_used"), U0["branch"] + 10 * n + sum(BR_UNITS[:b + 1]))
            if b == 0:
                dve.wait_ge(sem(f"gates_loaded{n % 2}"), 16 * (n // 2 + 1))
            acc, gate, dst = ps[:, 2 * b:2 * b + 2, :], gates_in[:, n % 2, b, :, :], br_stage[:, n % 2, :, :]
            if b == 0:
                dve.tensor_tensor(dst, acc, gate, ALU.mult).then_inc(sem("evac_v"), 1)
                return
            dve.tensor_tensor(br_tmp[:, :, :], acc, gate, ALU.mult).then_inc(sem("evac_v"), 1)
            dve.wait_ge(sem("evac_v"), V0["branch"] + 3 * n + b + 1)
            add = dve.tensor_tensor(dst, dst, br_tmp[:, :, :], ALU.add)
            add.then_inc(sem("merge_done" if b == 2 else "merge_steps"), 1)
            if b == 1:
                dve.wait_ge(sem("merge_steps"), n + 1)

        for n in range(4):
            u0 = U0["branch"] + 10 * n
            for b in range(3):
                before = sum(BR_UNITS[:b])
                for j in range(BR_UNITS[b]):
                    split(Pos(u0 + before + j + LEAD), (10 * n + before + j + LEAD) % RING)
                    if n > 0 and before + j == 5:
                        t_split(Pos(T0["branch"] + n - 1), h_lo[:, 4 * (n - 1):4 * n, :], h_hi[:, 4 * (n - 1):4 * n, :])
                merge(n, b)
        t_split(Pos(T0["branch"] + 3), h_lo[:, 12:16, :], h_hi[:, 12:16, :])

        with dve.Fori(0, 4) as i:
            u = Pos(U0["out"], CH, i)
            chunk(u, CH)
            copy_out(y[:, 0, bass.ds(i * W, W)], 0, u.count(CH))

        def residual(k, ready):
            dve.wait_ge(sem("gain_loaded"), 16 * (1 if k == 1 else 2))
            for t in range(2):
                dve.scalar_tensor_tensor(y[:, t, :], y[:, t, :], rstd[:, k, t:t + 1], gain_row[:, :], ALU.mult,
                                         ALU.mult).then_inc(sem(f"scaled{k}"), 1)
            for t in range(2):
                dve.wait_ge(sem(f"scaled{k}"), t + 1)
                dve.tensor_tensor(mid[:, t, :], mid[:, t, :], y[:, t, :], ALU.add).then_inc(sem(ready), 1)

        dve.wait_ge(sem("evac_v"), V0["up0"])
        dve.wait_ge(sem("evac_s"), S0["up0"])
        norm_stats(1, y)
        dve.wait_ge(sem("x_again"), 32)
        residual(1, "mid_ready")
        dve.wait_ge(sem("mid_ready"), 2)
        norm_stats(2, mid)
        norm_split(2, mid, mid_normed)

        def up(name, i):
            u, t, e, es = Pos(U0[name], 2 * CH, i), Pos(T0[name], 2, i), Pos(V0[name], 2, i), Pos(S0[name], 2, i)

            def square(c):
                dve.wait_ge(sem("evac_s"), es.count(c + 1))
                dve.tensor_tensor(up_stage[:, c, :, :], up_stage[:, c, :, :], up_stage[:, c, :, :], ALU.mult).then_inc(
                    sem("evac_v"), 1)

            chunk(u, CH)
            square(0)
            chunk(u + CH, CH, after={2: [lambda: t_split(t, u_lo[:, bass.ds(i * 8, 4), :],
                                                         u_hi[:, bass.ds(i * 8, 4), :])]})
            square(1)
            t_split(t + 1, u_lo[:, bass.ds(i * 8 + 4, 4), :], u_hi[:, bass.ds(i * 8 + 4, 4), :])

        def down(h, i):
            u = Pos(U0[f"down{h}"], 16, i)
            chunk(u, 16)
            dve.wait_ge(sem("unit_used"), u.count(16))
            part = y[:, 0, bass.ds(i * W, W)]
            if h == 0:
                dve.tensor_copy(part, ps[:, 0, :]).then_inc(sem("evac_v"), 1)
            else:
                part = y[:, :, bass.ds(i * W, W)]
                dve.tensor_tensor(part, ps[:, 0:2, :], part, ALU.add).then_inc(sem("evac_v"), 1)

        for h in range(2):
            with dve.Fori(0, 4) as i:
                up(f"up{h}", i)
            if h == 0:
                with dve.Fori(0, 4) as i:
                    down(h, i)
            else:
                with dve.Fori(0, 3) as i:
                    down(h, i)
                down(h, 3)
        dve.wait_ge(sem("evac_v"), V0["down1"] + 4)
        norm_stats(3, y)
        residual(3, "result_ready")


def _constants():
    import numpy as np

    exact, buckets = 16, 32
    dist = np.arange(512) - 127
    d = np.maximum(dist, 0)
    logd = np.log(np.maximum(d, 1).astype(np.float32) / np.float32(exact))
    far = exact + (logd / np.float32(math.log(2048 / exact)) * (buckets - exact)).astype(np.int32)
    bucket = np.where(d < exact, d, np.minimum(far, buckets - 1))
    onehot = (bucket[None, :] == np.arange(buckets)[:, None]).astype(np.float32)
    mask = np.zeros((48, 512), np.float32)
    mask[:, dist < 0] = NEG
    for g, (window, step) in enumerate(((128, 1), (512, 4), (2048, 16))):
        mask[8 * g:8 * g + 8, (dist < 0) | (dist > window) | (dist % step != 0)] = NEG
    t = np.arange(SEQ)
    seen = (np.arange(NCMP) * CSTRIDE + 31)[None, :] <= t[:, None]
    blocks = np.where(seen, 0.0, NEG).astype(np.float32).reshape(2, P, NCMP).transpose(1, 0, 2)
    return {"identity": np.eye(P, dtype=np.float32), "bucket_onehot": onehot, "distance_mask": mask,
            "block_mask": np.ascontiguousarray(blocks)}


_INS = ["x", "rel_bias", "w_in", "cmp_k_pos", "cmp_v_pos", "cmp_k_w1", "cmp_k_w2", "cmp_v_w1", "cmp_v_w2",
        "diff_lambda", "diff_norm", "w_branch_a", "w_branch_b", "w_branch_c", "w_out", "norm_mix_pre",
        "norm_mix_post", "norm_mlp_pre", "norm_mlp_post", "w_up", "w_down"]


def kernel(**inputs):
    import numpy as np
    import concourse.bacc as bacc
    from concourse.bass_utils import run_bass_kernel_spmd

    nc = bacc.Bacc("TRN2", target_bir_lowering=False, num_devices=1)
    given = {name: np.ascontiguousarray(inputs[name]) for name in _INS}
    given.update(_constants())
    arrays, args = {}, []
    for name, a in given.items():
        arrays[f"in_{name}_dram"] = a
        args.append(nc.dram_tensor(f"in_{name}_dram", a.shape, mybir.dt.from_np(a.dtype), kind="ExternalInput").ap())
    args.append(nc.dram_tensor("out_0_dram", (1, SEQ, D), F32, kind="ExternalOutput").ap())
    trunk(nc, *args)
    r = run_bass_kernel_spmd(nc, [arrays], core_ids=[0])
    return r.results[0]["out_0_dram"]
```

```python
import math
from contextlib import ExitStack

import concourse.bass as bass
from concourse import mybir
from concourse.alu_op_type import AluOpType as ALU

F32 = mybir.dt.float32
F32R = mybir.dt.float32r
ACT = mybir.ActivationFunctionType
AX = mybir.AxisListType.X

P = 128
D = 2048
SEQ = 256
HD = 64
DFF = 8192
KC = D // P
W = 512
UR = 2
RING = 4
LEAD = 3
EPS = 1e-6
SCALE = HD ** -0.5
TINY = 1e-30
NEG = -1e30
LAM_INIT = 0.8 - 0.6
NCMP = 15
CSTRIDE = 16

A_Q, A_K, A_V = 0, 1536, 3072
B_Q, B_KV = 4608, 5632
C_Q, C_K, C_V = 6448, 7472, 8496
M_G = 9520
B_LAST = 304

CH = KC // UR
ORDER = [("qk_a", 6, CH), ("v_a", 3, CH), ("q_b", 2, CH), ("kv_b", 2, CH), ("qk_c", 4, CH), ("v_c", 2, CH),
         ("gate", 12, CH), ("branch", 4, 10), ("out", 4, CH),
         ("up0", 8, CH), ("down0", 4, 16), ("up1", 8, CH), ("down1", 4, 16)]
U0, C0 = {}, {}
_u = _c0 = 0
for _n, _c, _k in ORDER:
    U0[_n], C0[_n] = _u, _c0
    _u += _c * _k
    _c0 += 3 * _c if _n == "branch" else _c
UNITS = _u
V_OF = {"gate": 0, "branch": 6, "down1": 2}
S_OF = {"branch": 0, "down1": 0, "gate": 2, "up0": 2, "up1": 2}
T_OF = {"v_a": 0, "v_c": 0, "gate": 0, "out": 0, "down0": 0, "down1": 0}
V0, S0, T0 = {}, {}, {}
_v = _s = _t = 0
for _n, _c, _k in ORDER:
    V0[_n], S0[_n], T0[_n] = _v, _s, _t
    _v += _c * V_OF.get(_n, 1)
    _s += _c * S_OF.get(_n, 1)
    _t += _c * T_OF.get(_n, 1)

SCORES_AT = [0, 0, 1, 2, 3, 3, 4, 5]
GATE_PARTS = {1: (0, 256), 2: (256, 384), 3: (384, 512), 4: (512, 768), 5: (768, 1024)}
NSTEP = 24
O_PAIRS = [0, 1, 6, 7, 8, 9, 2, 3, 4, 5]
O_BANKS = [4, 5, 6, 7, 4, 5, 6, 7, 2, 3]
O_AT = [2, 2, 3, 3, 4, 5, 15, 15, 17, 18]


class Pos:

    def __init__(self, k, per=0, i=0):
        self.k, self.per, self.i = k, per, i

    def __add__(self, n):
        return Pos(self.k + n, self.per, self.i)

    def count(self, n=0):
        if isinstance(self.i, int):
            return self.k + n + self.per * self.i
        return self.i * self.per + (self.k + n)

    def loads(self):
        r = 16 * (self.k // RING + 1)
        if isinstance(self.i, int):
            return r + 16 * (self.per // RING) * self.i
        return self.i * (16 * (self.per // RING)) + r


def wait(eng, sem, value):
    if not (isinstance(value, int) and value <= 0):
        eng.wait_ge(sem, value)


def held(eng, register, value):
    if isinstance(value, int):
        return value
    eng.reg_add(register, eng.snap(value - 1), 1)
    return register


def trunk(nc, x, rel_bias, w_in, cmp_k_pos, cmp_v_pos, cmp_k_w1, cmp_k_w2, cmp_v_w1, cmp_v_w2, diff_lambda,
          diff_norm, w_branch_a, w_branch_b, w_branch_c, w_out, norm_mix_pre, norm_mix_post, norm_mlp_pre,
          norm_mlp_post, w_up, w_down, identity, bucket_onehot, distance_mask, block_mask, out):
    bias_table = nc.dram_tensor("bias_table", (48, 512), F32, kind="Internal").ap()
    gate_dram = nc.dram_tensor("gate_dram", (P, 12, 1024), F32, kind="Internal").ap()
    hankel = bass.AP(bias_table.tensor, 0, [[512, 48], [1, P], [1, 256]])

    ctx = ExitStack()
    sems = {}

    def sem(name):
        if name not in sems:
            sems[name] = ctx.enter_context(nc.semaphore(name))
        return sems[name]

    base = 16512
    regions = {"small": [0, 5888], "ring": [5888, 49152], "h": [55040, 32768], "u": [87808, 65536],
               "f": [153344, 59392]}
    marks = {k: v[0] for k, v in regions.items()}

    def put(region, name, shape, dt=F32, at=None):
        size = 4 * math.prod(shape[1:])
        off = marks[region] if at is None else regions[region][0] + at
        off = (off + 31) // 32 * 32
        assert off + size <= regions[region][0] + regions[region][1], (name, off + size)
        if at is None:
            marks[region] = off + size
        return nc.alloc_sbuf_tensor_at(name, shape, dt, offset=base + off)

    ident = put("small", "ident", [P, P])
    columns = put("small", "columns", [P, 64])
    ssq = put("small", "ssq", [P, 4, 2])
    mean = put("small", "mean", [P, 4, 2])
    root = put("small", "root", [P, 4, 2])
    inv = put("small", "inv", [P, 4, 2])
    newton = put("small", "newton", [P, 4, 2])
    rstd = put("small", "rstd", [P, 4, 2])
    head_gates = put("small", "head_gates", [P, 2, 3, 16])
    negmax = put("small", "negmax", [P, 2, 8])
    sums = put("small", "sums", [P, 2, 8])
    coef = put("small", "coef", [P, 2, 4])
    rsum = put("small", "rsum", [P, 2, 4])
    a_negmax = put("small", "a_negmax", [P, 2, 24])
    a_sums = put("small", "a_sums", [P, 2, 24])
    a_min = put("small", "a_min", [P, 2, 8])
    a_w = put("small", "a_w", [P, 2, 24])
    a_ws = put("small", "a_ws", [P, 2, 24])
    a_tot = put("small", "a_tot", [P, 2, 8])
    lam2 = put("small", "lam2", [P, 4])
    neg_lam = put("small", "neg_lam", [P, 1])
    c_ssq = put("small", "c_ssq", [P, 2, 8])
    c_mean = put("small", "c_mean", [P, 2, 8])
    c_root = put("small", "c_root", [P, 2, 8])
    c_rstd = put("small", "c_rstd", [P, 2, 8])
    sub_gain = put("small", "sub_gain", [P, P])
    bmask = put("small", "bmask", [P, 2, NCMP])
    m_max = put("small", "m_max", [P, 2, 16])
    m_sum = put("small", "m_sum", [P, 2, 16])
    m_coef = put("small", "m_coef", [P, 2, 16])
    kc_t = put("small", "kc_t", [P, 2 * NCMP])

    raw = put("ring", "raw", [P, RING, UR, W])
    w_hi = put("ring", "w_hi", [P, RING, UR, W], F32R)
    w_lo = put("ring", "w_lo", [P, RING, UR, W], F32R)
    h_hi = put("h", "h_hi", [P, KC, SEQ], F32R)
    h_lo = put("h", "h_lo", [P, KC, SEQ], F32R)

    q_c = put("u", "q_c", [P, 8, SEQ])
    k_c = put("u", "k_c", [P, 8, SEQ])
    v_c = put("u", "v_c", [P, 2, 1024])
    v_a = put("u", "v_a", [P, 2, 1536])
    logits = put("u", "logits", [P, 4, 384])
    blocks_t = put("u", "blocks_t", [P, 2, KC, 2 * NCMP])
    q_b = put("u", "q_b", [P, 8, SEQ])
    k_b = put("u", "k_b", [P, 4, SEQ])
    v_b = put("u", "v_b", [P, 2, 2, P])
    cmp_t = put("u", "cmp_t", [P, 4, SEQ])
    x_in = put("u", "x_in", [P, 2, D], at=0)
    x_normed = put("u", "x_normed", [P, 2, D], at=16384)
    w1k = put("u", "w1k", [P, KC, 256], at=0)
    w1v = put("u", "w1v", [P, KC, 256], at=16384)
    hid = put("u", "hid", [P, 3, 8 * NCMP], at=43008)
    hid_k = put("u", "hid_k", [P, 2, 2 * NCMP], at=43008 + 1536)
    hid_v = put("u", "hid_v", [P, 2, 2, 4, 32], at=40960)
    o_hi = put("u", "o_hi", [P, 20, SEQ], F32R, at=0)
    o_lo = put("u", "o_lo", [P, 20, SEQ], F32R, at=20480)
    u_hi = put("u", "u_hi", [P, 32, SEQ], F32R, at=0)
    u_lo = put("u", "u_lo", [P, 32, SEQ], F32R, at=32768)
    mid_normed = put("u", "mid_normed", [P, 2, D], at=0)
    square_out = put("u", "square_out", [P, 2, D], at=32768)

    o_a = put("f", "o_a", [P, 3, 2, 512])
    k_a = put("f", "k_a", [P, 12, SEQ])
    q_a = put("f", "q_a", [P, 12, SEQ])
    stage = put("f", "stage", [P, 2, 2, W])
    q_pad = put("f", "q_pad", [P, 4, SEQ])
    bias = put("f", "bias", [P, 4, SEQ])
    p_t = put("f", "p_t", [P, 2, 384])
    w2k = put("f", "w2k", [P, 2, 2, HD])
    w2v = put("f", "w2v", [P, 2, HD])
    o_c = put("f", "o_c", [P, 2, 1024], at=12288)
    o_b = put("f", "o_b", [P, 2, 1024], at=24576)
    merged = put("f", "merged", [P, 2, 2, 128], at=36864 + 4096)
    dup = put("f", "dup", [P, 2, 8, 2, HD], at=0)
    rows64 = put("f", "rows64", [64, P], at=0)
    onehot = put("f", "onehot", [32, 512], at=1024)
    dmask = put("f", "dmask", [48, 512], at=3072)
    rel = put("f", "rel", [32, 48], at=5120)
    table = put("f", "table", [48, 512], at=6144)
    lam_rows = put("f", "lam_rows", [P, 4, HD], at=8192)
    lam_prod = put("f", "lam_prod", [P, 2, HD], at=9216)
    cmp_l = put("f", "cmp_l", [P, 2, 16, NCMP], at=36864 + 8192 + 4096)
    cmp_p = put("f", "cmp_p", [P, 2, 16, 32], at=36864 + 8192)
    cmp_pt = put("f", "cmp_pt", [P, 8, P], at=36864 + 4096)
    vc_diag = put("f", "vc_diag", [P, 2, 4, HD], at=36864 + 16384)
    c_square = put("f", "c_square", [P, 16, P], at=4096)
    gates_in = put("f", "gates_in", [P, 2, 3, 2, W], at=0)
    br_tmp = put("f", "br_tmp", [P, 2, W], at=24576)
    br_stage = put("f", "br_stage", [P, 2, 2, W], at=45056)
    mid = put("f", "mid", [P, 2, D], at=0)
    y = put("f", "y", [P, 2, D], at=16384)
    gain_row = put("f", "gain_row", [P, D], at=32768)
    up_stage = put("f", "up_stage", [P, 2, 2, W], at=40960)

    ps = ctx.enter_context(nc.psum_tensor("ps", [P, 8, 512], F32))
    T_BANK = 6

    w_in_v = w_in.rearrange("l (c p) n -> p (l c) n", p=P)
    w_out_v = w_out.rearrange("l (c p) n -> p (l c) n", p=P)
    w_up_v = w_up.rearrange("l (c p) n -> p (l c) n", p=P)
    w_down_v = w_down.rearrange("l (c p) n -> p (l c) n", p=P)
    w_br_v = [w.rearrange("l (c p) n -> p (l c) n", p=P) for w in (w_branch_a, w_branch_b, w_branch_c)]
    BR_UNITS = [2, 4, 4]
    BR_KC = [0, 4, 12]

    def attn(kind, i, j):
        if kind == "a":
            return i * 4 + j // 2, i * 4 + j // 2, i * 8 + j
        if kind == "b":
            key = i // 2 + 2 * ((j // 2) % 2)
            return i * 2 + j // 4, key, i * 4 + (24 + 2 * (j // 4) + j % 2)
        return i * 4 + j // 2, i * 4 + j // 2, i * 4 + (40 + j // 2)

    FIRST_IT = {"a": 0, "c": 3, "b": 5}
    LOOPS = [("a", 3), ("c", 2), ("b", 4)]

    def bank_of(kind, j):
        n = j // 2 if kind == "c" else j // 4
        return n, 6 + n % 2

    def banks_before(kind):
        return {"a": 0, "c": 6, "b": 14}[kind], 4 if kind == "c" else 2

    def bank_last(kind):
        return [1, 3, 5, 7] if kind == "c" else [3, 7]

    block = ctx.enter_context(nc.Block())

    @block.sync
    def _(sp):
        def load(u, slot, view, kc, col, cols=W):
            wait(sp, sem("lo_ready"), u.count(1 - RING))
            sp.dma_start(raw[:, slot, :, 0:cols], view[:, kc:kc + UR, bass.ds(col, cols)]).then_inc(
                sem(f"raw_loaded{slot}"), 16)

        def chunk(u, view, kc, n, col, cols=W, s0=0):
            for j in range(n):
                load(u + j, (s0 + j) % RING, view, kc + UR * j, col, cols)

        for t in range(2):
            sp.dma_start(x_in[:, t, :], x[0, t * P:(t + 1) * P, :]).then_inc(sem(f"x_loaded{t}"), 16)

        def qk_a(i):
            chunk(Pos(U0["qk_a"], 2 * CH, i), w_in_v, 0, CH, i * W + A_Q)
            chunk(Pos(U0["qk_a"] + CH, 2 * CH, i), w_in_v, 0, CH, i * W + A_K)

        qk_a(0)
        with sp.Fori(1, 3) as i:
            qk_a(i)
        with sp.Fori(0, 3) as i:
            chunk(Pos(U0["v_a"], CH, i), w_in_v, 0, CH, i * W + A_V)
        for c in range(2):
            chunk(Pos(U0["q_b"] + CH * c), w_in_v, 0, CH, B_Q + W * c)
        chunk(Pos(U0["kv_b"]), w_in_v, 0, CH, B_KV)
        chunk(Pos(U0["kv_b"] + CH), w_in_v, 0, CH, B_KV + W, B_LAST)
        with sp.Fori(0, 2) as i:
            chunk(Pos(U0["qk_c"], 2 * CH, i), w_in_v, 0, CH, i * W + C_Q)
            chunk(Pos(U0["qk_c"] + CH, 2 * CH, i), w_in_v, 0, CH, i * W + C_K)
        with sp.Fori(0, 2) as i:
            chunk(Pos(U0["v_c"], CH, i), w_in_v, 0, CH, i * W + C_V)

        def store_gates(c):
            sp.wait_ge(sem("gates_made"), c + 1)
            sp.dma_start(gate_dram[:, bass.ds(c, 1), :].rearrange("p a n -> p (a n)"),
                         stage[:, 0, :, :].rearrange("p t n -> p (t n)")).then_inc(sem("gates_stored"), 16)

        for c in range(2):
            chunk(Pos(U0["gate"] + CH * c), w_in_v, 0, CH, M_G + W * c)
        with sp.Fori(2, 12) as i:
            chunk(Pos(U0["gate"], CH, i), w_in_v, 0, CH // 2, i * W + M_G)
            store_gates(i - 2)
            chunk(Pos(U0["gate"] + CH // 2, CH, i), w_in_v, KC // 2, CH // 2, i * W + M_G)

        def load_gates(n):
            sp.wait_ge(sem("gates_stored"), 16 * (n + 9))
            wait(sp, sem("merge_done"), n - 1)
            sp.dma_start(gates_in[:, n % 2, :, :, :].rearrange("p b t n -> p b (t n)"),
                         gate_dram[:, n:n + 9:4, :]).then_inc(sem(f"gates_loaded{n % 2}"), 16)

        for n in range(4):
            for b in range(3):
                before = sum(BR_UNITS[:b])
                if n == 0 and b == 1:
                    sp.wait_ge(sem("o_split_lo"), 10)
                    load_gates(0)
                chunk(Pos(U0["branch"] + 10 * n + before), w_br_v[b], 0, BR_UNITS[b], W * n,
                      s0=(10 * n + before) % RING)
                if (n, b) in ((0, 1), (1, 0)):
                    store_gates(10 + n)
                if b == 1 and n < 3:
                    load_gates(n + 1)
        with sp.Fori(0, 4) as i:
            chunk(Pos(U0["out"], CH, i), w_out_v, 0, CH, i * W)

        def up(h, i):
            for c in range(2):
                chunk(Pos(U0[f"up{h}"] + CH * c, 2 * CH, i), w_up_v, 0, CH, i * (2 * W) + (h * DFF // 2 + W * c))

        def down(h, i):
            chunk(Pos(U0[f"down{h}"], 16, i), w_down_v, 32 * h, 16, i * W)

        for h in range(2):
            with sp.Fori(0, 4) as i:
                up(h, i)
            with sp.Fori(0, 4) as i:
                down(h, i)

    @block.gpsimd
    def _(pool):
        pool_count = pool.alloc_register("pool_count")

        def load(dst, src, name="const_loaded"):
            pool.dma_start(dst, src).then_inc(sem(name), 16)

        load(ident[:, :], identity)
        load(rows64[0:16, :], norm_mix_pre.rearrange("l (c p) -> (l c) p", p=P))
        load(rows64[16:32, :], norm_mlp_pre.rearrange("l (c p) -> (l c) p", p=P))
        load(rows64[32:48, :], cmp_k_pos.rearrange("l (c a) d -> (l c) (a d)", a=2))
        load(rows64[48:64, :], cmp_v_pos.rearrange("l (c a) d -> (l c) (a d)", a=2))
        load(onehot[:, :], bucket_onehot)
        load(dmask[:, :], distance_mask)
        load(rel[:, :], rel_bias)
        load(bmask[:, :, :], block_mask)
        load(lam_rows[:, :, :], bass.AP(diff_lambda.tensor, 0, [[0, P], [HD, 4], [1, HD]]))
        load(sub_gain[:, :], bass.AP(diff_norm.tensor, 0, [[0, P], [1, P]]))
        pool.wait_ge(sem("table_ready"), 1)
        pool.dma_start(bias_table, table[:, :]).then_inc(sem("table_stored"), 16)
        pool.memset(q_pad[:, :, :], 0.0).then_inc(sem("pad_zero"), 1)

        def queries_and_bias(kind, i):
            src = {"a": q_a, "b": q_b, "c": q_c}[kind]
            m0 = Pos(8 * FIRST_IT[kind], 8, i)
            for j in range(8):
                tile, _, row = attn(kind, i, j)
                half = slice(64 * (j % 2), 64 * (j % 2) + 64)
                behind = held(pool, pool_count, (m0 + j).count(-3))
                pool.wait_ge(sem("pad_zero"), 1)
                wait(pool, sem("scores_ready"), behind)
                pool.tensor_copy(q_pad[half, j % 4, :], src[half, bass.ds(tile, 1), :].rearrange("p a n -> p (a n)")
                                 ).then_inc(sem("query_ready"), 1)
                pool.wait_ge(sem("table_stored"), 16)
                wait(pool, sem("logits_ready"), behind)
                pool.dma_start(bias[:, j % 4, :], hankel[bass.ds(row, 1)].rearrange("a p n -> (a p) n")).then_inc(
                    sem(f"bias_loaded{j % 4}"), 16)

        def cmp_weights(i):
            for dst, src in ((w1k, cmp_k_w1), (w1v, cmp_v_w1)):
                pool.dma_start(dst[:, bass.ds(i * 4, 4), :], src.rearrange("l (c p) n -> p (l c) n", p=P)[
                    :, bass.ds(i * 4, 4), :]).then_inc(sem("w1_loaded"), 16)

        for name, n in (("tevac_v", T0["gate"]), ("tevac_s", T0["gate"])):
            pool.wait_ge(sem(name), n)
        for kind, n in LOOPS:
            queries_and_bias(kind, 0)
            if kind == "b":
                pool.wait_ge(sem("pv_done"), 8 * FIRST_IT["b"])
                cmp_weights(0)
            with pool.Fori(1, n) as i:
                queries_and_bias(kind, i)
                if kind == "b":
                    cmp_weights(i)
        pool.wait_ge(sem("pv_done"), 72)
        w2_k = cmp_k_w2.rearrange("l (c p) n -> p (l c) n", p=P)
        for a in range(2):
            pool.dma_start(w2k[:, :, a, :], w2_k).then_inc(sem("w2_loaded"), 16)
        pool.dma_start(w2v[:, :, :], cmp_v_w2.rearrange("l (c p) n -> p (l c) n", p=P)).then_inc(sem("w2_loaded"), 16)
        pool.memset(hid_v[:, :, :, :, :], 0.0).then_inc(sem("cmp_zero"), 1)
        pool.memset(vc_diag[:, :, :, :], 0.0).then_inc(sem("cmp_zero"), 1)
        pool.memset(cmp_p[:, :, :, :], 0.0).then_inc(sem("cmp_zero"), 1)
        pool.wait_ge(sem("merge_done"), 4)
        for t in range(2):
            pool.dma_start(mid[:, t, :], x[0, t * P:(t + 1) * P, :]).then_inc(sem("x_again"), 16)
        pool.wait_ge(sem("tevac_v"), T0["out"])
        pool.dma_start(gain_row[:, :], bass.AP(norm_mix_post.tensor, 0, [[0, P], [1, D]])).then_inc(sem("gain_loaded"), 16)
        pool.wait_ge(sem("mid_ready"), 2)
        pool.dma_start(gain_row[:, :], bass.AP(norm_mlp_post.tensor, 0, [[0, P], [1, D]])).then_inc(sem("gain_loaded"), 16)
        for t in range(2):
            pool.wait_ge(sem("result_ready"), t + 1)
            pool.dma_start(out[0, t * P:(t + 1) * P, :], mid[:, t, :]).then_inc(sem("stored"), 16)
        pool.wait_ge(sem("stored"), 32)

    @block.tensor
    def _(pe):
        def unit(u, slot, hi, lo, kc, pair, cols=W, first=False, last=False, free=None):
            pe.wait_ge(sem("lo_ready"), u.count(1))
            for t in range(2):
                if free is not None:
                    for name, value in free[t]:
                        wait(pe, sem(name), value)
                acc = ps[:, 2 * pair + t, 0:cols]
                for k in range(UR):
                    tok = slice(t * P, (t + 1) * P)
                    a, b = first and k == 0, last and k == UR - 1
                    pe.matmul(acc, hi[:, kc + k, tok], w_hi[:, slot, k, 0:cols], start=a, stop=False)
                    pe.matmul(acc, hi[:, kc + k, tok], w_lo[:, slot, k, 0:cols], start=False, stop=False)
                    mm = pe.matmul(acc, lo[:, kc + k, tok], w_hi[:, slot, k, 0:cols], start=False, stop=b)
                if last and t == 0:
                    mm.then_inc(sem("half_done"), 1)
            mm.then_inc(sem("unit_used"), 1)

        def chunk(u, n, hi, lo, kc, pair, cols=W, s0=0, between=(), free=None, before_last=None):
            for j in range(n):
                if before_last and j == n - 2:
                    before_last()
                unit(u + j, (s0 + j) % RING, hi, lo, kc + UR * j, pair, cols, j == 0, j == n - 1,
                     free if j == 0 else None)
                if j == 1:
                    for f in between:
                        f()

        def transposed(t, source, ready):
            for name, value in ready:
                wait(pe, sem(name), value)
            wait(pe, sem("tevac_v"), t.count())
            wait(pe, sem("tevac_s"), t.count())
            for q in range(4):
                for h in range(2):
                    tr = pe.transpose(ps[:, T_BANK + q // 2, 256 * (q % 2) + P * h:256 * (q % 2) + P * h + P],
                                      source(q, h), ident[:, :])
            tr.then_inc(sem("transposed"), 1)

        def norm_transposes(k, src):
            pe.wait_ge(sem(f"normed_v{k}"), 1)
            pe.wait_ge(sem(f"normed_s{k}"), 1)
            for g in range(8):
                wait(pe, sem(f"norm_lo{k}"), 2 * (g - 5))
                for c in range(2):
                    for t in range(2):
                        kc = 2 * g + c
                        tr = pe.transpose(ps[:, g % 6, 256 * c + P * t:256 * c + P * t + P],
                                          src[:, t, kc * P:(kc + 1) * P], ident[:, :])
                tr.then_inc(sem(f"norm_t{k}"), 1)
            pe.wait_ge(sem(f"norm_lo{k}"), 16)

        pe.wait_ge(sem("const_loaded"), 16 * 11)
        pe.transpose(ps[:, 7, 0:64], rows64[:, :], ident[0:64, 0:64]).then_inc(sem("columns_t"), 1)
        pe.matmul(ps[0:48, 6, :], rel[:, :], onehot[:, :], start=True, stop=True).then_inc(sem("table_mm"), 1)
        norm_transposes(0, x_normed)

        def stage_tiles(slot):
            return lambda q, h: stage[:, slot, h, q * P:(q + 1) * P]

        def pair_free(name, n, i=0):
            per = 2 if name.startswith("qk") else 1
            return [[("evac_v", Pos(V0[name] + n, per, i).count())], [("evac_s", Pos(S0[name] + n, per, i).count())]]

        def tiles_out(t, slot, name, n, per=0, i=0):
            e, es = Pos(V0[name] + n, per, i), Pos(S0[name] + n, per, i)
            return lambda: transposed(t, stage_tiles(slot), [("evac_v", e.count()), ("evac_s", es.count())])

        def qk(name, i, between):
            chunk(Pos(U0[name], 2 * CH, i), CH, h_hi, h_lo, 0, 0, between=between, free=pair_free(name, -1, i))
            chunk(Pos(U0[name] + CH, 2 * CH, i), CH, h_hi, h_lo, 0, 1, free=pair_free(name, 0, i),
                  between=[tiles_out(Pos(T0[name], 2, i), 0, name, 1, 2, i)])

        def values(name, i, between=()):
            chunk(Pos(U0[name], CH, i), CH, h_hi, h_lo, 0, 0, between=between, free=pair_free(name, 0, i))

        def dup_tiles(first):
            return lambda q, h: dup[:, h, first + q, :, :].rearrange("p a n -> p (a n)")

        qk("qk_a", 0, ())
        with pe.Fori(1, 3) as i:
            qk("qk_a", i, [tiles_out(Pos(T0["qk_a"] - 1, 2, i), 1, "qk_a", 0, 2, i)])
        values("v_a", 0, [tiles_out(Pos(T0["v_a"] - 1), 1, "v_a", 0)])
        with pe.Fori(1, 3) as i:
            values("v_a", i)
        chunk(Pos(U0["q_b"]), CH, h_hi, h_lo, 0, 0, free=pair_free("q_b", 0))
        chunk(Pos(U0["q_b"] + CH), CH, h_hi, h_lo, 0, 1, free=pair_free("q_b", 0),
              between=[tiles_out(Pos(T0["q_b"]), 0, "q_b", 1)])
        chunk(Pos(U0["kv_b"]), CH, h_hi, h_lo, 0, 0, free=pair_free("kv_b", 0),
              between=[tiles_out(Pos(T0["q_b"] + 1), 1, "q_b", 2)])
        chunk(Pos(U0["kv_b"] + CH), CH, h_hi, h_lo, 0, 1, B_LAST, free=pair_free("kv_b", 0),
              between=[lambda: transposed(Pos(T0["kv_b"]), dup_tiles(0), [("dup_ready", 1)])])
        qk("qk_c", 0, [lambda: transposed(Pos(T0["kv_b"] + 1), dup_tiles(4), [("dup_ready", 2)])])
        qk("qk_c", 1, [tiles_out(Pos(T0["qk_c"] + 1), 1, "qk_c", 2)])
        values("v_c", 0, [tiles_out(Pos(T0["v_c"] - 1), 1, "v_c", 0)])
        values("v_c", 1)
        pe.wait_ge(sem("tevac_v"), T0["gate"])
        pe.wait_ge(sem("tevac_s"), T0["gate"])

        def maps(kind, i):
            it = FIRST_IT[kind]
            m0 = Pos(8 * it, 8, i)
            keys = {"a": k_a, "b": k_b, "c": k_c}[kind]
            ob0, ob_n = banks_before(kind)

            def scores(j):
                _, tile, _ = attn(kind, i, j)
                wait(pe, sem("query_ready"), (m0 + j).count(1))
                wait(pe, sem("logits_ready"), (m0 + j).count(-1))
                key = keys[:, bass.ds(tile, 1), :].rearrange("p a n -> p (a n)")
                pe.matmul(ps[:, 2 + j % 2, 0:P], q_pad[:, j % 4, 0:P], key[:, 0:P], start=True, stop=True)
                pe.matmul(ps[:, 2 + j % 2, P:3 * P], q_pad[:, j % 4, P:2 * P], key, start=True,
                          stop=True).then_inc(sem("scores_ready"), 1)

            def transposes(j):
                half = Pos(4 * it, 4, i) + j // 2
                wait(pe, sem("probs_ready"), (m0 + j).count(1))
                wait(pe, sem(f"pt_copied{j % 2}"), half.count())
                for b in range(3):
                    tr = pe.transpose(ps[:, 4 + j % 2, b * P:(b + 1) * P], logits[:, j % 4, b * P:(b + 1) * P],
                                      ident[:, :])
                tr.then_inc(sem("pt_ready"), 1)

            def outputs(j):
                half = Pos(4 * it, 4, i) + j // 2
                n, bank = bank_of(kind, j)
                wait(pe, sem(f"pt_copied{j % 2}"), half.count(1))
                if j == 0 or bank_of(kind, j - 1)[0] != n:
                    wait(pe, sem("o_taken"), (Pos(ob0, ob_n, i) + n).count(-1))
                if kind == "a":
                    at = j % 4
                    val = [v_a[:, s, bass.ds(i * 512 + 64 * j, 64)] for s in range(2)]
                elif kind == "b":
                    at = j % 4
                    val = [v_b[:, s, (j // 2) % 2, bass.ds((i // 2) * 64, 64)] for s in range(2)]
                else:
                    at = j % 2
                    val = [v_c[:, s, bass.ds(i * 512 + 128 * (j // 2), 128)] for s in range(2)]
                n_out = 128 if kind == "c" else 64
                o = [ps[:, bank, 256 * t + n_out * at:256 * t + n_out * at + n_out] for t in range(2)]
                pe.matmul(o[0], p_t[:, j % 2, 0:P], val[0], start=True, stop=True)
                pe.matmul(o[1], p_t[:, j % 2, P:2 * P], val[0], start=True, stop=False)
                pe.matmul(o[1], p_t[:, j % 2, 2 * P:3 * P], val[1], start=False, stop=True).then_inc(
                    sem("pv_done"), 1)

            u = Pos(U0["gate"] + CH * it, CH, i)
            for s in range(CH):
                unit(u + s, s % RING, h_hi, h_lo, UR * s, 0, W, s == 0, s == CH - 1,
                     gates_free(Pos(it, 1, i)) if s == 0 else None)
                for j in range(8):
                    if SCORES_AT[j] + 1 == s:
                        transposes(j)
                for j in range(8):
                    if SCORES_AT[j] + 2 == s:
                        outputs(j)
                for j in range(8):
                    if SCORES_AT[j] == s:
                        scores(j)

        def gates_free(c):
            first = isinstance(c.count(), int) and c.count() == 0
            e = Pos(S0["gate"] + 2 * c.k, 2 * c.per, c.i)
            return [[("evac_v", V0["gate"])] if first else [("evac_s", e.count(-1))], [("evac_s", e.count())]]

        for kind, n in LOOPS:
            maps(kind, 0)
            with pe.Fori(1, n) as i:
                maps(kind, i)

        def compress_first(v):
            w1 = (w1k, w1v)[v]
            for hc in range(2):
                for c in range(KC):
                    mm = pe.matmul(ps[:, 2, 30 * (2 * v + hc):30 * (2 * v + hc) + 30],
                                   w1[:, c, hc * P:(hc + 1) * P], blocks_t[:, v, c, :], start=c == 0,
                                   stop=c == KC - 1)
            return mm

        def compress_k():
            pe.wait_ge(sem("w1_loaded"), 2 * 4 * 16)
            pe.wait_ge(sem("blocks_ready"), 8)
            compress_first(0)

        def compress_v():
            compress_first(1).then_inc(sem("hidden_mm"), 1)

        def compress2():
            pe.wait_ge(sem("w2_loaded"), 48)
            pe.wait_ge(sem("gelu_ready"), 3)
            for hc in range(2):
                pe.matmul(ps[:, 3, 0:30], w2k[:, hc, :, :].rearrange("p a n -> p (a n)"), hid_k[:, hc, :],
                          start=hc == 0, stop=hc == 1)
            for g in range(2):
                for hc in range(2):
                    mm = pe.matmul(ps[:, 3, 64 + 64 * g:128 + 64 * g],
                                   hid_v[:, hc, g, :, :].rearrange("p a n -> p (a n)"), w2v[:, hc, :],
                                   start=hc == 0, stop=hc == 1)
            mm.then_inc(sem("compressed_mm"), 1)

        def cmp_scores():
            pe.wait_ge(sem("compressed"), 1)
            pe.wait_ge(sem("o_split_lo"), 6)
            for t in range(2):
                for h in range(16):
                    half = slice(64 * (h % 2), 64 * (h % 2) + 64)
                    at = 16 * (h // 2)
                    mm = pe.matmul(ps[:, 4 + 2 * (h % 2) + t, at:at + NCMP], q_b[half, h // 2, t * P:(t + 1) * P],
                                   kc_t[half, NCMP * (h // 8):NCMP * (h // 8) + NCMP], start=True, stop=True)
            mm.then_inc(sem("cmp_scores"), 1)

        def cmp_transposes():
            pe.wait_ge(sem("cmp_probs"), 1)
            for n in range(8):
                t, q = n // 4, n % 4
                tr = pe.transpose(ps[:, 6 + n // 4, P * (n % 4):P * (n % 4) + P],
                                  cmp_p[:, t, 4 * q:4 * q + 4, :].rearrange("p a n -> p (a n)"), ident[:, :])
            tr.then_inc(sem("cmp_pt"), 1)

        def cmp_outputs():
            pe.wait_ge(sem("cmp_pt_copied"), 1)
            for n in range(8):
                t, q = n // 4, n % 4
                mm = pe.matmul(ps[:, 2 + 2 * t + q // 2, 256 * (q % 2):256 * (q % 2) + 256], cmp_pt[:, n, :],
                               vc_diag[:, q // 2, :, :].rearrange("p a n -> p (a n)"), start=True, stop=True)
            mm.then_inc(sem("cmp_pv"), 1)

        def output_transposes(q):
            g, bank = O_PAIRS[q], O_BANKS[q]
            pe.wait_ge(sem("a_ready" if g < 2 else "b_ready" if g < 6 else "c_ready"), 1)
            before = [k for k in range(q) if O_BANKS[k] == bank]
            wait(pe, sem("o_split_lo"), before[-1] + 1 if before else 0)
            for c in range(2):
                b = 2 * g + c
                for t in range(2):
                    src = (o_a[:, 0, t, P * b:P * b + P] if b < 4 else
                           o_b[:, t, P * (b - 4):P * (b - 3)] if b < 12 else o_c[:, t, P * (b - 12):P * (b - 11)])
                    tr = pe.transpose(ps[:, bank, 256 * c + P * t:256 * c + P * t + P], src, ident[:, :])
            tr.then_inc(sem("o_transposed"), 1)

        pe_steps = {0: [compress_k], 1: [compress_v], 5: [compress2], 7: [cmp_scores], 11: [cmp_transposes],
                    13: [cmp_outputs]}
        for q, n in enumerate(O_AT):
            pe_steps.setdefault(n, []).append(lambda q=q: output_transposes(q))
        for n in range(NSTEP):
            c, s = divmod(n, CH)
            unit(Pos(U0["gate"] + 72 + n), s % RING, h_hi, h_lo, UR * s, 0, W, s == 0, s == CH - 1,
                 gates_free(Pos(9 + c)) if s == 0 else None)
            for f in pe_steps.get(n, ()):
                f()
        pe.wait_ge(sem("o_split_lo"), 10)
        pe.wait_ge(sem("evac_s"), S0["branch"])

        for n in range(4):
            for b in range(3):
                before = sum(BR_UNITS[:b])
                t = Pos(T0["branch"] + n - 1)
                between = [] if (n == 0 or b != 1) else [
                    lambda t=t, n=n: transposed(t, lambda q, h: br_stage[:, (n - 1) % 2, h, q * P:(q + 1) * P],
                                                [("merge_done", n)])]
                chunk(Pos(U0["branch"] + 10 * n + before), BR_UNITS[b], o_hi, o_lo, BR_KC[b], b,
                      s0=(10 * n + before) % RING, between=between,
                      free=[[("evac_v", V0["branch"] + 2 * (3 * n + b - 3) + 1 + h if n else 0)] for h in range(2)])
        transposed(Pos(T0["branch"] + 3), lambda q, h: br_stage[:, 1, h, q * P:(q + 1) * P], [("merge_done", 4)])
        pe.wait_ge(sem("tevac_v"), T0["out"])

        def plain(name, i, n, hi, lo, between=(), before_last=None):
            if name == "down1":
                free = [[("evac_v", Pos(V0[name], 2, i).count(-1))], [("evac_v", Pos(V0[name], 2, i).count())]]
                if isinstance(i, int):
                    free = [[("evac_s", S0[name] - 1), ("evac_v", V0[name])], [("evac_s", S0[name])]]
            elif name == "down0" and isinstance(i, int):
                free = [[("evac_s", S0[name] - 1), ("evac_v", V0[name])], [("evac_s", S0[name])]]
            else:
                free = [[("evac_v", Pos(V0[name], 1, i).count())], [("evac_s", Pos(S0[name], 1, i).count())]]
            chunk(Pos(U0[name], n, i), n, hi, lo, 0, 0, free=free, between=between, before_last=before_last)

        with pe.Fori(0, 4) as i:
            plain("out", i, CH, h_hi, h_lo)
        pe.wait_ge(sem("evac_v"), V0["up0"])
        pe.wait_ge(sem("evac_s"), S0["up0"])
        norm_transposes(2, mid_normed)

        def up_tiles(name, c, i):
            e = Pos(V0[name] + c + 1, 2, i)
            return lambda: transposed(Pos(T0[name] + c, 2, i), lambda q, h: up_stage[:, c % 2, h, q * P:(q + 1) * P],
                                      [("evac_v", e.count())])

        def up(name, i, between):
            for c in range(2):
                e = Pos(S0[name] + 2 * (c - 2), 4, i)
                free = [[("evac_s", e.count(1 + h))] for h in range(2)]
                if isinstance(i, int):
                    free = [[("evac_v", V0[name]), ("evac_s", S0[name])], []]
                chunk(Pos(U0[name] + CH * c, 2 * CH, i), CH, h_hi, h_lo, 0, c, free=free,
                      between=between if c == 0 else [up_tiles(name, 0, i)])

        for h in range(2):
            up(f"up{h}", 0, ())
            with pe.Fori(1, 4) as i:
                up(f"up{h}", i, [up_tiles(f"up{h}", -1, i)])
            plain(f"down{h}", 0, 16, u_hi, u_lo, [up_tiles(f"up{h}", -1, 4)],
                  before_last=lambda h=h: pe.wait_ge(sem("tevac_v"), T0[f"down{h}"]))
            with pe.Fori(1, 4) as i:
                plain(f"down{h}", i, 16, u_hi, u_lo)
        pe.wait_ge(sem("unit_used"), UNITS)

    @block.scalar
    def _(act):
        act_count = act.alloc_register("act_count")

        def split(u, slot):
            if isinstance(u.count(), int) and u.count() >= UNITS:
                return
            act.wait_ge(sem(f"raw_loaded{slot}"), u.loads())
            wait(act, sem("unit_used"), u.count(1 - RING))
            act.activation(w_hi[:, slot, :, :], raw[:, slot, :, :], ACT.Copy).then_inc(sem("hi_ready"), 1)

        def chunk(u, n, s0=0, after=None):
            for j in range(n):
                split(u + (j + LEAD), (s0 + j + LEAD) % RING)
                for f in (after or {}).get(j, ()):
                    f()

        def copy_out(dst, pair, e, scale=1.0):
            u_done, count = e
            act.wait_ge(sem("unit_used"), u_done)
            act.activation(dst, ps[:, 2 * pair + 1, 0:dst.shape[-1]], ACT.Copy, scale=scale).then_inc(sem("evac_s"), 1)

        def t_out(t, dst):
            act.wait_ge(sem("transposed"), t.count(1))
            act.activation(dst, ps[:, T_BANK + 1, :].rearrange("p (a n) -> p a n", a=2), ACT.Copy).then_inc(
                sem("tevac_s"), 1)

        def t_split(t, dst):
            act.wait_ge(sem("transposed"), t.count(1))
            act.activation(dst, ps[:, T_BANK:T_BANK + 2, :].rearrange("p b (a n) -> p (b a) n", a=2), ACT.Copy
                           ).then_inc(sem("tevac_s"), 1)

        def norm_stats(k, src):
            if k >= 2:
                act.wait_ge(sem(f"ssq_s{k - 1}"), 1)
            act.activation(square_out[:, 1, :] if k else x_normed[:, 1, :], src[:, 1, :], ACT.Square,
                           accum_out=ssq[:, k, 1:2]).then_inc(sem(f"ssq_s{k}"), 1)
            act.wait_ge(sem(f"rstd_steps{k}"), 1)
            act.activation(root[:, k, :], mean[:, k, :], ACT.Sqrt).then_inc(sem(f"root{k}"), 1)

        def norm_split(k, src, dst):
            act.wait_ge(sem(f"rstd_steps{k}"), 6)
            act.activation(dst[:, 1, :], src[:, 1, :], ACT.Copy, scale=rstd[:, k, 1:2]).then_inc(sem(f"normed_s{k}"), 1)
            for g in range(8):
                act.wait_ge(sem(f"norm_t{k}"), g + 1)
                for c in range(2):
                    kc = 2 * g + c
                    act.activation(h_hi[:, kc, :], ps[:, g % 6, 256 * c:256 * c + 256], ACT.Copy,
                                   scale=columns[:, 8 * k + kc:8 * k + kc + 1]).then_inc(sem(f"norm_hi{k}"), 1)

        act.wait_ge(sem("x_loaded1"), 16)
        norm_stats(0, x_in)
        act.wait_ge(sem("columns_ready"), 1)
        norm_split(0, x_in, x_normed)
        act.wait_ge(sem("lam_steps"), 2)
        act.activation(lam2[:, 2:4], lam2[:, 0:2], ACT.Exp).then_inc(sem("lam_exp"), 1)
        for j in range(LEAD):
            split(Pos(j), j)

        def tiles(t, dst, first):
            return {2: [lambda: t_out(t, dst[:, bass.ds(first + 2, 2), :])]}

        def qk(name, i, q_dst, k_dst, after):
            u = Pos(U0[name], 2 * CH, i)
            chunk(u, CH, after=after)
            copy_out(stage[:, 0, 1, :], 0, (u.count(CH), 1), SCALE)
            chunk(u + CH, CH, after=tiles(Pos(T0[name], 2, i), q_dst, i * 4))
            copy_out(stage[:, 1, 1, :], 1, (u.count(2 * CH), 1))

        def values(name, i, dst, after=None):
            u = Pos(U0[name], CH, i)
            chunk(u, CH, after=after)
            copy_out(dst[:, 1, bass.ds(i * W, W)], 0, (u.count(CH), 1))

        qk("qk_a", 0, q_a, k_a, None)
        with act.Fori(1, 3) as i:
            qk("qk_a", i, q_a, k_a, tiles(Pos(T0["qk_a"] - 1, 2, i), k_a, i * 4 - 4))
        values("v_a", 0, v_a, tiles(Pos(T0["v_a"] - 1), k_a, 8))
        with act.Fori(1, 3) as i:
            values("v_a", i, v_a)
        u, t = Pos(U0["q_b"]), Pos(T0["q_b"])
        chunk(u, CH)
        copy_out(stage[:, 0, 1, :], 0, (u.count(CH), 1), SCALE)
        chunk(u + CH, CH, after=tiles(t, q_b, 0))
        copy_out(stage[:, 1, 1, :], 1, (u.count(2 * CH), 1), SCALE)
        u2, t2 = Pos(U0["kv_b"]), Pos(T0["kv_b"])
        chunk(u2, CH, after=tiles(t + 1, q_b, 4))
        copy_out(stage[:, 0, 1, :], 0, (u2.count(CH), 1))
        chunk(u2 + CH, CH, after=tiles(t2, cmp_t, 0))
        copy_out(stage[:, 1, 1, 0:B_LAST], 1, (u2.count(2 * CH), 1))
        act.wait_ge(sem("bgate_steps"), 1)
        act.activation(head_gates[:, :, :, :], head_gates[:, :, :, :], ACT.Exp, scale=-1.0).then_inc(sem("bgate_exp"), 1)
        qk("qk_c", 0, q_c, k_c, tiles(t2 + 1, k_b, 0))
        qk("qk_c", 1, q_c, k_c, tiles(Pos(T0["qk_c"] + 1), k_c, 0))
        values("v_c", 0, v_c, tiles(Pos(T0["v_c"] - 1), k_c, 4))
        values("v_c", 1, v_c)

        def gate_exp(c):
            stored = held(act, act_count, c * 16)
            act.wait_ge(sem("half_done"), Pos(C0["gate"] + 1, 1, c).count())
            wait(act, sem("gates_stored"), stored)
            act.activation(stage[:, 0, 0, :], ps[:, 0, :], ACT.Exp, scale=-1.0).then_inc(sem("evac_s"), 1)
            act.wait_ge(sem("unit_used"), Pos(U0["gate"] + CH, CH, c).count())
            act.activation(stage[:, 0, 1, :], ps[:, 1, :], ACT.Exp, scale=-1.0).then_inc(sem("evac_s"), 1)

        def maps(kind, i, extra=None):
            it = FIRST_IT[kind]
            m0 = Pos(8 * it, 8, i)
            u = Pos(U0["gate"] + CH * it, CH, i)

            def exps(j):
                wait(act, sem("logits_ready"), (m0 + j).count(1))
                if isinstance(i, int) and i == 0:
                    prev = {"a": None, "c": ("a", 2), "b": ("c", 1)}[kind]
                    if prev is not None:
                        n0, n1 = banks_before(prev[0])
                        wait(act, sem("o_taken"), n0 + n1 * prev[1] + bank_of(prev[0], j)[0] + 1)
                else:
                    n0, n1 = banks_before(kind)
                    wait(act, sem("o_taken"), (Pos(n0 - n1, n1, i) + (bank_of(kind, j)[0] + 1)).count())
                for t in range(2):
                    part = logits[:, j % 4, 0:P] if t == 0 else logits[:, j % 4, P:3 * P]
                    e = act.activation(part, part, ACT.Exp, bias=negmax[:, t, j:j + 1], scale=-1.0,
                                       accum_out=sums[:, t, j:j + 1])
                e.then_inc(sem("probs_ready"), 1)

            def pt_copy(j):
                half = Pos(4 * it, 4, i) + j // 2
                act.wait_ge(sem("pt_ready"), (m0 + j).count(1))
                wait(act, sem("pv_done"), (m0 + j).count(-1))
                act.activation(p_t[:, 1, :], ps[:, 5, 0:384], ACT.Copy).then_inc(sem("pt_copied1"), 1)

            for s in range(CH):
                split(u + (s + LEAD), (s + LEAD) % RING)
                for j in range(1, 8, 2):
                    if SCORES_AT[j] + 1 == s:
                        pt_copy(j)
                for j in range(8):
                    if SCORES_AT[j] == s:
                        exps(j)
                for f in (extra or {}).get(s, ()):
                    f()
            gate_exp(i + it)

        def gelu_exp():
            act.wait_ge(sem("gelu_steps"), 5)
            act.activation(hid[:, 2, :], hid[:, 1, :], ACT.Exp, scale=-2.0 * math.sqrt(2.0 / math.pi)).then_inc(
                sem("gelu_exp"), 1)

        def a_exp():
            act.wait_ge(sem("a_steps"), 2)
            act.activation(a_w[:, :, :], a_w[:, :, :], ACT.Exp, scale=-1.0).then_inc(sem("a_exp"), 1)

        def c_root_step():
            act.wait_ge(sem("c_steps"), 3)
            act.activation(c_root[:, :, :], c_mean[:, :, :], ACT.Sqrt).then_inc(sem("c_root"), 1)

        def cmp_exp():
            act.wait_ge(sem("cmp_steps"), 4)
            act.activation(cmp_l[:, :, :, :], cmp_l[:, :, :, :], ACT.Exp).then_inc(sem("cmp_exp"), 1)

        between_maps = {"c": {2: [a_exp]}, "b": {7: [c_root_step]}}
        for kind, n in LOOPS:
            maps(kind, 0, between_maps.get(kind))
            with act.Fori(1, n) as i:
                maps(kind, i)

        def o_split(q):
            g, bank = O_PAIRS[q], O_BANKS[q]
            act.wait_ge(sem("o_transposed"), q + 1)
            act.activation(o_hi[:, 2 * g:2 * g + 2, :], ps[:, bank, :].rearrange("p (a n) -> p a n", a=2),
                           ACT.Copy).then_inc(sem("o_split_hi"), 1)

        act_steps = {3: [gelu_exp], 9: [cmp_exp]}
        for q, n in enumerate(O_AT):
            act_steps.setdefault(n + 1, []).append(lambda q=q: o_split(q))
        for n in range(NSTEP):
            c, s = divmod(n, CH)
            split(Pos(U0["gate"] + 72 + n + LEAD), (s + LEAD) % RING)
            for f in act_steps.get(n, ()):
                f()
            if s == CH - 1:
                gate_exp(9 + c)

        for n in range(4):
            chunk(Pos(U0["branch"] + 10 * n), 10, s0=(10 * n) % RING, after={5: [] if n == 0 else [
                lambda n=n: t_split(Pos(T0["branch"] + n - 1), h_hi[:, 4 * (n - 1):4 * n, :])]})
        t_split(Pos(T0["branch"] + 3), h_hi[:, 12:16, :])

        with act.Fori(0, 4) as i:
            u = Pos(U0["out"], CH, i)
            chunk(u, CH)
            copy_out(y[:, 1, bass.ds(i * W, W)], 0, (u.count(CH), 1))
        act.wait_ge(sem("evac_s"), S0["up0"])
        norm_stats(1, y)
        act.wait_ge(sem("mid_ready"), 2)
        norm_stats(2, mid)
        norm_split(2, mid, mid_normed)

        def up(name, i, h):
            u, t = Pos(U0[name], 2 * CH, i), Pos(T0[name], 2, i)

            def relu(c):
                act.wait_ge(sem("half_done"), Pos(C0[name] + c + 1, 2, i).count())
                act.activation(up_stage[:, c, 0, :], ps[:, 2 * c, :], ACT.Relu).then_inc(sem("evac_s"), 1)
                act.wait_ge(sem("unit_used"), (u + CH * (c + 1)).count())
                act.activation(up_stage[:, c, 1, :], ps[:, 2 * c + 1, :], ACT.Relu).then_inc(sem("evac_s"), 1)

            chunk(u, CH, after={2: [lambda: t_split(t + (-1), u_hi[:, bass.ds(i * 8 - 4, 4), :])]}
                  if not isinstance(i, int) else None)
            relu(0)
            chunk(u + CH, CH, after={2: [lambda: t_split(t, u_hi[:, bass.ds(i * 8, 4), :])]})
            relu(1)

        def down(h, i):
            u = Pos(U0[f"down{h}"], 16, i)
            chunk(u, 16, after={2: [lambda: t_split(Pos(T0[f"down{h}"] - 1), u_hi[:, 28:32, :])]} 
                  if isinstance(i, int) and i == 0 else None)
            if h == 0:
                act.wait_ge(sem("unit_used"), u.count(16))
                act.activation(y[:, 1, bass.ds(i * W, W)], ps[:, 1, :], ACT.Copy).then_inc(sem("evac_s"), 1)

        for h in range(2):
            up(f"up{h}", 0, h)
            with act.Fori(1, 4) as i:
                up(f"up{h}", i, h)
            down(h, 0)
            with act.Fori(1, 4 - h) as i:
                down(h, i)
            if h == 1:
                down(h, 3)
        act.wait_ge(sem("evac_v"), V0["down1"] + 8)
        norm_stats(3, y)

    @block.vector
    def _(dve):
        dve_count = dve.alloc_register("dve_count")

        def split(u, slot):
            if isinstance(u.count(), int) and u.count() >= UNITS:
                return
            dve.wait_ge(sem("hi_ready"), u.count(1))
            wait(dve, sem("unit_used"), u.count(1 - RING))
            dve.tensor_tensor(w_lo[:, slot, :, :], raw[:, slot, :, :], w_hi[:, slot, :, :].bitcast(F32),
                              ALU.subtract).then_inc(sem("lo_ready"), 1)

        def chunk(u, n, s0=0, after=None):
            for j in range(n):
                split(u + (j + LEAD), (s0 + j + LEAD) % RING)
                for f in (after or {}).get(j, ()):
                    f()

        def copy_out(dst, pair, half_done, scale=None):
            dve.wait_ge(sem("half_done"), half_done)
            src = ps[:, 2 * pair, 0:dst.shape[-1]]
            if scale is None:
                dve.tensor_copy(dst, src).then_inc(sem("evac_v"), 1)
            else:
                dve.tensor_scalar(dst, src, scale, None, ALU.mult).then_inc(sem("evac_v"), 1)

        def t_out(t, dst):
            dve.wait_ge(sem("transposed"), t.count(1))
            dve.tensor_copy(dst, ps[:, T_BANK, :].rearrange("p (a n) -> p a n", a=2)).then_inc(sem("tevac_v"), 1)

        def t_split(t, dst, hi):
            dve.wait_ge(sem("tevac_s"), t.count(1))
            dve.tensor_tensor(dst, ps[:, T_BANK:T_BANK + 2, :].rearrange("p b (a n) -> p (b a) n", a=2),
                              hi.bitcast(F32), ALU.subtract).then_inc(sem("tevac_v"), 1)

        def chain(name, ops):
            s = sem(name)
            for op in ops:
                done[name] = done.get(name, 0) + 1
                op().then_inc(s, 1)
                dve.wait_ge(s, done[name])

        done = {}

        def norm_stats(k, src):
            name = f"rstd_steps{k}"
            dve.tensor_tensor_reduce(square_out[:, 0, :] if k else x_normed[:, 0, :], src[:, 0, :], src[:, 0, :], 1.0,
                                     0.0, ALU.mult, ALU.add, ssq[:, k, 0:1]).then_inc(sem(f"ssq_v{k}"), 1)
            dve.wait_ge(sem(f"ssq_v{k}"), 1)
            dve.wait_ge(sem(f"ssq_s{k}"), 1)
            chain(name, [lambda: dve.tensor_scalar(mean[:, k, :], ssq[:, k, :], 1.0 / D, EPS, ALU.mult, ALU.add)])
            dve.wait_ge(sem(f"root{k}"), 1)
            a, b, c, n = inv[:, k, :], newton[:, k, :], rstd[:, k, :], mean[:, k, :]
            chain(name, [
                lambda: dve.reciprocal(a, root[:, k, :]),
                lambda: dve.tensor_tensor(b, a, a, ALU.mult),
                lambda: dve.tensor_tensor(b, b, n, ALU.mult),
                lambda: dve.tensor_scalar(b, b, -0.5, 1.5, ALU.mult, ALU.add),
                lambda: dve.tensor_tensor(c, a, b, ALU.mult)])

        def norm_split(k, src, dst):
            dve.tensor_scalar(dst[:, 0, :], src[:, 0, :], rstd[:, k, 0:1], None, ALU.mult).then_inc(
                sem(f"normed_v{k}"), 1)
            for g in range(8):
                dve.wait_ge(sem(f"norm_hi{k}"), 2 * g + 2)
                for c in range(2):
                    kc = 2 * g + c
                    dve.scalar_tensor_tensor(h_lo[:, kc, :], ps[:, g % 6, 256 * c:256 * c + 256],
                                             columns[:, 8 * k + kc:8 * k + kc + 1], h_hi[:, kc, :].bitcast(F32),
                                             ALU.mult, ALU.subtract).then_inc(sem(f"norm_lo{k}"), 1)

        dve.wait_ge(sem("columns_t"), 1)
        dve.tensor_copy(columns[:, :], ps[:, 7, 0:64]).then_inc(sem("columns_ready"), 1)
        dve.wait_ge(sem("table_mm"), 1)
        dve.tensor_tensor(table[:, :], ps[0:48, 6, :], dmask[:, :], ALU.add).then_inc(sem("table_ready"), 1)
        for n in range(2):
            dve.tensor_tensor_reduce(lam_prod[:, n, :], lam_rows[:, 2 * n, :], lam_rows[:, 2 * n + 1, :], 1.0, 0.0,
                                     ALU.mult, ALU.add, lam2[:, n:n + 1]).then_inc(sem("lam_steps"), 1)
        dve.wait_ge(sem("x_loaded0"), 16)
        norm_stats(0, x_in)
        dve.wait_ge(sem("columns_ready"), 1)
        norm_split(0, x_in, x_normed)
        dve.wait_ge(sem("lam_exp"), 1)
        dve.scalar_tensor_tensor(neg_lam[:, :], lam2[:, 3:4], -LAM_INIT, lam2[:, 2:3], ALU.add, ALU.subtract).then_inc(
            sem("neg_lam"), 1)
        for j in range(LEAD):
            split(Pos(j), j)

        def tiles(t, dst, first):
            return {2: [lambda: t_out(t, dst[:, bass.ds(first, 2), :])]}

        def qk(name, i, q_dst, k_dst, after):
            u = Pos(U0[name], 2 * CH, i)
            c = Pos(C0[name], 2, i)
            chunk(u, CH, after=after)
            copy_out(stage[:, 0, 0, :], 0, c.count(1), SCALE)
            chunk(u + CH, CH, after=tiles(Pos(T0[name], 2, i), q_dst, i * 4))
            copy_out(stage[:, 1, 0, :], 1, c.count(2))

        def values(name, i, dst, after=None):
            u = Pos(U0[name], CH, i)
            chunk(u, CH, after=after)
            copy_out(dst[:, 0, bass.ds(i * W, W)], 0, Pos(C0[name], 1, i).count(1))

        qk("qk_a", 0, q_a, k_a, None)
        with dve.Fori(1, 3) as i:
            qk("qk_a", i, q_a, k_a, tiles(Pos(T0["qk_a"] - 1, 2, i), k_a, i * 4 - 4))
        values("v_a", 0, v_a, tiles(Pos(T0["v_a"] - 1), k_a, 8))
        with dve.Fori(1, 3) as i:
            values("v_a", i, v_a)
        u, t = Pos(U0["q_b"]), Pos(T0["q_b"])
        chunk(u, CH)
        copy_out(stage[:, 0, 0, :], 0, C0["q_b"] + 1, SCALE)
        chunk(u + CH, CH, after=tiles(t, q_b, 0))
        copy_out(stage[:, 1, 0, :], 1, C0["q_b"] + 2, SCALE)

        u2, t2 = Pos(U0["kv_b"]), Pos(T0["kv_b"])

        def double(slot, cols, first, wait_for=True):
            dve.wait_ge(sem("evac_v"), V0["kv_b"] + 1 + slot)
            dve.wait_ge(sem("evac_s"), S0["kv_b"] + 1 + slot)
            for h in range(2):
                for a in range(2):
                    last = dve.tensor_copy(dup[:, h, first:first + cols // HD, a, :],
                                           stage[:, slot, h, 0:cols].rearrange("p (q n) -> p q n", n=HD)
                                           if first != 4 else
                                           stage[:, slot, h, 256:256 + cols].rearrange("p (q n) -> p q n", n=HD))
            return last

        chunk(u2, CH, after=tiles(t + 1, q_b, 4))
        copy_out(stage[:, 0, 0, :], 0, C0["kv_b"] + 1)
        dve.wait_ge(sem("table_stored"), 16)
        double(0, 256, 0).then_inc(sem("dup_ready"), 1)
        double(0, 128, 4)
        dve.tensor_copy(v_b[:, :, 0, :], stage[:, 0, :, 384:512]).then_inc(sem("v_b_copied"), 1)
        chunk(u2 + CH, CH, after=tiles(t2, cmp_t, 0))
        copy_out(stage[:, 1, 0, 0:B_LAST], 1, C0["kv_b"] + 2)
        double(1, 128, 6).then_inc(sem("dup_ready"), 1)
        dve.tensor_copy(v_b[:, :, 1, :], stage[:, 1, :, 128:256]).then_inc(sem("v_b_copied"), 1)
        for h in range(2):
            last = dve.tensor_copy(head_gates[:, h, :, :], stage[:, 1, h, 256:304].rearrange("p (h b) -> p b h", b=3))
        last.then_inc(sem("bgate_steps"), 1)
        dve.wait_ge(sem("bgate_exp"), 1)
        done["bgate_steps"] = 1
        chain("bgate_steps", [
            lambda: dve.tensor_scalar(head_gates[:, :, :, :], head_gates[:, :, :, :], 1.0, None, ALU.add),
            lambda: dve.reciprocal(head_gates[:, :, :, :], head_gates[:, :, :, :])])
        qk("qk_c", 0, q_c, k_c, tiles(t2 + 1, k_b, 0))
        qk("qk_c", 1, q_c, k_c, tiles(Pos(T0["qk_c"] + 1), k_c, 0))
        values("v_c", 0, v_c, tiles(Pos(T0["v_c"] - 1), k_c, 4))
        values("v_c", 1, v_c)

        def gate_plus(c):
            dve.wait_ge(sem("evac_s"), Pos(S0["gate"] + 2, 2, c).count())
            dve.tensor_scalar(stage[:, 0, :, :], stage[:, 0, :, :], 1.0, None, ALU.add).then_inc(sem("gate_plus1"), 1)

        gates_flat = stage[:, 0, :, :].rearrange("p t n -> p (t n)")

        def gate_part(c, s):
            if s == 0:
                gate_plus(c)
            if s not in GATE_PARTS:
                return
            first, last = GATE_PARTS[s]
            if first == 0:
                dve.wait_ge(sem("gate_plus1"), Pos(1, 1, c).count())
            part = dve.reciprocal(gates_flat[:, first:last], gates_flat[:, first:last])
            if last == 2 * W:
                part.then_inc(sem("gates_made"), 1)

        def blocks():
            for v in range(2):
                for g in range(2):
                    for par in range(2):
                        half = slice(64 * par, 64 * par + 64)
                        t = cmp_t[half, 2 * v + g, :]
                        src = bass.AP(t.tensor, t.offset + par, [list(t.ap[0]), [2, KC], [CSTRIDE, NCMP]])
                        pos = columns[half, 32 + 16 * v:48 + 16 * v].rearrange("p (c a) -> p c a", a=1)
                        dve.tensor_tensor(blocks_t[half, v, :, NCMP * g:NCMP * g + NCMP], src,
                                          pos.to_broadcast([64, KC, NCMP]), ALU.add).then_inc(sem("blocks_ready"), 1)

        dve.wait_ge(sem("tevac_s"), T0["gate"])
        dve.wait_ge(sem("tevac_v"), T0["gate"])
        blocks()

        def maps(kind, i, extra=None):
            it = FIRST_IT[kind]
            m0 = Pos(8 * it, 8, i)
            u = Pos(U0["gate"] + CH * it, CH, i)
            ob0, ob_n = banks_before(kind)

            def add_bias(j):
                wait(dve, sem("scores_ready"), (m0 + j).count(1))
                loads = Pos(2 * it + j // 4 + 1, 2, i)
                dve.wait_ge(sem(f"bias_loaded{j % 4}"), Pos(16 * loads.k, 32, i).count())
                transposed_before = held(dve, dve_count, (m0 + j).count(-3))
                dve.wait_ge(sem("table_ready"), 1)
                wait(dve, sem("pt_ready"), transposed_before)
                dve.tensor_tensor_reduce(logits[:, j % 4, 0:P], ps[:, 2 + j % 2, 0:P], bias[:, j % 4, P - 1::-1], -1.0,
                                         3.0e38, ALU.add, ALU.min, negmax[:, 0, j:j + 1])
                dve.tensor_tensor_reduce(logits[:, j % 4, P:3 * P], ps[:, 2 + j % 2, P:3 * P], bias[:, j % 4, ::-1],
                                         -1.0, 3.0e38, ALU.add, ALU.min, negmax[:, 1, j:j + 1]).then_inc(
                    sem("logits_ready"), 1)

            def pt_copy(j):
                dve.wait_ge(sem("pt_ready"), (m0 + j).count(1))
                wait(dve, sem("pv_done"), (m0 + j).count(-1))
                dve.tensor_copy(p_t[:, 0, :], ps[:, 4, 0:384]).then_inc(sem("pt_copied0"), 1)

            def take(j):
                n, bank = bank_of(kind, j)
                dve.wait_ge(sem("pv_done"), (m0 + j).count(1))
                if kind == "a":
                    dve.tensor_copy(o_a[:, bass.ds(i, 1), :, 256 * n:256 * n + 256].rearrange("p a t n -> p (a t) n"),
                                    ps[:, bank, :].rearrange("p (t n) -> p t n", t=2))
                    dve.tensor_copy(a_negmax[:, :, bass.ds(i * 8 + 4 * n, 4)], negmax[:, :, 4 * n:4 * n + 4])
                    dve.tensor_copy(a_sums[:, :, bass.ds(i * 8 + 4 * n, 4)], sums[:, :, 4 * n:4 * n + 4]).then_inc(
                        sem("o_taken"), 1)
                    return
                steps = Pos(24, 6, i) + 3 * n if kind == "b" else Pos(0, 12, i) + 3 * n
                s = sem("take_steps")
                if kind == "b":
                    cf = coef[:, :, 0:4]
                    dve.reciprocal(rsum[:, :, :], sums[:, :, 4 * n:4 * n + 4]).then_inc(s, 1)
                    dve.wait_ge(s, steps.count(1))
                    dve.tensor_tensor(
                        coef[:, :, :].rearrange("p t (b h) -> p t b h", b=2),
                        rsum[:, :, :].rearrange("p t (b h) -> p t b h", b=2),
                        head_gates[:, :, 1:3, bass.ds(i * 4 + 2 * n, 2)], ALU.mult).then_inc(s, 1)
                    width, dst = 64, o_b[:, :, bass.ds(i * 256 + 128 * n, 128)]
                else:
                    cf = coef[:, :, 0:2]
                    dve.reciprocal(coef[:, :, 0:2], sums[:, :, 2 * n:2 * n + 2]).then_inc(s, 1)
                    dve.wait_ge(s, steps.count(1))
                    dve.tensor_scalar(coef[:, :, 1:2], coef[:, :, 1:2], neg_lam[:, 0:1], None, ALU.mult).then_inc(s, 1)
                    width, dst = 128, o_c[:, :, bass.ds(i * 512 + 128 * n, 128)]
                dve.wait_ge(s, steps.count(2))
                k = 256 // width
                dve.tensor_tensor(merged[:, :, :, :].rearrange("p t b n -> p t (b n)").rearrange(
                    "p t (k n) -> p t k n", k=k), ps[:, bank, :].rearrange("p (t k n) -> p t k n", t=2, k=k),
                    cf.rearrange("p t (k a) -> p t k a", a=1).to_broadcast([P, 2, k, width]), ALU.mult).then_inc(s, 1)
                dve.wait_ge(s, steps.count(3))
                dve.tensor_tensor(dst, merged[:, :, 0, :], merged[:, :, 1, :], ALU.add).then_inc(sem("o_taken"), 1)

            ends = bank_last(kind)
            wait(dve, sem("o_taken"), Pos(ob0, ob_n, i).count())
            for s in range(CH):
                split(u + (s + LEAD), (s + LEAD) % RING)
                for j in range(0, 8, 2):
                    if SCORES_AT[j] + 1 == s:
                        pt_copy(j)
                for j in range(8):
                    if SCORES_AT[j] == s:
                        add_bias(j)
                for j in ends:
                    if SCORES_AT[j] + 3 == s:
                        take(j)
                before = i + (it - 1)
                if not (isinstance(before, int) and before < 0):
                    gate_part(before, s)
                for f in (extra or {}).get(s, ()):
                    f()
            for j in ends:
                if SCORES_AT[j] + 3 >= CH:
                    take(j)

        def a_first():
            dve.wait_ge(sem("o_taken"), 6)
            w = a_w[:, :, :].rearrange("p t (g h) -> p t g h", g=3)
            chain("a_steps", [
                lambda: dve.tensor_reduce(a_min[:, :, :], a_negmax[:, :, :].rearrange("p t (g h) -> p t h g", g=3), AX,
                                          ALU.min),
                lambda: dve.tensor_tensor(w, a_negmax[:, :, :].rearrange("p t (g h) -> p t g h", g=3),
                                          a_min[:, :, :].rearrange("p t (a h) -> p t a h", a=1).to_broadcast(
                                              [P, 2, 3, 8]), ALU.subtract)])

        def a_second():
            dve.wait_ge(sem("a_exp"), 1)
            w = a_w[:, :, :].rearrange("p t (g h) -> p t g h", g=3)
            ops = [
                lambda: dve.tensor_tensor(a_ws[:, :, :], a_w[:, :, :], a_sums[:, :, :], ALU.mult),
                lambda: dve.tensor_reduce(a_tot[:, :, :], a_ws[:, :, :].rearrange("p t (g h) -> p t h g", g=3), AX,
                                          ALU.add),
                lambda: dve.reciprocal(a_tot[:, :, :], a_tot[:, :, :]),
                lambda: dve.tensor_tensor(w, w, a_tot[:, :, :].rearrange("p t (a h) -> p t a h", a=1).to_broadcast(
                    [P, 2, 3, 8]), ALU.mult)]

            chain("a_steps", ops)

        def a_scale(part):
            def scaled(g):
                o = o_a[:, g, :, :].rearrange("p t (h n) -> p t h n", n=HD)
                return lambda: dve.tensor_tensor(o, o, a_w[:, :, 8 * g:8 * g + 8].rearrange(
                    "p t (h a) -> p t h a", a=1).to_broadcast([P, 2, 8, HD]), ALU.mult)

            if part == 0:
                chain("a_steps", [scaled(0), scaled(1)])
                return
            ops = [scaled(2)]
            ops.append(lambda: dve.tensor_tensor(o_a[:, 0, :, :], o_a[:, 0, :, :], o_a[:, 1, :, :], ALU.add))
            chain("a_steps", ops)
            dve.tensor_tensor(o_a[:, 0, :, :], o_a[:, 0, :, :], o_a[:, 2, :, :], ALU.add).then_inc(sem("a_ready"), 1)

        c_heads = o_c[:, :, :].rearrange("p t (h n) -> p (t h) n", n=P)

        def c_squares():
            dve.wait_ge(sem("a_ready"), 1)
            dve.wait_ge(sem("o_taken"), 14)
            chain("c_steps", [lambda: dve.tensor_tensor(c_square[:, :, :], c_heads, c_heads, ALU.mult)])

        def c_means():
            sq = c_square[:, :, :]
            chain("c_steps", [
                lambda: dve.tensor_reduce(c_ssq[:, :, :].rearrange("p t h -> p (t h)"), sq, AX, ALU.add),
                lambda: dve.tensor_scalar(c_mean[:, :, :], c_ssq[:, :, :], 1.0 / P, EPS, ALU.mult, ALU.add)])

        def c_second():
            dve.wait_ge(sem("c_root"), 1)
            flat = lambda a: a[:, :, :].rearrange("p t h -> p (t h)")
            chain("c_steps", [
                lambda: dve.reciprocal(flat(c_rstd), flat(c_root)),
                lambda: dve.tensor_tensor(flat(c_ssq), flat(c_rstd), flat(c_rstd), ALU.mult),
                lambda: dve.tensor_tensor(flat(c_ssq), flat(c_ssq), flat(c_mean), ALU.mult),
                lambda: dve.tensor_scalar(flat(c_ssq), flat(c_ssq), -0.5, 1.5, ALU.mult, ALU.add),
                lambda: dve.tensor_tensor(flat(c_rstd), flat(c_rstd), flat(c_ssq), ALU.mult),
                lambda: dve.tensor_scalar(flat(c_rstd), flat(c_rstd), 1.0 - LAM_INIT, None, ALU.mult),
                lambda: dve.tensor_tensor(c_heads, c_heads, flat(c_rstd).rearrange("p (h a) -> p h a", a=1)
                                          .to_broadcast([P, 16, P]), ALU.mult)])
            dve.tensor_tensor(c_heads, c_heads, sub_gain[:, :].rearrange("p (a n) -> p a n", a=1)
                              .to_broadcast([P, 16, P]), ALU.mult).then_inc(sem("c_ready"), 1)

        def gelu_first():
            dve.wait_ge(sem("hidden_mm"), 1)
            h, a = hid[:, 0, :], hid[:, 1, :]
            chain("gelu_steps", [
                lambda: dve.tensor_copy(h, ps[:, 2, 0:120]),
                lambda: dve.tensor_tensor(a, h, h, ALU.mult),
                lambda: dve.tensor_scalar(a, a, 0.044715, 1.0, ALU.mult, ALU.add),
                lambda: dve.tensor_tensor(a, a, h, ALU.mult),
                lambda: dve.tensor_scalar(a, a, -50.0, None, ALU.max)])

        def gelu_second():
            dve.wait_ge(sem("gelu_exp"), 1)
            h, e = hid[:, 0, :], hid[:, 2, :]
            chain("gelu_steps", [
                lambda: dve.tensor_scalar(e, e, 1.0, None, ALU.add),
                lambda: dve.reciprocal(e, e)])
            dve.tensor_tensor(hid_k[:, :, :].rearrange("p a n -> p (a n)"), h[:, 0:60], e[:, 0:60], ALU.mult).then_inc(
                sem("gelu_ready"), 1)
            dve.wait_ge(sem("cmp_zero"), 3)
            chain("gelu_steps", [lambda: dve.tensor_tensor(h[:, 60:120], h[:, 60:120], e[:, 60:120], ALU.mult)])
            for g in range(2):
                dve.tensor_copy(hid_v[:, :, g, :, 0:NCMP], h[:, 60:120].rearrange(
                    "p (c g n) -> p c g n", c=2, g=2)[:, :, g, :].rearrange("p c (a n) -> p c a n", a=1)
                    .to_broadcast([P, 2, 4, NCMP])).then_inc(sem("gelu_ready"), 1)

        def compressed():
            dve.wait_ge(sem("compressed_mm"), 1)
            for q in range(4):
                part = slice(32 * q, 32 * q + 32)
                dve.tensor_copy(vc_diag[part, :, q, :], ps[part, 3, 64:192].rearrange("p (g n) -> p g n", g=2))
            dve.tensor_copy(kc_t[:, :], ps[:, 3, 0:30]).then_inc(sem("compressed"), 1)

        def cmp_first():
            dve.wait_ge(sem("cmp_scores"), 1)
            for t in range(2):
                for odd in range(2):
                    last = dve.tensor_tensor(
                        cmp_l[:, t, odd::2, :], ps[:, 4 + 2 * odd + t, 0:128].rearrange("p (h n) -> p h n", h=8)[
                            :, :, 0:NCMP], bmask[:, t, :].rearrange("p (a n) -> p a n", a=1).to_broadcast(
                                [P, 8, NCMP]), ALU.add)
            last.then_inc(sem("cmp_steps"), 1)
            dve.wait_ge(sem("cmp_steps"), 1)
            done["cmp_steps"] = 1
            l4 = cmp_l[:, :, :, :].rearrange("p t h n -> p (t h) n")
            mx = m_max[:, :, :].rearrange("p t h -> p (t h)")
            chain("cmp_steps", [
                lambda: dve.tensor_reduce(mx, l4, AX, ALU.max),
                lambda: dve.tensor_scalar(mx, mx, 0.5 * NEG, None, ALU.max),
                lambda: dve.tensor_tensor(l4, l4, mx.rearrange("p (h a) -> p h a", a=1).to_broadcast([P, 32, NCMP]),
                                          ALU.subtract)])

        def cmp_second():
            dve.wait_ge(sem("cmp_exp"), 1)
            l4 = cmp_l[:, :, :, :].rearrange("p t h n -> p (t h) n")
            sm = m_sum[:, :, :].rearrange("p t h -> p (t h)")
            chain("cmp_steps", [
                lambda: dve.tensor_reduce(sm, l4, AX, ALU.add),
                lambda: dve.tensor_scalar(sm, sm, TINY, None, ALU.max),
                lambda: dve.reciprocal(sm, sm),
                lambda: dve.tensor_tensor(m_coef[:, :, :], m_sum[:, :, :], head_gates[:, :, 0, :], ALU.mult)])
            dve.tensor_tensor(cmp_p[:, :, :, 0:NCMP].rearrange("p t h n -> p (t h) n"), l4,
                              m_coef[:, :, :].rearrange("p t (h a) -> p (t h) a", a=1).to_broadcast([P, 32, NCMP]),
                              ALU.mult).then_inc(sem("cmp_probs"), 1)

        def cmp_third():
            dve.wait_ge(sem("cmp_pt"), 1)
            dve.tensor_copy(cmp_pt[:, :, :].rearrange("p (b a) n -> p b (a n)", b=2), ps[:, 6:8, :]).then_inc(
                sem("cmp_pt_copied"), 1)

        def cmp_fourth():
            dve.wait_ge(sem("cmp_pv"), 1)
            for t in range(2):
                o = o_b[:, t, :].rearrange("p (b n) -> p b n", b=2)
                last = dve.tensor_tensor(o, ps[:, 2 + 2 * t:4 + 2 * t, :], o, ALU.add)
            last.then_inc(sem("b_ready"), 1)

        between_maps = {"c": {1: [a_first], 4: [a_second], 6: [lambda: a_scale(0)], 7: [lambda: a_scale(1)]},
                        "b": {5: [c_squares], 6: [c_means]}}
        for kind, n in LOOPS:
            maps(kind, 0, between_maps.get(kind))
            with dve.Fori(1, n) as i:
                maps(kind, i)

        def o_split(q):
            g, bank = O_PAIRS[q], O_BANKS[q]
            dve.wait_ge(sem("o_split_hi"), q + 1)
            dve.tensor_tensor(o_lo[:, 2 * g:2 * g + 2, :], ps[:, bank, :].rearrange("p (a n) -> p a n", a=2),
                              o_hi[:, 2 * g:2 * g + 2, :].bitcast(F32), ALU.subtract).then_inc(sem("o_split_lo"), 1)

        dve_steps = {0: [c_second], 2: [gelu_first], 4: [gelu_second], 6: [compressed], 8: [cmp_first],
                     10: [cmp_second], 12: [cmp_third], 14: [cmp_fourth]}
        for q, n in enumerate(O_AT):
            dve_steps.setdefault(n + 1, []).append(lambda q=q: o_split(q))
        for n in range(NSTEP):
            c, s = divmod(n, CH)
            split(Pos(U0["gate"] + 72 + n + LEAD), (s + LEAD) % RING)
            for f in dve_steps.get(n, ()):
                f()
            gate_part(8 + c, s)

        def merge(n, b):
            if b == 0:
                dve.wait_ge(sem(f"gates_loaded{n % 2}"), 16 * (n // 2 + 1))
            dst = br_stage[:, n % 2, :, :] if b == 0 else br_tmp[:, :, :]
            for h in range(2):
                if h == 0:
                    dve.wait_ge(sem("half_done"), C0["branch"] + 3 * n + b + 1)
                else:
                    dve.wait_ge(sem("unit_used"), U0["branch"] + 10 * n + sum(BR_UNITS[:b + 1]))
                dve.tensor_tensor(dst[:, h, :], ps[:, 2 * b + h, :], gates_in[:, n % 2, b, h, :], ALU.mult).then_inc(
                    sem("evac_v"), 1)
            if b == 0:
                return
            dve.wait_ge(sem("evac_v"), V0["branch"] + 2 * (3 * n + b + 1))
            whole = br_stage[:, n % 2, :, :]
            add = dve.tensor_tensor(whole, whole, br_tmp[:, :, :], ALU.add)
            add.then_inc(sem("merge_done" if b == 2 else "merge_steps"), 1)
            if b == 1:
                dve.wait_ge(sem("merge_steps"), n + 1)

        for n in range(4):
            u0 = U0["branch"] + 10 * n
            for b in range(3):
                before = sum(BR_UNITS[:b])
                for j in range(BR_UNITS[b]):
                    if n == 0 and before + j <= max(GATE_PARTS):
                        gate_part(11, before + j)
                    split(Pos(u0 + before + j + LEAD), (10 * n + before + j + LEAD) % RING)
                    if n > 0 and before + j == 5:
                        t_split(Pos(T0["branch"] + n - 1), h_lo[:, 4 * (n - 1):4 * n, :], h_hi[:, 4 * (n - 1):4 * n, :])
                merge(n, b)
        t_split(Pos(T0["branch"] + 3), h_lo[:, 12:16, :], h_hi[:, 12:16, :])

        with dve.Fori(0, 4) as i:
            u = Pos(U0["out"], CH, i)
            chunk(u, CH)
            copy_out(y[:, 0, bass.ds(i * W, W)], 0, Pos(C0["out"], 1, i).count(1))

        def residual(k, ready):
            dve.wait_ge(sem("gain_loaded"), 16 * (1 if k == 1 else 2))
            for t in range(2):
                dve.scalar_tensor_tensor(y[:, t, :], y[:, t, :], rstd[:, k, t:t + 1], gain_row[:, :], ALU.mult,
                                         ALU.mult).then_inc(sem(f"scaled{k}"), 1)
            for t in range(2):
                dve.wait_ge(sem(f"scaled{k}"), t + 1)
                dve.tensor_tensor(mid[:, t, :], mid[:, t, :], y[:, t, :], ALU.add).then_inc(sem(ready), 1)

        dve.wait_ge(sem("evac_v"), V0["up0"])
        dve.wait_ge(sem("evac_s"), S0["up0"])
        norm_stats(1, y)
        dve.wait_ge(sem("x_again"), 32)
        residual(1, "mid_ready")
        dve.wait_ge(sem("mid_ready"), 2)
        norm_stats(2, mid)
        norm_split(2, mid, mid_normed)

        def up(name, i):
            u, t, es = Pos(U0[name], 2 * CH, i), Pos(T0[name], 2, i), Pos(S0[name], 4, i)

            def square(c):
                dve.wait_ge(sem("evac_s"), es.count(2 * c + 2))
                dve.tensor_tensor(up_stage[:, c, :, :], up_stage[:, c, :, :], up_stage[:, c, :, :], ALU.mult).then_inc(
                    sem("evac_v"), 1)

            def group(t, first):
                return {2: [lambda: t_split(t, u_lo[:, bass.ds(first, 4), :], u_hi[:, bass.ds(first, 4), :])]}

            chunk(u, CH, after=None if isinstance(i, int) else group(t + (-1), i * 8 - 4))
            square(0)
            chunk(u + CH, CH, after=group(t, i * 8))
            square(1)

        def down(h, i):
            u = Pos(U0[f"down{h}"], 16, i)
            chunk(u, 16, after={2: [lambda: t_split(Pos(T0[f"down{h}"] - 1), u_lo[:, 28:32, :], u_hi[:, 28:32, :])]}
                  if isinstance(i, int) and i == 0 else None)
            half = Pos(C0[f"down{h}"], 1, i).count(1)
            part = y[:, 0, bass.ds(i * W, W)]
            if h == 0:
                copy_out(part, 0, half)
                return
            for t in range(2):
                if t == 0:
                    dve.wait_ge(sem("half_done"), half)
                else:
                    dve.wait_ge(sem("unit_used"), u.count(16))
                part = y[:, t, bass.ds(i * W, W)]
                dve.tensor_tensor(part, ps[:, t, :], part, ALU.add).then_inc(sem("evac_v"), 1)

        for h in range(2):
            up(f"up{h}", 0)
            with dve.Fori(1, 4) as i:
                up(f"up{h}", i)
            down(h, 0)
            with dve.Fori(1, 4 - h) as i:
                down(h, i)
            if h == 1:
                down(h, 3)
        dve.wait_ge(sem("evac_v"), V0["down1"] + 8)
        norm_stats(3, y)
        residual(3, "result_ready")


def _constants():
    import numpy as np

    exact, buckets = 16, 32
    dist = np.arange(512) - 127
    d = np.maximum(dist, 0)
    logd = np.log(np.maximum(d, 1).astype(np.float32) / np.float32(exact))
    far = exact + (logd / np.float32(math.log(2048 / exact)) * (buckets - exact)).astype(np.int32)
    bucket = np.where(d < exact, d, np.minimum(far, buckets - 1))
    onehot = (bucket[None, :] == np.arange(buckets)[:, None]).astype(np.float32)
    mask = np.zeros((48, 512), np.float32)
    mask[:, dist < 0] = NEG
    for g, (window, step) in enumerate(((128, 1), (512, 4), (2048, 16))):
        mask[8 * g:8 * g + 8, (dist < 0) | (dist > window) | (dist % step != 0)] = NEG
    t = np.arange(SEQ)
    seen = (np.arange(NCMP) * CSTRIDE + 31)[None, :] <= t[:, None]
    blocks = np.where(seen, 0.0, NEG).astype(np.float32).reshape(2, P, NCMP).transpose(1, 0, 2)
    return {"identity": np.eye(P, dtype=np.float32), "bucket_onehot": onehot, "distance_mask": mask,
            "block_mask": np.ascontiguousarray(blocks)}


_INS = ["x", "rel_bias", "w_in", "cmp_k_pos", "cmp_v_pos", "cmp_k_w1", "cmp_k_w2", "cmp_v_w1", "cmp_v_w2",
        "diff_lambda", "diff_norm", "w_branch_a", "w_branch_b", "w_branch_c", "w_out", "norm_mix_pre",
        "norm_mix_post", "norm_mlp_pre", "norm_mlp_post", "w_up", "w_down"]


def kernel(**inputs):
    import numpy as np
    import concourse.bacc as bacc
    from concourse.bass_utils import run_bass_kernel_spmd

    nc = bacc.Bacc("TRN2", target_bir_lowering=False, num_devices=1)
    given = {name: np.ascontiguousarray(inputs[name]) for name in _INS}
    given.update(_constants())
    arrays, args = {}, []
    for name, a in given.items():
        arrays[f"in_{name}_dram"] = a
        args.append(nc.dram_tensor(f"in_{name}_dram", a.shape, mybir.dt.from_np(a.dtype), kind="ExternalInput").ap())
    args.append(nc.dram_tensor("out_0_dram", (1, SEQ, D), F32, kind="ExternalOutput").ap())
    trunk(nc, *args)
    r = run_bass_kernel_spmd(nc, [arrays], core_ids=[0])
    return r.results[0]["out_0_dram"]
```

```python
import math
from contextlib import ExitStack

import concourse.bass as bass
from concourse import mybir
from concourse.alu_op_type import AluOpType as ALU

F32 = mybir.dt.float32
F32R = mybir.dt.float32r
ACT = mybir.ActivationFunctionType
AX = mybir.AxisListType.X

P = 128
D = 2048
SEQ = 256
HD = 64
DFF = 8192
KC = D // P
W = 512
UR = 2
RING = 4
LEAD = 3
EPS = 1e-6
SCALE = HD ** -0.5
TINY = 1e-30
NEG = -1e30
LAM_INIT = 0.8 - 0.6
NCMP = 15
CSTRIDE = 16

A_Q, A_K, A_V = 0, 1536, 3072
B_Q, B_KV = 4608, 5632
C_Q, C_K, C_V = 6448, 7472, 8496
M_G = 9520
B_LAST = 304

CH = KC // UR
ORDER = [("qk_a", 6, CH), ("v_a", 3, CH), ("q_b", 2, CH), ("kv_b", 2, CH), ("qk_c", 4, CH), ("v_c", 2, CH),
         ("gate", 12, CH), ("branch", 4, 10), ("out", 4, CH),
         ("up0", 8, CH), ("down0", 4, 16), ("up1", 8, CH), ("down1", 4, 16)]
U0, C0 = {}, {}
_u = _c0 = 0
for _n, _c, _k in ORDER:
    U0[_n], C0[_n] = _u, _c0
    _u += _c * _k
    _c0 += 3 * _c if _n == "branch" else _c
UNITS = _u
V_OF = {"gate": 0, "branch": 6, "out": 2, "down1": 2}
S_OF = {"branch": 0, "out": 2, "down1": 2, "gate": 2, "up0": 2, "up1": 2}
T_OF = {"v_a": 0, "v_c": 0, "gate": 0, "out": 0, "down0": 0, "down1": 0}
V0, S0, T0 = {}, {}, {}
_v = _s = _t = 0
for _n, _c, _k in ORDER:
    V0[_n], S0[_n], T0[_n] = _v, _s, _t
    _v += _c * V_OF.get(_n, 1)
    _s += _c * S_OF.get(_n, 1)
    _t += _c * T_OF.get(_n, 1)

SCORES_AT = [0, 0, 1, 2, 3, 3, 4, 5]
STORE_AT = 3
GATE_PARTS = {0: (0, 256), 1: (256, 512), 2: (512, 640), 3: (640, 768), 4: (768, 1024)}
NSTEP = 24
O_PAIRS = [0, 1, 6, 7, 8, 9, 2, 3, 4, 5]
O_BANKS = [4, 5, 6, 7, 4, 5, 6, 7, 2, 3]
O_AT = [2, 2, 3, 4, 5, 5, 15, 15, 17, 18]


FIRST = "first"


class Pos:

    def __init__(self, k, per=0, i=0):
        self.k, self.per, self.i = k, per, i

    def __add__(self, n):
        return Pos(self.k + n, self.per, self.i)

    def count(self, n=0):
        if isinstance(self.i, int):
            return self.k + n + self.per * self.i
        return self.i * self.per + (self.k + n)

    def loads(self):
        r = 16 * (self.k // RING + 1)
        if isinstance(self.i, int):
            return r + 16 * (self.per // RING) * self.i
        return self.i * (16 * (self.per // RING)) + r


def wait(eng, sem, value):
    if not (isinstance(value, int) and value <= 0):
        eng.wait_ge(sem, value)


def held(eng, register, value):
    if isinstance(value, int):
        return value
    eng.reg_add(register, eng.snap(value - 1), 1)
    return register


def trunk(nc, x, rel_bias, w_in, cmp_k_pos, cmp_v_pos, cmp_k_w1, cmp_k_w2, cmp_v_w1, cmp_v_w2, diff_lambda,
          diff_norm, w_branch_a, w_branch_b, w_branch_c, w_out, norm_mix_pre, norm_mix_post, norm_mlp_pre,
          norm_mlp_post, w_up, w_down, identity, bucket_onehot, distance_mask, block_mask, out):
    bias_table = nc.dram_tensor("bias_table", (48, 512), F32, kind="Internal").ap()
    gate_dram = nc.dram_tensor("gate_dram", (P, 12, 1024), F32, kind="Internal").ap()
    hankel = bass.AP(bias_table.tensor, 0, [[512, 48], [1, P], [1, 256]])

    ctx = ExitStack()
    sems = {}

    def sem(name):
        if name not in sems:
            sems[name] = ctx.enter_context(nc.semaphore(name))
        return sems[name]

    base = 16512
    regions = {"small": [0, 5888], "ring": [5888, 49152], "h": [55040, 32768], "u": [87808, 65536],
               "f": [153344, 59392]}
    marks = {k: v[0] for k, v in regions.items()}

    def put(region, name, shape, dt=F32, at=None):
        size = 4 * math.prod(shape[1:])
        off = marks[region] if at is None else regions[region][0] + at
        off = (off + 31) // 32 * 32
        assert off + size <= regions[region][0] + regions[region][1], (name, off + size)
        if at is None:
            marks[region] = off + size
        return nc.alloc_sbuf_tensor_at(name, shape, dt, offset=base + off)

    ident = put("small", "ident", [P, P])
    columns = put("small", "columns", [P, 64])
    ssq_parts = put("small", "ssq_parts", [P, 4, 2, 4])
    rstd_q = put("small", "rstd_q", [P, 2])
    rstd_neg = put("small", "rstd_neg", [P, 2])
    ssq = put("small", "ssq", [P, 4, 2])
    mean = put("small", "mean", [P, 4, 2])
    root = put("small", "root", [P, 4, 2])
    inv = put("small", "inv", [P, 4, 2])
    newton = put("small", "newton", [P, 4, 2])
    rstd = put("small", "rstd", [P, 4, 2])
    head_gates = put("small", "head_gates", [P, 2, 3, 16])
    negmax = put("small", "negmax", [P, 2, 8])
    sums = put("small", "sums", [P, 2, 8])
    coef = put("small", "coef", [P, 2, 4])
    rsum = put("small", "rsum", [P, 2, 4])
    a_negmax = put("small", "a_negmax", [P, 2, 24])
    a_sums = put("small", "a_sums", [P, 2, 24])
    a_min = put("small", "a_min", [P, 2, 8])
    a_w = put("small", "a_w", [P, 2, 24])
    a_ws = put("small", "a_ws", [P, 2, 24])
    a_tot = put("small", "a_tot", [P, 2, 8])
    lam2 = put("small", "lam2", [P, 4])
    neg_lam = put("small", "neg_lam", [P, 1])
    c_ssq = put("small", "c_ssq", [P, 2, 8])
    c_mean = put("small", "c_mean", [P, 2, 8])
    c_root = put("small", "c_root", [P, 2, 8])
    c_rstd = put("small", "c_rstd", [P, 2, 8])
    sub_gain = put("small", "sub_gain", [P, P])
    bmask = put("small", "bmask", [P, 2, NCMP])
    m_max = put("small", "m_max", [P, 2, 16])
    m_sum = put("small", "m_sum", [P, 2, 16])
    m_coef = put("small", "m_coef", [P, 2, 16])
    kc_diag = put("small", "kc_diag", [P, 2, 2, NCMP])

    raw = put("ring", "raw", [P, RING, UR, W])
    w_hi = put("ring", "w_hi", [P, RING, UR, W], F32R)
    w_lo = put("ring", "w_lo", [P, RING, UR, W], F32R)
    h_hi = put("h", "h_hi", [P, KC, SEQ], F32R)
    h_lo = put("h", "h_lo", [P, KC, SEQ], F32R)

    q_c = put("u", "q_c", [P, 8, SEQ])
    k_c = put("u", "k_c", [P, 8, SEQ])
    v_c = put("u", "v_c", [P, 2, 1024])
    v_a = put("u", "v_a", [P, 2, 1536])
    logits = put("u", "logits", [P, 4, 384])
    blocks_t = put("u", "blocks_t", [P, 2, KC, 2 * NCMP])
    q_b = put("u", "q_b", [P, 8, SEQ])
    k_b = put("u", "k_b", [P, 4, SEQ])
    v_b = put("u", "v_b", [P, 2, 2, P])
    cmp_t = put("u", "cmp_t", [P, 4, SEQ])
    x_in = put("u", "x_in", [P, 2, D], at=0)
    w1k = put("u", "w1k", [P, KC, 256], at=0)
    w1v = put("u", "w1v", [P, KC, 256], at=16384)
    hid_rows = put("f", "hid_rows", [2 * NCMP, 2, 256], at=4096)
    hid = put("u", "hid", [P, 3, 8 * NCMP], at=43008)
    hid_k = put("u", "hid_k", [P, 2, 2 * NCMP], at=43008 + 1536)
    hid_v = put("u", "hid_v", [P, 2, 2, 4, 32], at=40960)
    o_hi = put("u", "o_hi", [P, 20, SEQ], F32R, at=0)
    o_lo = put("u", "o_lo", [P, 20, SEQ], F32R, at=20480)
    u_hi = put("u", "u_hi", [P, 32, SEQ], F32R, at=0)
    u_lo = put("u", "u_lo", [P, 32, SEQ], F32R, at=32768)

    o_a = put("f", "o_a", [P, 3, 2, 512])
    k_a = put("f", "k_a", [P, 12, SEQ])
    q_a = put("f", "q_a", [P, 12, SEQ])
    stage = put("f", "stage", [P, 2, 2, W])
    q_pad = put("f", "q_pad", [P, 4, SEQ])
    bias = put("f", "bias", [P, 4, SEQ])
    p_t = put("f", "p_t", [P, 2, 384])
    w2k = put("f", "w2k", [P, 2, 2, HD])
    w2v = put("f", "w2v", [P, 2, HD])
    o_c = put("f", "o_c", [P, 2, 1024], at=12288)
    o_b = put("f", "o_b", [P, 2, 1024], at=24576)
    merged = put("f", "merged", [P, 2, 2, 128], at=36864 + 4096)
    dup = put("f", "dup", [P, 2, 8, 2, HD], at=0)
    rows64 = put("f", "rows64", [64, P], at=0)
    onehot = put("f", "onehot", [32, 512], at=1024)
    dmask = put("f", "dmask", [48, 512], at=3072)
    rel = put("f", "rel", [32, 48], at=5120)
    table = put("f", "table", [48, 512], at=6144)
    lam_rows = put("f", "lam_rows", [P, 4, HD], at=8192)
    lam_prod = put("f", "lam_prod", [P, 2, HD], at=9216)
    cmp_l = put("f", "cmp_l", [P, 2, 16, NCMP], at=36864 + 8192 + 4096)
    cmp_p = put("f", "cmp_p", [P, 2, 16, 32], at=36864 + 8192)
    cmp_pt = put("f", "cmp_pt", [P, 8, P], at=36864 + 4096)
    vc_diag = put("f", "vc_diag", [P, 2, 4, HD], at=36864 + 16384)
    c_square = put("f", "c_square", [P, 8, P], at=20480)
    gates_in = put("f", "gates_in", [P, 2, 3, 2, W], at=0)
    br_tmp = put("f", "br_tmp", [P, 2, W], at=24576)
    br_stage = put("f", "br_stage", [P, 2, 2, W], at=45056)
    mid = put("f", "mid", [P, 2, D], at=0)
    y = put("f", "y", [P, 2, D], at=16384)
    gain_row = put("f", "gain_row", [P, D], at=32768)
    squares = put("f", "squares", [P, W], at=53248)
    up_stage = put("f", "up_stage", [P, 2, 2, W], at=40960)

    ps = ctx.enter_context(nc.psum_tensor("ps", [P, 8, 512], F32))
    T_BANK = 6

    w_in_v = w_in.rearrange("l (c p) n -> p (l c) n", p=P)
    w_out_v = w_out.rearrange("l (c p) n -> p (l c) n", p=P)
    w_up_v = w_up.rearrange("l (c p) n -> p (l c) n", p=P)
    w_down_v = w_down.rearrange("l (c p) n -> p (l c) n", p=P)
    w_br_v = [w.rearrange("l (c p) n -> p (l c) n", p=P) for w in (w_branch_a, w_branch_b, w_branch_c)]
    BR_UNITS = [2, 4, 4]
    BR_KC = [0, 4, 12]

    def attn(kind, i, j):
        if kind == "a":
            return i * 4 + j // 2, i * 4 + j // 2, i * 8 + j
        if kind == "b":
            key = i // 2 + 2 * ((j // 2) % 2)
            return i * 2 + j // 4, key, i * 4 + (24 + 2 * (j // 4) + j % 2)
        return i * 4 + j // 2, i * 4 + j // 2, i * 4 + (40 + j // 2)

    FIRST_IT = {"a": 0, "c": 3, "b": 5}
    LOOPS = [("a", 3), ("c", 2), ("b", 4)]

    def bank_of(kind, j):
        n = j // 2 if kind == "c" else j // 4
        return n, 6 + n % 2

    def banks_before(kind):
        return {"a": 0, "c": 6, "b": 14}[kind], 4 if kind == "c" else 2

    def bank_last(kind):
        return [1, 3, 5, 7] if kind == "c" else [3, 7]

    block = ctx.enter_context(nc.Block())

    @block.sync
    def _(sp):
        def load(u, slot, view, kc, col, cols=W):
            wait(sp, sem("lo_ready"), u.count(1 - RING))
            sp.dma_start(raw[:, slot, :, 0:cols], view[:, kc:kc + UR, bass.ds(col, cols)]).then_inc(
                sem(f"raw_loaded{slot}"), 16)

        def chunk(u, view, kc, n, col, cols=W, s0=0):
            for j in range(n):
                load(u + j, (s0 + j) % RING, view, kc + UR * j, col, cols)

        def load_x(b):
            sp.dma_start(x_in[:, :, W * b:W * b + W], x[0].rearrange("(t p) n -> p t n", p=P)[:, :, W * b:W * b + W]
                         ).then_inc(sem(f"x_loaded{b}"), 16)

        def qk_a(i):
            chunk(Pos(U0["qk_a"], 2 * CH, i), w_in_v, 0, CH, i * W + A_Q)
            chunk(Pos(U0["qk_a"] + CH, 2 * CH, i), w_in_v, 0, CH, i * W + A_K)

        sp.dma_start(ident[:, :], identity).then_inc(sem("ident_loaded"), 16)
        for b in range(2):
            load_x(b)
            chunk(Pos(U0["qk_a"] + 2 * b), w_in_v, 2 * UR * b, 2, A_Q, s0=2 * b)
        load_x(2)
        load_x(3)
        chunk(Pos(U0["qk_a"] + 4), w_in_v, 4 * UR, 4, A_Q)
        chunk(Pos(U0["qk_a"] + CH), w_in_v, 0, CH, A_K)
        with sp.Fori(1, 3) as i:
            qk_a(i)
        with sp.Fori(0, 3) as i:
            chunk(Pos(U0["v_a"], CH, i), w_in_v, 0, CH, i * W + A_V)
        for c in range(2):
            chunk(Pos(U0["q_b"] + CH * c), w_in_v, 0, CH, B_Q + W * c)
        chunk(Pos(U0["kv_b"]), w_in_v, 0, CH, B_KV)
        chunk(Pos(U0["kv_b"] + CH), w_in_v, 0, CH, B_KV + W, B_LAST)
        with sp.Fori(0, 2) as i:
            chunk(Pos(U0["qk_c"], 2 * CH, i), w_in_v, 0, CH, i * W + C_Q)
            chunk(Pos(U0["qk_c"] + CH, 2 * CH, i), w_in_v, 0, CH, i * W + C_K)
        with sp.Fori(0, 2) as i:
            chunk(Pos(U0["v_c"], CH, i), w_in_v, 0, CH, i * W + C_V)

        def store_gates(c):
            sp.wait_ge(sem("gates_made"), c + 1)
            sp.dma_start(gate_dram[:, bass.ds(c, 1), :].rearrange("p a n -> p (a n)"),
                         stage[:, 0, :, :].rearrange("p t n -> p (t n)")).then_inc(sem("gates_stored"), 16)

        for c in range(2):
            chunk(Pos(U0["gate"] + CH * c), w_in_v, 0, CH, M_G + W * c)
        with sp.Fori(2, 12) as i:
            chunk(Pos(U0["gate"], CH, i), w_in_v, 0, STORE_AT, i * W + M_G)
            store_gates(i - 2)
            chunk(Pos(U0["gate"] + STORE_AT, CH, i), w_in_v, UR * STORE_AT, CH - STORE_AT, i * W + M_G, s0=STORE_AT)

        def load_gates(n, b):
            sp.wait_ge(sem("gates_stored"), 16 * (4 * b + n + 1))
            wait(sp, sem("merge_done"), n - 1)
            sp.dma_start(gates_in[:, n % 2, b, :, :].rearrange("p t n -> p (t n)"), gate_dram[:, 4 * b + n, :]
                         ).then_inc(sem(f"gates_loaded{n % 2}_{b}"), 16)

        for n in range(4):
            gates_at = {4: [(0, 2)] if n else [], 6: [] if n else [(0, 2)], 7: [(1, 0)], 9: [(1, 1)]}
            for b in range(3):
                for j in range(BR_UNITS[b]):
                    before = sum(BR_UNITS[:b]) + j
                    chunk(Pos(U0["branch"] + 10 * n + before), w_br_v[b], UR * j, 1, W * n, s0=(10 * n + before) % RING)
                    if n == 0 and before == 2:
                        store_gates(10)
                    if n == 0 and before == 3:
                        sp.wait_ge(sem("o_split_lo"), 10)
                        load_gates(0, 0)
                    if n == 0 and before == 5:
                        load_gates(0, 1)
                    if n == 1 and before == 1:
                        store_gates(11)
                    for ahead, branch in gates_at.get(before, ()):
                        if n + ahead < 4:
                            load_gates(n + ahead, branch)
        with sp.Fori(0, 4) as i:
            chunk(Pos(U0["out"], CH, i), w_out_v, 0, CH, i * W)

        def up(h, i):
            for c in range(2):
                chunk(Pos(U0[f"up{h}"] + CH * c, 2 * CH, i), w_up_v, 0, CH, i * (2 * W) + (h * DFF // 2 + W * c))

        def down(h, i):
            chunk(Pos(U0[f"down{h}"], 16, i), w_down_v, 32 * h, 16, i * W)

        for h in range(2):
            with sp.Fori(0, 4) as i:
                up(h, i)
            with sp.Fori(0, 4) as i:
                down(h, i)
        for b in range(4):
            sp.wait_ge(sem("result_ready"), 2 * b + 2)
            sp.dma_start(out[0].rearrange("(t p) n -> p t n", p=P)[:, :, W * b:W * b + W],
                         mid[:, :, W * b:W * b + W]).then_inc(sem("stored"), 16)
        sp.wait_ge(sem("stored"), 64)

    @block.gpsimd
    def _(pool):
        pool_count = pool.alloc_register("pool_count")

        def load(dst, src, name="const_loaded"):
            pool.dma_start(dst, src).then_inc(sem(name), 16)

        load(onehot[:, :], bucket_onehot)
        load(dmask[:, :], distance_mask)
        load(rel[:, :], rel_bias)
        load(bmask[:, :, :], block_mask)
        load(lam_rows[:, :, :], bass.AP(diff_lambda.tensor, 0, [[0, P], [HD, 4], [1, HD]]))
        load(sub_gain[:, :], bass.AP(diff_norm.tensor, 0, [[0, P], [1, P]]))
        pool.wait_ge(sem("table_ready"), 1)
        pool.dma_start(bias_table, table[:, :]).then_inc(sem("table_stored"), 16)
        pool.memset(q_pad[:, :, :], 0.0).then_inc(sem("pad_zero"), 1)

        def queries_and_bias(kind, i):
            src = {"a": q_a, "b": q_b, "c": q_c}[kind]
            m0 = Pos(8 * FIRST_IT[kind], 8, i)
            for j in range(8):
                tile, _, row = attn(kind, i, j)
                half = slice(64 * (j % 2), 64 * (j % 2) + 64)
                behind = held(pool, pool_count, (m0 + j).count(-3))
                pool.wait_ge(sem("pad_zero"), 1)
                wait(pool, sem("scores_ready"), behind)
                pool.tensor_copy(q_pad[half, j % 4, :], src[half, bass.ds(tile, 1), :].rearrange("p a n -> p (a n)")
                                 ).then_inc(sem("query_ready"), 1)
                pool.wait_ge(sem("table_stored"), 16)
                wait(pool, sem("logits_ready"), behind)
                pool.dma_start(bias[:, j % 4, :], hankel[bass.ds(row, 1)].rearrange("a p n -> (a p) n")).then_inc(
                    sem(f"bias_loaded{j % 4}"), 16)

        def cmp_weights(i):
            for dst, src in ((w1k, cmp_k_w1), (w1v, cmp_v_w1)):
                pool.dma_start(dst[:, bass.ds(i * 4, 4), :], src.rearrange("l (c p) n -> p (l c) n", p=P)[
                    :, bass.ds(i * 4, 4), :]).then_inc(sem("w1_loaded"), 16)

        for name, n in (("tevac_v", T0["gate"]), ("tevac_s", T0["gate"])):
            pool.wait_ge(sem(name), n)
        for kind, n in LOOPS:
            queries_and_bias(kind, 0)
            if kind == "b":
                pool.wait_ge(sem("pv_done"), 8 * FIRST_IT["b"])
                cmp_weights(0)
            with pool.Fori(1, n) as i:
                queries_and_bias(kind, i)
                if kind == "b":
                    cmp_weights(i)
        pool.wait_ge(sem("pv_done"), 72)
        w2_k = cmp_k_w2.rearrange("l (c p) n -> p (l c) n", p=P)
        for a in range(2):
            pool.dma_start(w2k[:, :, a, :], w2_k).then_inc(sem("w2_loaded"), 16)
        pool.dma_start(w2v[:, :, :], cmp_v_w2.rearrange("l (c p) n -> p (l c) n", p=P)).then_inc(sem("w2_loaded"), 16)
        pool.memset(kc_diag[:, :, :, :], 0.0).then_inc(sem("cmp_zero"), 1)
        pool.memset(hid_v[:, :, :, :, :], 0.0).then_inc(sem("cmp_zero"), 1)
        pool.memset(vc_diag[:, :, :, :], 0.0).then_inc(sem("cmp_zero"), 1)
        pool.memset(cmp_p[:, :, :, :], 0.0).then_inc(sem("cmp_zero"), 1)
        pool.wait_ge(sem("gates_stored"), 16 * 12)
        pool.dma_start(gain_row[:, :], bass.AP(norm_mix_post.tensor, 0, [[0, P], [1, D]])).then_inc(sem("gain_loaded"), 16)
        pool.wait_ge(sem("merge_done"), 4)
        for t in range(2):
            pool.dma_start(mid[:, t, :], x[0, t * P:(t + 1) * P, :]).then_inc(sem("x_again"), 16)
        pool.wait_ge(sem("evac_v"), V0["up0"])
        pool.dma_start(gain_row[:, :], bass.AP(norm_mlp_post.tensor, 0, [[0, P], [1, D]])).then_inc(sem("gain_loaded"), 16)

    @block.tensor
    def _(pe):
        def unit(u, slot, hi, lo, kc, pair, cols=W, first=False, last=False, free=None):
            pe.wait_ge(sem("lo_ready"), u.count(1))
            for t in range(2):
                if free is not None:
                    for name, value in free[t]:
                        wait(pe, sem(name), value)
                acc = ps[:, 2 * pair + t, 0:cols]
                for k in range(UR):
                    tok = slice(t * P, (t + 1) * P)
                    a, b = first and k == 0, last and k == UR - 1
                    pe.matmul(acc, hi[:, kc + k, tok], w_hi[:, slot, k, 0:cols], start=a, stop=False)
                    pe.matmul(acc, hi[:, kc + k, tok], w_lo[:, slot, k, 0:cols], start=False, stop=False)
                    mm = pe.matmul(acc, lo[:, kc + k, tok], w_hi[:, slot, k, 0:cols], start=False, stop=b)
                if last and t == 0:
                    mm.then_inc(sem("half_done"), 1)
            mm.then_inc(sem("unit_used"), 1)

        def chunk(u, n, hi, lo, kc, pair, cols=W, s0=0, between=(), free=None, before_last=None):
            for j in range(n):
                if before_last and j == n - 2:
                    before_last()
                unit(u + j, (s0 + j) % RING, hi, lo, kc + UR * j, pair, cols, j == 0, j == n - 1,
                     free if j == 0 else None)
                if j == 1:
                    for f in between:
                        f()

        def transposed(t, source, ready):
            for name, value in ready:
                wait(pe, sem(name), value)
            wait(pe, sem("tevac_v"), t.count())
            wait(pe, sem("tevac_s"), t.count())
            for q in range(4):
                for h in range(2):
                    tr = pe.transpose(ps[:, T_BANK + q // 2, 256 * (q % 2) + P * h:256 * (q % 2) + P * h + P],
                                      source(q, h), ident[:, :])
            tr.then_inc(sem("transposed"), 1)

        def first_chunk(k, u, src, ready, free, also=None):
            def pair(g):
                ready(g)
                wait(pe, sem(f"h_lo{k}"), 2 * (g - 3))
                for c in range(2):
                    for t in range(2):
                        kc = 2 * g + c
                        tr = pe.transpose(ps[:, 2 + g % 4, 256 * c + P * t:256 * c + P * t + P],
                                          src[:, t, kc * P:(kc + 1) * P], ident[:, :])
                tr.then_inc(sem(f"h_t{k}"), 1)

            pair(0)
            if k == 0:
                columns_transpose()
            pair(1)
            for j in range(CH):
                pe.wait_ge(sem(f"h_lo{k}"), 2 * j + 2)
                unit(u + j, j % RING, h_hi, h_lo, UR * j, 0, W, j == 0, j == CH - 1, free if j == 0 else None)
                if j + 2 < CH:
                    pair(j + 2)
                if also and j in also:
                    also[j]()
            pe.wait_ge(sem(f"h_lo{k}"), 2 * CH)

        def columns_transpose():
            pe.wait_ge(sem("columns_loaded"), 16 * 4)
            pe.transpose(ps[:, 7, 0:64], rows64[:, :], ident[0:64, 0:64]).then_inc(sem("columns_t"), 1)

        pe.wait_ge(sem("ident_loaded"), 16)

        def bias_table_product():
            pe.wait_ge(sem("const_loaded"), 16 * 6)
            pe.matmul(ps[0:48, 6, :], rel[:, :], onehot[:, :], start=True, stop=True).then_inc(sem("table_mm"), 1)

        def stage_tiles(slot):
            return lambda q, h: stage[:, slot, h, q * P:(q + 1) * P]

        def pair_free(name, n, i=0):
            per = 2 if name.startswith("qk") else 1
            return [[("evac_v", Pos(V0[name] + n, per, i).count())], [("evac_s", Pos(S0[name] + n, per, i).count())]]

        def tiles_out(t, slot, name, n, per=0, i=0):
            e, es = Pos(V0[name] + n, per, i), Pos(S0[name] + n, per, i)
            return lambda: transposed(t, stage_tiles(slot), [("evac_v", e.count()), ("evac_s", es.count())])

        def qk(name, i, between):
            chunk(Pos(U0[name], 2 * CH, i), CH, h_hi, h_lo, 0, 0, between=between, free=pair_free(name, -1, i))
            chunk(Pos(U0[name] + CH, 2 * CH, i), CH, h_hi, h_lo, 0, 1, free=pair_free(name, 0, i),
                  between=[tiles_out(Pos(T0[name], 2, i), 0, name, 1, 2, i)])

        def values(name, i, between=()):
            chunk(Pos(U0[name], CH, i), CH, h_hi, h_lo, 0, 0, between=between, free=pair_free(name, 0, i))

        def dup_tiles(first):
            return lambda q, h: dup[:, h, first + q, :, :].rearrange("p a n -> p (a n)")

        first_chunk(0, Pos(U0["qk_a"]), x_in, lambda g: pe.wait_ge(sem(f"x_loaded{g // 2}"), 16), None,
                    {3: bias_table_product})
        pe.wait_ge(sem("table_ready"), 1)
        pe.wait_ge(sem("columns_ready"), 1)
        chunk(Pos(U0["qk_a"] + CH), CH, h_hi, h_lo, 0, 1, between=[tiles_out(Pos(T0["qk_a"]), 0, "qk_a", 1)])
        with pe.Fori(1, 3) as i:
            qk("qk_a", i, [tiles_out(Pos(T0["qk_a"] - 1, 2, i), 1, "qk_a", 0, 2, i)])
        values("v_a", 0, [tiles_out(Pos(T0["v_a"] - 1), 1, "v_a", 0)])
        with pe.Fori(1, 3) as i:
            values("v_a", i)
        chunk(Pos(U0["q_b"]), CH, h_hi, h_lo, 0, 0, free=pair_free("q_b", 0))
        chunk(Pos(U0["q_b"] + CH), CH, h_hi, h_lo, 0, 1, free=pair_free("q_b", 0),
              between=[tiles_out(Pos(T0["q_b"]), 0, "q_b", 1)])
        chunk(Pos(U0["kv_b"]), CH, h_hi, h_lo, 0, 0, free=pair_free("kv_b", 0),
              between=[tiles_out(Pos(T0["q_b"] + 1), 1, "q_b", 2)])
        chunk(Pos(U0["kv_b"] + CH), CH, h_hi, h_lo, 0, 1, B_LAST, free=pair_free("kv_b", 0),
              between=[lambda: transposed(Pos(T0["kv_b"]), dup_tiles(0), [("dup_ready", 1)])])
        qk("qk_c", 0, [lambda: transposed(Pos(T0["kv_b"] + 1), dup_tiles(4), [("dup_ready", 2)])])
        qk("qk_c", 1, [tiles_out(Pos(T0["qk_c"] + 1), 1, "qk_c", 2)])
        values("v_c", 0, [tiles_out(Pos(T0["v_c"] - 1), 1, "v_c", 0)])
        values("v_c", 1)
        pe.wait_ge(sem("tevac_v"), T0["gate"])
        pe.wait_ge(sem("tevac_s"), T0["gate"])

        def maps(kind, i):
            it = FIRST_IT[kind]
            m0 = Pos(8 * it, 8, i)
            keys = {"a": k_a, "b": k_b, "c": k_c}[kind]
            ob0, ob_n = banks_before(kind)

            def scores(j):
                _, tile, _ = attn(kind, i, j)
                wait(pe, sem("query_ready"), (m0 + j).count(1))
                wait(pe, sem("logits_ready"), (m0 + j).count(-1))
                key = keys[:, bass.ds(tile, 1), :].rearrange("p a n -> p (a n)")
                pe.matmul(ps[:, 2 + j % 2, 0:P], q_pad[:, j % 4, 0:P], key[:, 0:P], start=True, stop=True)
                pe.matmul(ps[:, 2 + j % 2, P:3 * P], q_pad[:, j % 4, P:2 * P], key, start=True,
                          stop=True).then_inc(sem("scores_ready"), 1)

            def transposes(j):
                half = Pos(4 * it, 4, i) + j // 2
                wait(pe, sem("probs_ready"), (m0 + j).count(1))
                wait(pe, sem(f"pt_copied{j % 2}"), half.count())
                for b in range(3):
                    tr = pe.transpose(ps[:, 4 + j % 2, b * P:(b + 1) * P], logits[:, j % 4, b * P:(b + 1) * P],
                                      ident[:, :])
                tr.then_inc(sem("pt_ready"), 1)

            def outputs(j):
                half = Pos(4 * it, 4, i) + j // 2
                n, bank = bank_of(kind, j)
                wait(pe, sem(f"pt_copied{j % 2}"), half.count(1))
                if j == 0 or bank_of(kind, j - 1)[0] != n:
                    wait(pe, sem("o_taken"), (Pos(ob0, ob_n, i) + n).count(-1))
                if kind == "a":
                    at = j % 4
                    val = [v_a[:, s, bass.ds(i * 512 + 64 * j, 64)] for s in range(2)]
                elif kind == "b":
                    at = j % 4
                    val = [v_b[:, s, (j // 2) % 2, bass.ds((i // 2) * 64, 64)] for s in range(2)]
                else:
                    at = j % 2
                    val = [v_c[:, s, bass.ds(i * 512 + 128 * (j // 2), 128)] for s in range(2)]
                n_out = 128 if kind == "c" else 64
                o = [ps[:, bank, 256 * t + n_out * at:256 * t + n_out * at + n_out] for t in range(2)]
                pe.matmul(o[0], p_t[:, j % 2, 0:P], val[0], start=True, stop=True)
                pe.matmul(o[1], p_t[:, j % 2, P:2 * P], val[0], start=True, stop=False)
                pe.matmul(o[1], p_t[:, j % 2, 2 * P:3 * P], val[1], start=False, stop=True).then_inc(
                    sem("pv_done"), 1)

            u = Pos(U0["gate"] + CH * it, CH, i)
            for s in range(-1, CH):
                if s >= 0:
                    unit(u + s, s % RING, h_hi, h_lo, UR * s, 0, W, s == 0, s == CH - 1,
                         gates_free(Pos(it, 1, i)) if s == 0 else None)
                for j in range(8):
                    if SCORES_AT[j] + 1 == s:
                        transposes(j)
                for j in range(8):
                    if SCORES_AT[j] + 2 == s:
                        outputs(j)
                for j in range(8):
                    if SCORES_AT[j] == s:
                        scores(j)

        def gates_free(c):
            first = isinstance(c.count(), int) and c.count() == 0
            e = Pos(S0["gate"] + 2 * c.k, 2 * c.per, c.i)
            return [[("evac_v", V0["gate"])] if first else [("evac_s", e.count(-1))], [("evac_s", e.count())]]

        for kind, n in LOOPS:
            maps(kind, 0)
            with pe.Fori(1, n) as i:
                maps(kind, i)

        def compress_first(v):
            if v == 0:
                pe.wait_ge(sem("w1_loaded"), 2 * 4 * 16)
                pe.wait_ge(sem("blocks_ready"), 8)
            for c in range(KC):
                mm = pe.matmul(ps[0:2 * NCMP, 2 + v, 0:256], blocks_t[:, v, c, :], (w1k, w1v)[v][:, c, :],
                               start=c == 0, stop=c == KC - 1)
            mm.then_inc(sem("hidden_rows"), 1)

        def hidden_transposes():
            pe.wait_ge(sem("hidden_copied"), 1)
            for v in range(2):
                for hc in range(2):
                    at = 2 * NCMP * (2 * v + hc)
                    tr = pe.transpose(ps[:, 2, at:at + 2 * NCMP], hid_rows[:, v, hc * P:(hc + 1) * P],
                                      ident[0:2 * NCMP, 0:2 * NCMP])
            tr.then_inc(sem("hidden_mm"), 1)

        def compress2():
            pe.wait_ge(sem("w2_loaded"), 48)
            pe.wait_ge(sem("gelu_ready"), 3)
            for hc in range(2):
                pe.matmul(ps[:, 3, 0:30], w2k[:, hc, :, :].rearrange("p a n -> p (a n)"), hid_k[:, hc, :],
                          start=hc == 0, stop=hc == 1)
            for g in range(2):
                for hc in range(2):
                    mm = pe.matmul(ps[:, 3, 64 + 64 * g:128 + 64 * g],
                                   hid_v[:, hc, g, :, :].rearrange("p a n -> p (a n)"), w2v[:, hc, :],
                                   start=hc == 0, stop=hc == 1)
            mm.then_inc(sem("compressed_mm"), 1)

        def cmp_scores():
            pe.wait_ge(sem("compressed"), 1)
            pe.wait_ge(sem("o_split_lo"), 6)
            for t in range(2):
                for h in range(8):
                    mm = pe.matmul(ps[:, 4 + t, 2 * NCMP * h:2 * NCMP * (h + 1)], q_b[:, h, t * P:(t + 1) * P],
                                   kc_diag[:, h // 4, :, :].rearrange("p a n -> p (a n)"), start=True, stop=True)
            mm.then_inc(sem("cmp_scores"), 1)

        def cmp_transposes():
            pe.wait_ge(sem("cmp_probs"), 1)
            for n in range(8):
                t, q = n // 4, n % 4
                tr = pe.transpose(ps[:, 6 + n // 4, P * (n % 4):P * (n % 4) + P],
                                  cmp_p[:, t, 4 * q:4 * q + 4, :].rearrange("p a n -> p (a n)"), ident[:, :])
            tr.then_inc(sem("cmp_pt"), 1)

        def cmp_outputs():
            pe.wait_ge(sem("cmp_pt_copied"), 1)
            for n in range(8):
                t, q = n // 4, n % 4
                mm = pe.matmul(ps[:, 2 + 2 * t + q // 2, 256 * (q % 2):256 * (q % 2) + 256], cmp_pt[:, n, :],
                               vc_diag[:, q // 2, :, :].rearrange("p a n -> p (a n)"), start=True, stop=True)
            mm.then_inc(sem("cmp_pv"), 1)

        def output_transposes(q):
            g, bank = O_PAIRS[q], O_BANKS[q]
            pe.wait_ge(sem("a_summed" if g < 2 else "b_ready" if g < 6 else "c_ready"), 2 if g < 2 else 1)
            if bank in (6, 7):
                pe.wait_ge(sem("o_taken"), 22)
            before = [k for k in range(q) if O_BANKS[k] == bank]
            wait(pe, sem("o_split_lo"), before[-1] + 1 if before else 0)
            for c in range(2):
                b = 2 * g + c
                for t in range(2):
                    src = (o_a[:, 0, t, P * b:P * b + P] if b < 4 else
                           o_b[:, t, P * (b - 4):P * (b - 3)] if b < 12 else o_c[:, t, P * (b - 12):P * (b - 11)])
                    tr = pe.transpose(ps[:, bank, 256 * c + P * t:256 * c + P * t + P], src, ident[:, :])
            tr.then_inc(sem("o_transposed"), 1)

        pe_steps = {0: [lambda: compress_first(0)], 1: [lambda: compress_first(1)], 3: [hidden_transposes], 5: [compress2], 7: [cmp_scores], 11: [cmp_transposes],
                    13: [cmp_outputs]}
        for q, n in enumerate(O_AT):
            pe_steps.setdefault(n, []).append(lambda q=q: output_transposes(q))
        for n in range(NSTEP):
            c, s = divmod(n, CH)
            unit(Pos(U0["gate"] + 72 + n), s % RING, h_hi, h_lo, UR * s, 0, W, s == 0, s == CH - 1,
                 gates_free(Pos(9 + c)) if s == 0 else None)
            for f in pe_steps.get(n, ()):
                f()
        pe.wait_ge(sem("o_split_lo"), 10)
        pe.wait_ge(sem("evac_s"), S0["branch"])

        for n in range(4):
            for b in range(3):
                before = sum(BR_UNITS[:b])
                t = Pos(T0["branch"] + n - 1)
                between = [] if (n == 0 or b != 1) else [
                    lambda t=t, n=n: transposed(t, lambda q, h: br_stage[:, (n - 1) % 2, h, q * P:(q + 1) * P],
                                                [("merge_done", n)])]
                chunk(Pos(U0["branch"] + 10 * n + before), BR_UNITS[b], o_hi, o_lo, BR_KC[b], b,
                      s0=(10 * n + before) % RING, between=between,
                      free=[[("evac_v", V0["branch"] + 2 * (3 * n + b - 3) + 1 + h if n else 0)] for h in range(2)])

        def plain(name, i, n, hi, lo, between=(), before_last=None):
            if name.startswith("down") and isinstance(i, int):
                free = [[("evac_s", S0[name] - 3)], [("evac_s", S0[name] - 2)]]
            elif name == "out" and isinstance(i, int):
                free = [[("evac_v", V0[name] - 5)], [("evac_v", V0[name] - 4)]]
            elif name in ("out", "down1"):
                free = [[("evac_v", Pos(V0[name] + h, 2, i).count(-1))] for h in range(2)]
            else:
                free = [[("evac_v", Pos(V0[name], 1, i).count())], [("evac_s", Pos(S0[name], 1, i).count())]]
            chunk(Pos(U0[name], n, i), n, hi, lo, 0, 0, free=free, between=between, before_last=before_last)

        plain("out", 0, CH, h_hi, h_lo, [lambda: transposed(
            Pos(T0["branch"] + 3), lambda q, h: br_stage[:, 1, h, q * P:(q + 1) * P], [("merge_done", 4)])],
            before_last=lambda: pe.wait_ge(sem("tevac_v"), T0["out"]))
        with pe.Fori(1, 4) as i:
            plain("out", i, CH, h_hi, h_lo)
        def up_tiles(name, c, i):
            e = Pos(V0[name] + c + 1, 2, i)
            return lambda: transposed(Pos(T0[name] + c, 2, i), lambda q, h: up_stage[:, c % 2, h, q * P:(q + 1) * P],
                                      [("evac_v", e.count())])

        def up(name, i, between):
            for c in range(2):
                e = Pos(S0[name] + 2 * (c - 2), 4, i)
                free = [[("evac_s", e.count(1 + h))] for h in range(2)]
                if isinstance(i, int):
                    free = [[("evac_v", V0[name])], [("evac_s", S0[name])]] if c == 0 else None
                if name == "up0" and isinstance(i, int) and c == 0:
                    first_chunk(2, Pos(U0[name]), mid, lambda g: pe.wait_ge(sem("mid_ready"), 2 * (g // 2) + 2),
                                [[("evac_v", V0[name] - 1)], [("evac_v", V0[name])]])
                    continue
                chunk(Pos(U0[name] + CH * c, 2 * CH, i), CH, h_hi, h_lo, 0, c, free=free,
                      between=between if c == 0 else [up_tiles(name, 0, i)])

        for h in range(2):
            up(f"up{h}", 0, ())
            with pe.Fori(1, 4) as i:
                up(f"up{h}", i, [up_tiles(f"up{h}", -1, i)])
            plain(f"down{h}", 0, 16, u_hi, u_lo, [up_tiles(f"up{h}", -1, 4)],
                  before_last=lambda h=h: pe.wait_ge(sem("tevac_v"), T0[f"down{h}"]))
            with pe.Fori(1, 4) as i:
                plain(f"down{h}", i, 16, u_hi, u_lo)
        pe.wait_ge(sem("unit_used"), UNITS)

    @block.scalar
    def _(act):
        act_count = act.alloc_register("act_count")

        def split(u, slot):
            if isinstance(u.count(), int) and u.count() >= UNITS:
                return
            act.wait_ge(sem(f"raw_loaded{slot}"), u.loads())
            wait(act, sem("unit_used"), u.count(1 - RING))
            act.activation(w_hi[:, slot, :, :], raw[:, slot, :, :], ACT.Copy).then_inc(sem("hi_ready"), 1)

        def chunk(u, n, s0=0, after=None, early=None):
            for j in range(n):
                if early and j == n - 1:
                    early()
                split(u + (j + LEAD), (s0 + j + LEAD) % RING)
                for f in (after or {}).get(j, ()):
                    f()

        def copy_out(dst, pair, e, scale=None):
            u_done, count = e
            act.wait_ge(sem("unit_used"), u_done)
            act.activation(dst, ps[:, 2 * pair + 1, 0:dst.shape[-1]], ACT.Copy,
                           scale=1.0 if scale is None else scale).then_inc(sem("evac_s"), 1)

        def t_out(t, dst):
            act.wait_ge(sem("transposed"), t.count(1))
            act.activation(dst, ps[:, T_BANK + 1, :].rearrange("p (a n) -> p a n", a=2), ACT.Copy).then_inc(
                sem("tevac_s"), 1)

        def t_split(t, dst):
            act.wait_ge(sem("transposed"), t.count(1))
            act.activation(dst, ps[:, T_BANK:T_BANK + 2, :].rearrange("p b (a n) -> p (b a) n", a=2), ACT.Copy
                           ).then_inc(sem("tevac_s"), 1)

        def square(k, t, b, src):
            return act.activation(squares[:, :], src, ACT.Square, accum_out=ssq_parts[:, k, t, b])

        def root_step(k):
            act.wait_ge(sem(f"rstd_steps{k}"), 2)
            act.activation(root[:, k, :], mean[:, k, :], ACT.Sqrt).then_inc(sem(f"root{k}"), 1)

        def first_chunk(k, u, src, ready):
            def pair(g):
                act.wait_ge(sem(f"h_t{k}"), g + 1)
                for c in range(2):
                    kc = 2 * g + c
                    act.activation(h_hi[:, kc, :], ps[:, 2 + g % 4, 256 * c:256 * c + 256], ACT.Copy,
                                   scale=columns[:, 8 * k + kc:8 * k + kc + 1]).then_inc(sem(f"h_hi{k}"), 1)

            if k == 0:
                split(Pos(0), 0)
                act.wait_ge(sem("columns_ready"), 1)
            for g in range(2):
                pair(g)
            if k == 0:
                split(Pos(1), 1)
                split(Pos(2), 2)
            for j in range(CH):
                split(u + (j + LEAD), (j + LEAD) % RING)
                if j + 2 < CH:
                    pair(j + 2)
                t, b = j % 2, j // 2
                ready(b)
                wait(act, sem(f"squared{k}"), j)
                square(k, t, slice(b, b + 1), src[:, t, W * b:W * b + W]).then_inc(sem(f"squared{k}"), 1)
            root_step(k)

        for dst, src in ((rows64[0:16, :], norm_mix_pre.rearrange("l (c p) -> (l c) p", p=P)),
                         (rows64[16:32, :], norm_mlp_pre.rearrange("l (c p) -> (l c) p", p=P)),
                         (rows64[32:48, :], cmp_k_pos.rearrange("l (c a) d -> (l c) (a d)", a=2)),
                         (rows64[48:64, :], cmp_v_pos.rearrange("l (c a) d -> (l c) (a d)", a=2))):
            act.dma_start(dst, src).then_inc(sem("columns_loaded"), 16)
        act.wait_ge(sem("ident_loaded"), 16)
        act.activation(root[:, 1, :], ident[:, 0:2], ACT.Sqrt).then_inc(sem("root_table"), 1)
        first_chunk(0, Pos(U0["qk_a"]), x_in, lambda b: act.wait_ge(sem(f"x_loaded{b}"), 16))
        act.wait_ge(sem("rstd_ready0"), 2)
        rstd_s = rstd[:, 0, 1:2]

        def tiles(t, dst, first):
            return {2: [lambda: t_out(t, dst[:, bass.ds(first + 2, 2), :])]}

        def qk(name, i, q_dst, k_dst, after):
            u = Pos(U0[name], 2 * CH, i)
            if after is not FIRST:
                chunk(u, CH, after=after)
            copy_out(stage[:, 0, 1, :], 0, (u.count(CH), 1), rstd_q[:, 1:2])
            chunk(u + CH, CH, after=tiles(Pos(T0[name], 2, i), q_dst, i * 4))
            copy_out(stage[:, 1, 1, :], 1, (u.count(2 * CH), 1), rstd_s)

        def values(name, i, dst, after=None):
            u = Pos(U0[name], CH, i)
            chunk(u, CH, after=after)
            copy_out(dst[:, 1, bass.ds(i * W, W)], 0, (u.count(CH), 1), rstd_s)

        qk("qk_a", 0, q_a, k_a, FIRST)
        act.wait_ge(sem("lam_steps"), 2)
        act.activation(lam2[:, 2:4], lam2[:, 0:2], ACT.Exp).then_inc(sem("lam_exp"), 1)
        with act.Fori(1, 3) as i:
            qk("qk_a", i, q_a, k_a, tiles(Pos(T0["qk_a"] - 1, 2, i), k_a, i * 4 - 4))
        values("v_a", 0, v_a, tiles(Pos(T0["v_a"] - 1), k_a, 8))
        with act.Fori(1, 3) as i:
            values("v_a", i, v_a)
        u, t = Pos(U0["q_b"]), Pos(T0["q_b"])
        chunk(u, CH)
        copy_out(stage[:, 0, 1, :], 0, (u.count(CH), 1), rstd_q[:, 1:2])
        chunk(u + CH, CH, after=tiles(t, q_b, 0))
        copy_out(stage[:, 1, 1, :], 1, (u.count(2 * CH), 1), rstd_q[:, 1:2])
        u2, t2 = Pos(U0["kv_b"]), Pos(T0["kv_b"])
        chunk(u2, CH, after=tiles(t + 1, q_b, 4))
        copy_out(stage[:, 0, 1, :], 0, (u2.count(CH), 1), rstd_s)
        chunk(u2 + CH, CH, after=tiles(t2, cmp_t, 0))
        copy_out(stage[:, 1, 1, 0:B_LAST], 1, (u2.count(2 * CH), 1), rstd_s)
        act.wait_ge(sem("bgate_steps"), 1)
        act.activation(head_gates[:, :, :, :], head_gates[:, :, :, :], ACT.Exp, scale=-1.0).then_inc(sem("bgate_exp"), 1)
        qk("qk_c", 0, q_c, k_c, tiles(t2 + 1, k_b, 0))
        qk("qk_c", 1, q_c, k_c, tiles(Pos(T0["qk_c"] + 1), k_c, 0))
        values("v_c", 0, v_c, tiles(Pos(T0["v_c"] - 1), k_c, 4))
        values("v_c", 1, v_c)

        def gate_exp(c, h):
            if h == 0:
                stored = held(act, act_count, c * 16)
                act.wait_ge(sem("half_done"), Pos(C0["gate"] + 1, 1, c).count())
                wait(act, sem("gates_stored"), stored)
            else:
                act.wait_ge(sem("unit_used"), Pos(U0["gate"] + CH, CH, c).count())
            act.activation(stage[:, 0, h, :], ps[:, h, :], ACT.Exp, scale=rstd_neg[:, h:h + 1]).then_inc(
                sem("evac_s"), 1)

        def maps(kind, i, extra=None):
            it = FIRST_IT[kind]
            m0 = Pos(8 * it, 8, i)
            u = Pos(U0["gate"] + CH * it, CH, i)

            def exps(j):
                wait(act, sem("logits_ready"), (m0 + j).count(1))
                if isinstance(i, int) and i == 0:
                    prev = {"a": None, "c": ("a", 2), "b": ("c", 1)}[kind]
                    if prev is not None:
                        n0, n1 = banks_before(prev[0])
                        wait(act, sem("o_taken"), n0 + n1 * prev[1] + bank_of(prev[0], j)[0] + 1)
                else:
                    n0, n1 = banks_before(kind)
                    wait(act, sem("o_taken"), (Pos(n0 - n1, n1, i) + (bank_of(kind, j)[0] + 1)).count())
                for t in range(2):
                    part = logits[:, j % 4, 0:P] if t == 0 else logits[:, j % 4, P:3 * P]
                    e = act.activation(part, part, ACT.Exp, bias=negmax[:, t, j:j + 1], scale=-1.0,
                                       accum_out=sums[:, t, j:j + 1])
                e.then_inc(sem("probs_ready"), 1)

            def pt_copy(j):
                half = Pos(4 * it, 4, i) + j // 2
                act.wait_ge(sem("pt_ready"), (m0 + j).count(1))
                wait(act, sem("pv_done"), (m0 + j).count(-1))
                act.activation(p_t[:, 1, :], ps[:, 5, 0:384], ACT.Copy).then_inc(sem("pt_copied1"), 1)

            for s in range(-1, CH):
                if s == CH - 1:
                    gate_exp(i + it, 0)
                if s >= 0:
                    split(u + (s + LEAD), (s + LEAD) % RING)
                for j in range(1, 8, 2):
                    if SCORES_AT[j] + 1 == s:
                        pt_copy(j)
                for j in range(8):
                    if SCORES_AT[j] == s:
                        exps(j)
                for f in (extra or {}).get(s, ()):
                    f()
            gate_exp(i + it, 1)

        def gelu_exp():
            act.wait_ge(sem("gelu_steps"), 5)
            act.activation(hid[:, 2, :], hid[:, 1, :], ACT.Exp, scale=-2.0 * math.sqrt(2.0 / math.pi)).then_inc(
                sem("gelu_exp"), 1)

        def a_exp():
            act.wait_ge(sem("a_steps"), 2)
            act.activation(a_w[:, :, :], a_w[:, :, :], ACT.Exp, scale=-1.0).then_inc(sem("a_exp"), 1)

        def c_root_step():
            act.wait_ge(sem("c_steps"), 5)
            act.activation(c_root[:, :, :], c_mean[:, :, :], ACT.Sqrt).then_inc(sem("c_root"), 1)

        def cmp_exp():
            act.wait_ge(sem("cmp_steps"), 4)
            act.activation(cmp_l[:, :, :, :], cmp_l[:, :, :, :], ACT.Exp).then_inc(sem("cmp_exp"), 1)

        between_maps = {"c": {2: [a_exp]}}
        for kind, n in LOOPS:
            maps(kind, 0, between_maps.get(kind))
            with act.Fori(1, n) as i:
                maps(kind, i)

        def o_split(q):
            g, bank = O_PAIRS[q], O_BANKS[q]
            act.wait_ge(sem("o_transposed"), q + 1)
            act.activation(o_hi[:, 2 * g:2 * g + 2, :], ps[:, bank, :].rearrange("p (a n) -> p a n", a=2),
                           ACT.Copy).then_inc(sem("o_split_hi"), 1)

        act_steps = {0: [c_root_step], 4: [gelu_exp], 9: [cmp_exp]}
        for q, n in enumerate(O_AT):
            act_steps.setdefault(n + 1, []).append(lambda q=q: o_split(q))
        for n in range(NSTEP):
            c, s = divmod(n, CH)
            if s == CH - 1:
                gate_exp(9 + c, 0)
            split(Pos(U0["gate"] + 72 + n + LEAD), (s + LEAD) % RING)
            for f in act_steps.get(n, ()):
                f()
            if s == CH - 1:
                gate_exp(9 + c, 1)

        for n in range(4):
            chunk(Pos(U0["branch"] + 10 * n), 10, s0=(10 * n) % RING, after={5: [] if n == 0 else [
                lambda n=n: t_split(Pos(T0["branch"] + n - 1), h_hi[:, 4 * (n - 1):4 * n, :])]})

        def product_squares(name, k, i):
            for t in range(2):
                if k == 1:
                    if t == 0:
                        act.wait_ge(sem("half_done"), Pos(C0[name], 1, i).count(1))
                    else:
                        act.wait_ge(sem("unit_used"), Pos(U0[name], CH, i).count(CH))
                    src = ps[:, t, :]
                else:
                    act.wait_ge(sem("evac_v"), Pos(V0[name] + t + 1, 2, i).count())
                    src = y[:, t, bass.ds(i * W, W)]
                act.wait_ge(sem("evac_s"), Pos(S0[name] + t, 2, i).count())
                square(k, t, bass.ds(i, 1), src).then_inc(sem("evac_s"), 1)

        def out_chunk(i):
            chunk(Pos(U0["out"], CH, i), CH, early=lambda: product_squares("out", 1, i),
                  after={2: [lambda: t_split(Pos(T0["out"] - 1), h_hi[:, 12:16, :])]}
                  if isinstance(i, int) and i == 0 else None)

        out_chunk(0)
        act.activation(root[:, 0, :], mean[:, 0, :], ACT.Sqrt).then_inc(sem("root_table"), 1)
        with act.Fori(1, 4) as i:
            out_chunk(i)
        root_step(1)
        first_chunk(2, Pos(U0["up0"]), mid, lambda b: act.wait_ge(sem("mid_ready"), 2 * b + 2))
        act.wait_ge(sem("rstd_steps2"), 7)

        def up(name, i, h):
            u, t = Pos(U0[name], 2 * CH, i), Pos(T0[name], 2, i)

            def relu(c):
                act.wait_ge(sem("half_done"), Pos(C0[name] + c + 1, 2, i).count())
                act.activation(up_stage[:, c, 0, :], ps[:, 2 * c, :], ACT.Relu, scale=rstd[:, 2, 0:1]).then_inc(sem("evac_s"), 1)
                act.wait_ge(sem("unit_used"), (u + CH * (c + 1)).count())
                act.activation(up_stage[:, c, 1, :], ps[:, 2 * c + 1, :], ACT.Relu, scale=rstd[:, 2, 1:2]).then_inc(sem("evac_s"), 1)

            if not (name == "up0" and isinstance(i, int)):
                chunk(u, CH, after={2: [lambda: t_split(t + (-1), u_hi[:, bass.ds(i * 8 - 4, 4), :])]}
                      if not isinstance(i, int) else None)
            relu(0)
            chunk(u + CH, CH, after={2: [lambda: t_split(t, u_hi[:, bass.ds(i * 8, 4), :])]})
            relu(1)

        def down(h, i):
            u = Pos(U0[f"down{h}"], 16, i)
            chunk(u, 16, after={2: [lambda: t_split(Pos(T0[f"down{h}"] - 1), u_hi[:, 28:32, :])]} 
                  if isinstance(i, int) and i == 0 else None)
            if h == 0:
                act.wait_ge(sem("unit_used"), u.count(16))
                act.activation(y[:, 1, bass.ds(i * W, W)], ps[:, 1, :], ACT.Copy).then_inc(sem("evac_s"), 1)
            else:
                product_squares("down1", 3, i)

        for h in range(2):
            up(f"up{h}", 0, h)
            with act.Fori(1, 4) as i:
                up(f"up{h}", i, h)
            down(h, 0)
            with act.Fori(1, 4 - h) as i:
                down(h, i)
            if h == 1:
                down(h, 3)
        root_step(3)

    @block.vector
    def _(dve):
        dve_count = dve.alloc_register("dve_count")

        def split(u, slot):
            if isinstance(u.count(), int) and u.count() >= UNITS:
                return
            dve.wait_ge(sem("hi_ready"), u.count(1))
            wait(dve, sem("unit_used"), u.count(1 - RING))
            dve.tensor_tensor(w_lo[:, slot, :, :], raw[:, slot, :, :], w_hi[:, slot, :, :].bitcast(F32),
                              ALU.subtract).then_inc(sem("lo_ready"), 1)

        def chunk(u, n, s0=0, after=None, early=None):
            for j in range(n):
                if early and j == n - 1:
                    early()
                split(u + (j + LEAD), (s0 + j + LEAD) % RING)
                for f in (after or {}).get(j, ()):
                    f()

        def copy_out(dst, pair, half_done, scale=None):
            dve.wait_ge(sem("half_done"), half_done)
            src = ps[:, 2 * pair, 0:dst.shape[-1]]
            if scale is None:
                dve.tensor_copy(dst, src).then_inc(sem("evac_v"), 1)
            else:
                dve.tensor_scalar(dst, src, scale, None, ALU.mult).then_inc(sem("evac_v"), 1)

        def t_out(t, dst):
            dve.wait_ge(sem("transposed"), t.count(1))
            dve.tensor_copy(dst, ps[:, T_BANK, :].rearrange("p (a n) -> p a n", a=2)).then_inc(sem("tevac_v"), 1)

        def t_split(t, dst, hi):
            dve.wait_ge(sem("tevac_s"), t.count(1))
            dve.tensor_tensor(dst, ps[:, T_BANK:T_BANK + 2, :].rearrange("p b (a n) -> p (b a) n", a=2),
                              hi.bitcast(F32), ALU.subtract).then_inc(sem("tevac_v"), 1)

        def chain(name, ops):
            s = sem(name)
            for op in ops:
                done[name] = done.get(name, 0) + 1
                op().then_inc(s, 1)
                dve.wait_ge(s, done[name])

        done = {}

        def rstd_first(k, name, value):
            dve.wait_ge(sem(name), value)
            chain(f"rstd_steps{k}", [
                lambda: dve.tensor_reduce(ssq[:, k, :], ssq_parts[:, k, :, :], AX, ALU.add),
                lambda: dve.tensor_scalar(mean[:, k, :], ssq[:, k, :], 1.0 / D, EPS, ALU.mult, ALU.add)])

        def rstd_second(k):
            dve.wait_ge(sem(f"root{k}"), 1)
            a, b, c, n = inv[:, k, :], newton[:, k, :], rstd[:, k, :], mean[:, k, :]
            chain(f"rstd_steps{k}", [
                lambda: dve.reciprocal(a, root[:, k, :]),
                lambda: dve.tensor_tensor(b, a, a, ALU.mult),
                lambda: dve.tensor_tensor(b, b, n, ALU.mult),
                lambda: dve.tensor_scalar(b, b, -0.5, 1.5, ALU.mult, ALU.add),
                lambda: dve.tensor_tensor(c, a, b, ALU.mult)])

        def first_chunk(k, u, also):
            def pair(g):
                dve.wait_ge(sem(f"h_hi{k}"), 2 * g + 2)
                for c in range(2):
                    kc = 2 * g + c
                    dve.scalar_tensor_tensor(h_lo[:, kc, :], ps[:, 2 + g % 4, 256 * c:256 * c + 256],
                                             columns[:, 8 * k + kc:8 * k + kc + 1], h_hi[:, kc, :].bitcast(F32),
                                             ALU.mult, ALU.subtract).then_inc(sem(f"h_lo{k}"), 1)

            if k == 0:
                split(Pos(0), 0)
            for g in range(2):
                pair(g)
            if k == 0:
                split(Pos(1), 1)
                split(Pos(2), 2)
            for j in range(CH):
                split(u + (j + LEAD), (j + LEAD) % RING)
                if j + 2 < CH:
                    if j in also:
                        also[j]()
                    pair(j + 2)
            rstd_first(k, f"squared{k}", 8)
            rstd_second(k)

        dve.wait_ge(sem("columns_t"), 1)
        dve.tensor_copy(columns[:, :], ps[:, 7, 0:64]).then_inc(sem("columns_ready"), 1)
        dve.wait_ge(sem("columns_ready"), 1)

        def make_table():
            dve.wait_ge(sem("table_mm"), 1)
            dve.tensor_tensor(table[:, :], ps[0:48, 6, :], dmask[:, :], ALU.add).then_inc(sem("table_ready"), 1)

        first_chunk(0, Pos(U0["qk_a"]), {5: make_table})
        dve.tensor_scalar(rstd_q[:, :], rstd[:, 0, :], SCALE, None, ALU.mult).then_inc(sem("rstd_ready0"), 1)
        dve.tensor_scalar(rstd_neg[:, :], rstd[:, 0, :], -1.0, None, ALU.mult).then_inc(sem("rstd_ready0"), 1)
        for n in range(2):
            dve.tensor_tensor_reduce(lam_prod[:, n, :], lam_rows[:, 2 * n, :], lam_rows[:, 2 * n + 1, :], 1.0, 0.0,
                                     ALU.mult, ALU.add, lam2[:, n:n + 1]).then_inc(sem("lam_steps"), 1)
        dve.wait_ge(sem("rstd_ready0"), 2)
        rstd_v = rstd[:, 0, 0:1]

        def tiles(t, dst, first):
            return {2: [lambda: t_out(t, dst[:, bass.ds(first, 2), :])]}

        def qk(name, i, q_dst, k_dst, after):
            u = Pos(U0[name], 2 * CH, i)
            c = Pos(C0[name], 2, i)
            if after is not FIRST:
                chunk(u, CH, after=after)
            copy_out(stage[:, 0, 0, :], 0, c.count(1), rstd_q[:, 0:1])
            chunk(u + CH, CH, after=tiles(Pos(T0[name], 2, i), q_dst, i * 4))
            copy_out(stage[:, 1, 0, :], 1, c.count(2), rstd_v)

        def values(name, i, dst, after=None):
            chunk(Pos(U0[name], CH, i), CH, after=after, early=lambda: copy_out(
                dst[:, 0, bass.ds(i * W, W)], 0, Pos(C0[name], 1, i).count(1), rstd_v))

        qk("qk_a", 0, q_a, k_a, FIRST)
        dve.wait_ge(sem("lam_exp"), 1)
        dve.scalar_tensor_tensor(neg_lam[:, :], lam2[:, 3:4], -LAM_INIT, lam2[:, 2:3], ALU.add, ALU.subtract).then_inc(
            sem("neg_lam"), 1)
        with dve.Fori(1, 3) as i:
            qk("qk_a", i, q_a, k_a, tiles(Pos(T0["qk_a"] - 1, 2, i), k_a, i * 4 - 4))
        values("v_a", 0, v_a, tiles(Pos(T0["v_a"] - 1), k_a, 8))
        with dve.Fori(1, 3) as i:
            values("v_a", i, v_a)
        u, t = Pos(U0["q_b"]), Pos(T0["q_b"])
        chunk(u, CH)
        copy_out(stage[:, 0, 0, :], 0, C0["q_b"] + 1, rstd_q[:, 0:1])
        chunk(u + CH, CH, after=tiles(t, q_b, 0))
        copy_out(stage[:, 1, 0, :], 1, C0["q_b"] + 2, rstd_q[:, 0:1])

        u2, t2 = Pos(U0["kv_b"]), Pos(T0["kv_b"])

        def double(slot, cols, first, wait_for=True):
            dve.wait_ge(sem("evac_v"), V0["kv_b"] + 1 + slot)
            dve.wait_ge(sem("evac_s"), S0["kv_b"] + 1 + slot)
            for h in range(2):
                for a in range(2):
                    last = dve.tensor_copy(dup[:, h, first:first + cols // HD, a, :],
                                           stage[:, slot, h, 0:cols].rearrange("p (q n) -> p q n", n=HD)
                                           if first != 4 else
                                           stage[:, slot, h, 256:256 + cols].rearrange("p (q n) -> p q n", n=HD))
            return last

        chunk(u2, CH, after=tiles(t + 1, q_b, 4))
        copy_out(stage[:, 0, 0, :], 0, C0["kv_b"] + 1, rstd_v)
        dve.wait_ge(sem("table_stored"), 16)
        double(0, 256, 0).then_inc(sem("dup_ready"), 1)
        double(0, 128, 4)
        dve.tensor_copy(v_b[:, :, 0, :], stage[:, 0, :, 384:512]).then_inc(sem("v_b_copied"), 1)
        chunk(u2 + CH, CH, after=tiles(t2, cmp_t, 0))
        copy_out(stage[:, 1, 0, 0:B_LAST], 1, C0["kv_b"] + 2, rstd_v)
        double(1, 128, 6).then_inc(sem("dup_ready"), 1)
        dve.tensor_copy(v_b[:, :, 1, :], stage[:, 1, :, 128:256]).then_inc(sem("v_b_copied"), 1)
        for h in range(2):
            last = dve.tensor_copy(head_gates[:, h, :, :], stage[:, 1, h, 256:304].rearrange("p (h b) -> p b h", b=3))
        last.then_inc(sem("bgate_steps"), 1)
        dve.wait_ge(sem("bgate_exp"), 1)
        done["bgate_steps"] = 1
        chain("bgate_steps", [
            lambda: dve.tensor_scalar(head_gates[:, :, :, :], head_gates[:, :, :, :], 1.0, None, ALU.add),
            lambda: dve.reciprocal(head_gates[:, :, :, :], head_gates[:, :, :, :])])
        qk("qk_c", 0, q_c, k_c, tiles(t2 + 1, k_b, 0))
        qk("qk_c", 1, q_c, k_c, tiles(Pos(T0["qk_c"] + 1), k_c, 0))
        values("v_c", 0, v_c, tiles(Pos(T0["v_c"] - 1), k_c, 4))
        values("v_c", 1, v_c)

        def gate_plus(c):
            dve.wait_ge(sem("evac_s"), Pos(S0["gate"] + 2, 2, c).count())
            dve.tensor_scalar(stage[:, 0, :, :], stage[:, 0, :, :], 1.0, None, ALU.add).then_inc(sem("gate_plus1"), 1)

        gates_flat = stage[:, 0, :, :].rearrange("p t n -> p (t n)")

        def gate_part(c, s):
            if s == 0:
                gate_plus(c)
            if s not in GATE_PARTS:
                return
            first, last = GATE_PARTS[s]
            if first == 0:
                dve.wait_ge(sem("gate_plus1"), Pos(1, 1, c).count())
            part = dve.reciprocal(gates_flat[:, first:last], gates_flat[:, first:last])
            if last == 2 * W:
                part.then_inc(sem("gates_made"), 1)

        def blocks():
            for v in range(2):
                for g in range(2):
                    for par in range(2):
                        half = slice(64 * par, 64 * par + 64)
                        t = cmp_t[half, 2 * v + g, :]
                        src = bass.AP(t.tensor, t.offset + par, [list(t.ap[0]), [2, KC], [CSTRIDE, NCMP]])
                        pos = columns[half, 32 + 16 * v:48 + 16 * v].rearrange("p (c a) -> p c a", a=1)
                        dve.tensor_tensor(blocks_t[half, v, :, NCMP * g:NCMP * g + NCMP], src,
                                          pos.to_broadcast([64, KC, NCMP]), ALU.add).then_inc(sem("blocks_ready"), 1)

        dve.wait_ge(sem("tevac_s"), T0["gate"])
        dve.wait_ge(sem("tevac_v"), T0["gate"])
        blocks()

        def maps(kind, i, extra=None):
            it = FIRST_IT[kind]
            m0 = Pos(8 * it, 8, i)
            u = Pos(U0["gate"] + CH * it, CH, i)
            ob0, ob_n = banks_before(kind)

            def add_bias(j):
                wait(dve, sem("scores_ready"), (m0 + j).count(1))
                loads = Pos(2 * it + j // 4 + 1, 2, i)
                dve.wait_ge(sem(f"bias_loaded{j % 4}"), Pos(16 * loads.k, 32, i).count())
                transposed_before = held(dve, dve_count, (m0 + j).count(-3))
                dve.wait_ge(sem("table_ready"), 1)
                wait(dve, sem("pt_ready"), transposed_before)
                dve.tensor_tensor_reduce(logits[:, j % 4, 0:P], ps[:, 2 + j % 2, 0:P], bias[:, j % 4, P - 1::-1], -1.0,
                                         3.0e38, ALU.add, ALU.min, negmax[:, 0, j:j + 1])
                dve.tensor_tensor_reduce(logits[:, j % 4, P:3 * P], ps[:, 2 + j % 2, P:3 * P], bias[:, j % 4, ::-1],
                                         -1.0, 3.0e38, ALU.add, ALU.min, negmax[:, 1, j:j + 1]).then_inc(
                    sem("logits_ready"), 1)

            def pt_copy(j):
                dve.wait_ge(sem("pt_ready"), (m0 + j).count(1))
                wait(dve, sem("pv_done"), (m0 + j).count(-1))
                dve.tensor_copy(p_t[:, 0, :], ps[:, 4, 0:384]).then_inc(sem("pt_copied0"), 1)

            def take(j):
                n, bank = bank_of(kind, j)
                dve.wait_ge(sem("pv_done"), (m0 + j).count(1))
                if kind == "a":
                    dve.tensor_copy(o_a[:, bass.ds(i, 1), :, 256 * n:256 * n + 256].rearrange("p a t n -> p (a t) n"),
                                    ps[:, bank, :].rearrange("p (t n) -> p t n", t=2))
                    dve.tensor_copy(a_negmax[:, :, bass.ds(i * 8 + 4 * n, 4)], negmax[:, :, 4 * n:4 * n + 4])
                    dve.tensor_copy(a_sums[:, :, bass.ds(i * 8 + 4 * n, 4)], sums[:, :, 4 * n:4 * n + 4]).then_inc(
                        sem("o_taken"), 1)
                    return
                steps = Pos(24, 6, i) + 3 * n if kind == "b" else Pos(0, 12, i) + 3 * n
                s = sem("take_steps")
                if kind == "b":
                    cf = coef[:, :, 0:4]
                    dve.reciprocal(rsum[:, :, :], sums[:, :, 4 * n:4 * n + 4]).then_inc(s, 1)
                    dve.wait_ge(s, steps.count(1))
                    dve.tensor_tensor(
                        coef[:, :, :].rearrange("p t (b h) -> p t b h", b=2),
                        rsum[:, :, :].rearrange("p t (b h) -> p t b h", b=2),
                        head_gates[:, :, 1:3, bass.ds(i * 4 + 2 * n, 2)], ALU.mult).then_inc(s, 1)
                    width, dst = 64, o_b[:, :, bass.ds(i * 256 + 128 * n, 128)]
                else:
                    cf = coef[:, :, 0:2]
                    dve.reciprocal(coef[:, :, 0:2], sums[:, :, 2 * n:2 * n + 2]).then_inc(s, 1)
                    dve.wait_ge(s, steps.count(1))
                    dve.tensor_scalar(coef[:, :, 1:2], coef[:, :, 1:2], neg_lam[:, 0:1], None, ALU.mult).then_inc(s, 1)
                    width, dst = 128, o_c[:, :, bass.ds(i * 512 + 128 * n, 128)]
                dve.wait_ge(s, steps.count(2))
                k = 256 // width
                dve.tensor_tensor(merged[:, :, :, :].rearrange("p t b n -> p t (b n)").rearrange(
                    "p t (k n) -> p t k n", k=k), ps[:, bank, :].rearrange("p (t k n) -> p t k n", t=2, k=k),
                    cf.rearrange("p t (k a) -> p t k a", a=1).to_broadcast([P, 2, k, width]), ALU.mult).then_inc(s, 1)
                dve.wait_ge(s, steps.count(3))
                dve.tensor_tensor(dst, merged[:, :, 0, :], merged[:, :, 1, :], ALU.add).then_inc(sem("o_taken"), 1)

            ends = bank_last(kind)
            wait(dve, sem("o_taken"), Pos(ob0, ob_n, i).count())
            before = i + (it - 1)
            for s in range(-1, CH):
                if s >= 0:
                    split(u + (s + LEAD), (s + LEAD) % RING)
                for j in range(0, 8, 2):
                    if SCORES_AT[j] + 1 == s:
                        pt_copy(j)
                for j in range(8):
                    if SCORES_AT[j] == s:
                        add_bias(j)
                for j in ends:
                    if SCORES_AT[j] + 3 == s:
                        take(j)
                if s >= 0 and not (isinstance(before, int) and before < 0):
                    gate_part(before, s)
                for f in (extra or {}).get(s, ()):
                    f()
            for j in ends:
                if SCORES_AT[j] + 3 >= CH:
                    take(j)

        def a_first():
            dve.wait_ge(sem("o_taken"), 6)
            w = a_w[:, :, :].rearrange("p t (g h) -> p t g h", g=3)
            chain("a_steps", [
                lambda: dve.tensor_reduce(a_min[:, :, :], a_negmax[:, :, :].rearrange("p t (g h) -> p t h g", g=3), AX,
                                          ALU.min),
                lambda: dve.tensor_tensor(w, a_negmax[:, :, :].rearrange("p t (g h) -> p t g h", g=3),
                                          a_min[:, :, :].rearrange("p t (a h) -> p t a h", a=1).to_broadcast(
                                              [P, 2, 3, 8]), ALU.subtract)])

        def a_second():
            dve.wait_ge(sem("a_exp"), 1)
            w = a_w[:, :, :].rearrange("p t (g h) -> p t g h", g=3)
            ops = [
                lambda: dve.tensor_tensor(a_ws[:, :, :], a_w[:, :, :], a_sums[:, :, :], ALU.mult),
                lambda: dve.tensor_reduce(a_tot[:, :, :], a_ws[:, :, :].rearrange("p t (g h) -> p t h g", g=3), AX,
                                          ALU.add),
                lambda: dve.reciprocal(a_tot[:, :, :], a_tot[:, :, :]),
                lambda: dve.tensor_tensor(w, w, a_tot[:, :, :].rearrange("p t (a h) -> p t a h", a=1).to_broadcast(
                    [P, 2, 3, 8]), ALU.mult)]

            chain("a_steps", ops)

        def a_scale(g):
            o = o_a[:, g, :, :].rearrange("p t (h n) -> p t h n", n=HD)
            chain("a_steps", [lambda: dve.tensor_tensor(o, o, a_w[:, :, 8 * g:8 * g + 8].rearrange(
                "p t (h a) -> p t h a", a=1).to_broadcast([P, 2, 8, HD]), ALU.mult)])

        def a_sum(g):
            add = dve.tensor_tensor(o_a[:, 0, :, :], o_a[:, 0, :, :], o_a[:, g, :, :], ALU.add)
            add.then_inc(sem("a_summed"), 1)
            dve.wait_ge(sem("a_summed"), g)

        c_heads = o_c[:, :, :].rearrange("p t (h n) -> p (t h) n", n=P)

        def c_squares(t):
            dve.wait_ge(sem("o_taken"), 14)
            chain("c_steps", [lambda: dve.tensor_tensor(c_square[:, :, :], c_heads[:, 8 * t:8 * t + 8, :],
                                                        c_heads[:, 8 * t:8 * t + 8, :], ALU.mult)])

        def c_sums(t):
            chain("c_steps", [lambda: dve.tensor_reduce(c_ssq[:, t, :], c_square[:, :, :], AX, ALU.add)])
            if t == 1:
                chain("c_steps", [lambda: dve.tensor_scalar(c_mean[:, :, :], c_ssq[:, :, :], 1.0 / P, EPS, ALU.mult,
                                                            ALU.add)])

        def c_second():
            dve.wait_ge(sem("c_root"), 1)
            flat = lambda a: a[:, :, :].rearrange("p t h -> p (t h)")
            chain("c_steps", [
                lambda: dve.reciprocal(flat(c_rstd), flat(c_root)),
                lambda: dve.tensor_tensor(flat(c_ssq), flat(c_rstd), flat(c_rstd), ALU.mult),
                lambda: dve.tensor_tensor(flat(c_ssq), flat(c_ssq), flat(c_mean), ALU.mult),
                lambda: dve.tensor_scalar(flat(c_ssq), flat(c_ssq), -0.5, 1.5, ALU.mult, ALU.add),
                lambda: dve.tensor_tensor(flat(c_rstd), flat(c_rstd), flat(c_ssq), ALU.mult),
                lambda: dve.tensor_scalar(flat(c_rstd), flat(c_rstd), 1.0 - LAM_INIT, None, ALU.mult),
                lambda: dve.tensor_tensor(c_heads, c_heads, flat(c_rstd).rearrange("p (h a) -> p h a", a=1)
                                          .to_broadcast([P, 16, P]), ALU.mult)])
            dve.tensor_tensor(c_heads, c_heads, sub_gain[:, :].rearrange("p (a n) -> p a n", a=1)
                              .to_broadcast([P, 16, P]), ALU.mult).then_inc(sem("c_ready"), 1)

        def hidden_copy():
            dve.wait_ge(sem("hidden_rows"), 2)
            dve.tensor_copy(hid_rows[:, :, :], ps[0:2 * NCMP, 2:4, 0:256]).then_inc(sem("hidden_copied"), 1)

        def gelu_first():
            dve.wait_ge(sem("hidden_mm"), 1)
            h, a = hid[:, 0, :], hid[:, 1, :]
            chain("gelu_steps", [
                lambda: dve.tensor_copy(h, ps[:, 2, 0:120]),
                lambda: dve.tensor_tensor(a, h, h, ALU.mult),
                lambda: dve.tensor_scalar(a, a, 0.044715, 1.0, ALU.mult, ALU.add),
                lambda: dve.tensor_tensor(a, a, h, ALU.mult),
                lambda: dve.tensor_scalar(a, a, -50.0, None, ALU.max)])

        def gelu_second():
            dve.wait_ge(sem("gelu_exp"), 1)
            h, e = hid[:, 0, :], hid[:, 2, :]
            chain("gelu_steps", [
                lambda: dve.tensor_scalar(e, e, 1.0, None, ALU.add),
                lambda: dve.reciprocal(e, e)])
            dve.tensor_tensor(hid_k[:, :, :].rearrange("p a n -> p (a n)"), h[:, 0:60], e[:, 0:60], ALU.mult).then_inc(
                sem("gelu_ready"), 1)
            dve.wait_ge(sem("cmp_zero"), 4)
            chain("gelu_steps", [lambda: dve.tensor_tensor(h[:, 60:120], h[:, 60:120], e[:, 60:120], ALU.mult)])
            for g in range(2):
                dve.tensor_copy(hid_v[:, :, g, :, 0:NCMP], h[:, 60:120].rearrange(
                    "p (c g n) -> p c g n", c=2, g=2)[:, :, g, :].rearrange("p c (a n) -> p c a n", a=1)
                    .to_broadcast([P, 2, 4, NCMP])).then_inc(sem("gelu_ready"), 1)

        def compressed():
            dve.wait_ge(sem("compressed_mm"), 1)
            for q in range(4):
                part = slice(32 * q, 32 * q + 32)
                dve.tensor_copy(vc_diag[part, :, q, :], ps[part, 3, 64:192].rearrange("p (g n) -> p g n", g=2))
            for a in range(2):
                part = slice(64 * a, 64 * a + 64)
                last = dve.tensor_copy(kc_diag[part, :, a, :], ps[part, 3, 0:30].rearrange("p (g n) -> p g n", g=2))
            last.then_inc(sem("compressed"), 1)

        def cmp_first():
            dve.wait_ge(sem("cmp_scores"), 1)
            for t in range(2):
                last = dve.tensor_tensor(
                    cmp_l[:, t, :, :], ps[:, 4 + t, 0:16 * NCMP].rearrange("p (h n) -> p h n", h=16),
                    bmask[:, t, :].rearrange("p (a n) -> p a n", a=1).to_broadcast([P, 16, NCMP]), ALU.add)
            last.then_inc(sem("cmp_steps"), 1)
            dve.wait_ge(sem("cmp_steps"), 1)
            done["cmp_steps"] = 1
            l4 = cmp_l[:, :, :, :].rearrange("p t h n -> p (t h) n")
            mx = m_max[:, :, :].rearrange("p t h -> p (t h)")
            chain("cmp_steps", [
                lambda: dve.tensor_reduce(mx, l4, AX, ALU.max),
                lambda: dve.tensor_scalar(mx, mx, 0.5 * NEG, None, ALU.max),
                lambda: dve.tensor_tensor(l4, l4, mx.rearrange("p (h a) -> p h a", a=1).to_broadcast([P, 32, NCMP]),
                                          ALU.subtract)])

        def cmp_second():
            dve.wait_ge(sem("cmp_exp"), 1)
            l4 = cmp_l[:, :, :, :].rearrange("p t h n -> p (t h) n")
            sm = m_sum[:, :, :].rearrange("p t h -> p (t h)")
            chain("cmp_steps", [
                lambda: dve.tensor_reduce(sm, l4, AX, ALU.add),
                lambda: dve.tensor_scalar(sm, sm, TINY, None, ALU.max),
                lambda: dve.reciprocal(sm, sm),
                lambda: dve.tensor_tensor(m_coef[:, :, :], m_sum[:, :, :], head_gates[:, :, 0, :], ALU.mult)])
            dve.tensor_tensor(cmp_p[:, :, :, 0:NCMP].rearrange("p t h n -> p (t h) n"), l4,
                              m_coef[:, :, :].rearrange("p t (h a) -> p (t h) a", a=1).to_broadcast([P, 32, NCMP]),
                              ALU.mult).then_inc(sem("cmp_probs"), 1)

        def cmp_third():
            dve.wait_ge(sem("cmp_pt"), 1)
            dve.tensor_copy(cmp_pt[:, :, :].rearrange("p (b a) n -> p b (a n)", b=2), ps[:, 6:8, :]).then_inc(
                sem("cmp_pt_copied"), 1)

        def cmp_fourth():
            dve.wait_ge(sem("cmp_pv"), 1)
            for t in range(2):
                o = o_b[:, t, :].rearrange("p (b n) -> p b n", b=2)
                last = dve.tensor_tensor(o, ps[:, 2 + 2 * t:4 + 2 * t, :], o, ALU.add)
            last.then_inc(sem("b_ready"), 1)

        maps("a", 0)
        with dve.Fori(1, 3) as i:
            maps("a", i)
        maps("c", 0, {1: [a_first], 3: [a_second], 5: [lambda: a_scale(0)], 6: [lambda: a_scale(1)]})
        maps("c", 1, {3: [lambda: a_scale(2)], 5: [lambda: a_sum(1)], 6: [lambda: a_sum(2)]})
        maps("b", 0, {5: [lambda: c_squares(0)], 6: [lambda: c_sums(0)]})
        with dve.Fori(1, 3) as i:
            maps("b", i)
        maps("b", 3, {5: [lambda: c_squares(1)], 6: [lambda: c_sums(1)]})

        def o_split(q):
            g, bank = O_PAIRS[q], O_BANKS[q]
            dve.wait_ge(sem("o_split_hi"), q + 1)
            dve.tensor_tensor(o_lo[:, 2 * g:2 * g + 2, :], ps[:, bank, :].rearrange("p (a n) -> p a n", a=2),
                              o_hi[:, 2 * g:2 * g + 2, :].bitcast(F32), ALU.subtract).then_inc(sem("o_split_lo"), 1)

        dve_steps = {1: [c_second], 2: [hidden_copy], 3: [gelu_first], 4: [gelu_second], 6: [compressed], 8: [cmp_first],
                     10: [cmp_second], 12: [cmp_third], 14: [cmp_fourth]}
        for q, n in enumerate(O_AT):
            dve_steps.setdefault(n + 1, []).append(lambda q=q: o_split(q))
        for n in range(NSTEP):
            c, s = divmod(n, CH)
            split(Pos(U0["gate"] + 72 + n + LEAD), (s + LEAD) % RING)
            for f in dve_steps.get(n, ()):
                f()
            gate_part(8 + c, s)

        def merge(n, b):
            dve.wait_ge(sem(f"gates_loaded{n % 2}_{b}"), 16 * (n // 2 + 1))
            dst = br_stage[:, n % 2, :, :] if b == 0 else br_tmp[:, :, :]
            for h in range(2):
                if h == 0:
                    dve.wait_ge(sem("half_done"), C0["branch"] + 3 * n + b + 1)
                else:
                    dve.wait_ge(sem("unit_used"), U0["branch"] + 10 * n + sum(BR_UNITS[:b + 1]))
                dve.tensor_tensor(dst[:, h, :], ps[:, 2 * b + h, :], gates_in[:, n % 2, b, h, :], ALU.mult).then_inc(
                    sem("evac_v"), 1)
            if b == 0:
                return
            dve.wait_ge(sem("evac_v"), V0["branch"] + 2 * (3 * n + b + 1))
            whole = br_stage[:, n % 2, :, :]
            add = dve.tensor_tensor(whole, whole, br_tmp[:, :, :], ALU.add)
            add.then_inc(sem("merge_done" if b == 2 else "merge_steps"), 1)
            if b == 1:
                dve.wait_ge(sem("merge_steps"), n + 1)

        for n in range(4):
            u0 = U0["branch"] + 10 * n
            for b in range(3):
                before = sum(BR_UNITS[:b])
                for j in range(BR_UNITS[b]):
                    if n == 0 and before + j <= max(GATE_PARTS):
                        gate_part(11, before + j)
                    split(Pos(u0 + before + j + LEAD), (10 * n + before + j + LEAD) % RING)
                    if n > 0 and before + j == 5:
                        t_split(Pos(T0["branch"] + n - 1), h_lo[:, 4 * (n - 1):4 * n, :], h_hi[:, 4 * (n - 1):4 * n, :])
                merge(n, b)

        def out_chunk(i):
            def gained_half(t):
                dve.wait_ge(sem("evac_s"), Pos(S0["out"] + t + 1, 2, i).count())
                dve.tensor_tensor(y[:, t, bass.ds(i * W, W)], ps[:, t, :], gain_row[:, bass.ds(i * W, W)], ALU.mult
                                  ).then_inc(sem("evac_v"), 1)

            chunk(Pos(U0["out"], CH, i), CH, early=lambda: [gained_half(t) for t in range(2)], after={2: [lambda: t_split(
                Pos(T0["out"] - 1), h_lo[:, 12:16, :], h_hi[:, 12:16, :])]} if isinstance(i, int) and i == 0 else None)

        dve.wait_ge(sem("gain_loaded"), 16)
        out_chunk(0)
        with dve.Fori(1, 4) as i:
            out_chunk(i)

        def residual(k, b, ready):
            for t in range(2):
                cols = slice(W * b, W * b + W)
                dve.scalar_tensor_tensor(mid[:, t, cols], y[:, t, cols], rstd[:, k, t:t + 1], mid[:, t, cols],
                                         ALU.mult, ALU.add).then_inc(sem(ready), 1)

        rstd_first(1, "evac_s", S0["up0"])
        rstd_second(1)
        dve.wait_ge(sem("x_again"), 32)
        dve.wait_ge(sem("evac_v"), V0["up0"])
        residual(1, 0, "mid_ready")
        residual(1, 1, "mid_ready")
        first_chunk(2, Pos(U0["up0"]), {1: lambda: residual(1, 2, "mid_ready"), 3: lambda: residual(1, 3, "mid_ready")})

        def up(name, i):
            u, t, es = Pos(U0[name], 2 * CH, i), Pos(T0[name], 2, i), Pos(S0[name], 4, i)

            def square(c):
                dve.wait_ge(sem("evac_s"), es.count(2 * c + 2))
                dve.tensor_tensor(up_stage[:, c, :, :], up_stage[:, c, :, :], up_stage[:, c, :, :], ALU.mult).then_inc(
                    sem("evac_v"), 1)

            def group(t, first):
                return {2: [lambda: t_split(t, u_lo[:, bass.ds(first, 4), :], u_hi[:, bass.ds(first, 4), :])]}

            if not (name == "up0" and isinstance(i, int)):
                chunk(u, CH, after=None if isinstance(i, int) else group(t + (-1), i * 8 - 4))
            square(0)
            chunk(u + CH, CH, after=group(t, i * 8))
            square(1)

        def gained_half(i, t):
            dve.wait_ge(sem("evac_s"), S0["down1"] + 2 * i + t + 1)
            part = y[:, t, W * i:W * i + W]
            dve.tensor_tensor(part, part, gain_row[:, W * i:W * i + W], ALU.mult).then_inc(sem("gained"), 1)

        def gained(i):
            dve.wait_ge(sem("evac_s"), Pos(S0["down1"] + 2, 2, i).count())
            part = y[:, :, bass.ds(i * W, W)]
            dve.tensor_tensor(part, part, gain_row[:, bass.ds(i * W, W)].rearrange("p (a n) -> p a n", a=1)
                              .to_broadcast([P, 2, W]), ALU.mult).then_inc(sem("gained"), 1)

        def down(h, i):
            u = Pos(U0[f"down{h}"], 16, i)
            after = {}
            if isinstance(i, int) and i == 0:
                after[2] = [lambda: t_split(Pos(T0[f"down{h}"] - 1), u_lo[:, 28:32, :], u_hi[:, 28:32, :])]
            elif h == 1:
                after[3] = [lambda: gained(i - 1)]
            def evacuate(t):
                if h == 0:
                    copy_out(y[:, 0, bass.ds(i * W, W)], 0, Pos(C0["down0"], 1, i).count(1))
                    return
                if t == 0:
                    dve.wait_ge(sem("half_done"), Pos(C0["down1"], 1, i).count(1))
                else:
                    dve.wait_ge(sem("unit_used"), u.count(16))
                part = y[:, t, bass.ds(i * W, W)]
                dve.tensor_tensor(part, ps[:, t, :], part, ALU.add).then_inc(sem("evac_v"), 1)

            chunk(u, 16, after=after, early=lambda: evacuate(0))
            if h == 1:
                evacuate(1)

        for h in range(2):
            up(f"up{h}", 0)
            with dve.Fori(1, 4) as i:
                up(f"up{h}", i)
            down(h, 0)
            if h == 1:
                dve.wait_ge(sem("gain_loaded"), 32)
            with dve.Fori(1, 4 - h) as i:
                down(h, i)
            if h == 1:
                down(h, 3)
        gained_half(3, 0)
        rstd_first(3, "evac_s", S0["down1"] + 8)
        gained_half(3, 1)
        rstd_second(3)
        dve.wait_ge(sem("gained"), 5)
        for b in range(4):
            residual(3, b, "result_ready")


def _constants():
    import numpy as np

    exact, buckets = 16, 32
    dist = np.arange(512) - 127
    d = np.maximum(dist, 0)
    logd = np.log(np.maximum(d, 1).astype(np.float32) / np.float32(exact))
    far = exact + (logd / np.float32(math.log(2048 / exact)) * (buckets - exact)).astype(np.int32)
    bucket = np.where(d < exact, d, np.minimum(far, buckets - 1))
    onehot = (bucket[None, :] == np.arange(buckets)[:, None]).astype(np.float32)
    mask = np.zeros((48, 512), np.float32)
    mask[:, dist < 0] = NEG
    for g, (window, step) in enumerate(((128, 1), (512, 4), (2048, 16))):
        mask[8 * g:8 * g + 8, (dist < 0) | (dist > window) | (dist % step != 0)] = NEG
    t = np.arange(SEQ)
    seen = (np.arange(NCMP) * CSTRIDE + 31)[None, :] <= t[:, None]
    blocks = np.where(seen, 0.0, NEG).astype(np.float32).reshape(2, P, NCMP).transpose(1, 0, 2)
    return {"identity": np.eye(P, dtype=np.float32), "bucket_onehot": onehot, "distance_mask": mask,
            "block_mask": np.ascontiguousarray(blocks)}


_INS = ["x", "rel_bias", "w_in", "cmp_k_pos", "cmp_v_pos", "cmp_k_w1", "cmp_k_w2", "cmp_v_w1", "cmp_v_w2",
        "diff_lambda", "diff_norm", "w_branch_a", "w_branch_b", "w_branch_c", "w_out", "norm_mix_pre",
        "norm_mix_post", "norm_mlp_pre", "norm_mlp_post", "w_up", "w_down"]


def kernel(**inputs):
    import numpy as np
    import concourse.bacc as bacc
    from concourse.bass_utils import run_bass_kernel_spmd

    nc = bacc.Bacc("TRN2", target_bir_lowering=False, num_devices=1)
    given = {name: np.ascontiguousarray(inputs[name]) for name in _INS}
    given.update(_constants())
    arrays, args = {}, []
    for name, a in given.items():
        arrays[f"in_{name}_dram"] = a
        args.append(nc.dram_tensor(f"in_{name}_dram", a.shape, mybir.dt.from_np(a.dtype), kind="ExternalInput").ap())
    args.append(nc.dram_tensor("out_0_dram", (1, SEQ, D), F32, kind="ExternalOutput").ap())
    trunk(nc, *args)
    r = run_bass_kernel_spmd(nc, [arrays], core_ids=[0])
    return r.results[0]["out_0_dram"]
```
